# Optimizing a Trainium2 kernel written in Bass

```python
import math
import jax
import jax.numpy as jnp
from jax import lax
import numpy as np

D_MODEL = 1024
BATCH = 1
SEQ = 1024
DEPTH = 1
DEC_BATCH = 8
DEC_SEQ = 8
PAST_LEN = 256
PAGE_SIZE = 128

MIX = D_MODEL
HEAD_DIM = 64
NSA_WIDTH = D_MODEL // 2
NSA_HEADS = NSA_WIDTH // HEAD_DIM
NSA_KV_HEADS = 2
NSA_GROUP = NSA_HEADS // NSA_KV_HEADS
NSA_BLOCK = 64
NSA_TOPK = 16
WINDOW = 512
N_NSA_KV = 6
DN_WIDTH = D_MODEL // 4
DN_HEADS = DN_WIDTH // HEAD_DIM
DN_DK = HEAD_DIM
DN_DV = HEAD_DIM
DN_CONV_W = 4
DN_CHUNK = 64
DN_CONV_DIM = 3 * DN_WIDTH
S5_WIDTH = D_MODEL - NSA_WIDTH - DN_WIDTH
S5_GROUP_CH = 16
S5_GROUPS = S5_WIDTH // S5_GROUP_CH
S5_STATE = 64
D_FF = 4 * D_MODEL
Q_BLOCK = 128
NORM_EPS = 1e-6
BIG = 1e9
NEG_INF = -1e30
SPLIT_WIDTHS = (NSA_WIDTH, N_NSA_KV * NSA_KV_HEADS * HEAD_DIM, NSA_HEADS * 3,
                3 * DN_WIDTH, DN_HEADS, DN_HEADS, DN_WIDTH, S5_WIDTH)
IN_WIDTH = sum(SPLIT_WIDTHS)

kernel_name = 'hymba_nsa_gdn_s5_decode_step'

def split_cols(a, widths):
    outs, start = [], 0
    for wdt in widths:
        outs.append(a[..., start:start + wdt])
        start += wdt
    return outs

def rmsnorm(x, g):
    xf = x.astype(jnp.float32)
    y = xf * lax.rsqrt(jnp.mean(xf * xf, axis=-1, keepdims=True) + NORM_EPS)
    return (y * g.astype(jnp.float32)).astype(x.dtype)

def l2norm(a):
    return a * lax.rsqrt(jnp.sum(a * a, axis=-1, keepdims=True) + 1e-6)

def masked_softmax(s, mask, axes):
    s = jnp.where(mask, s, NEG_INF)
    m = jnp.max(s, axis=axes, keepdims=True)
    p = jnp.exp(s - m) * mask
    return p / jnp.maximum(jnp.sum(p, axis=axes, keepdims=True), 1e-30)

def alibi_slopes():
    h = jnp.arange(1, NSA_HEADS + 1, dtype=jnp.float32)
    return jnp.exp2(-8.0 * h / NSA_HEADS).reshape(NSA_KV_HEADS, NSA_GROUP)

def nsa_attend(q, k_cmp, v_cmp, k_sel, v_sel, k_win, v_win, gates, w_ck, w_cv, q0, w0):
    B, Lq = q.shape[0], q.shape[1]
    Sk = k_cmp.shape[1]
    G, R, dh = NSA_KV_HEADS, NSA_GROUP, HEAD_DIM
    f32 = jnp.float32
    slopes = alibi_slopes()
    qg = q.reshape(B, Lq, G, R, dh)
    t = q0 + jnp.arange(Lq)
    nb = Sk // NSA_BLOCK
    kcb = k_cmp[:, :nb * NSA_BLOCK].reshape(B, nb, NSA_BLOCK, G, dh)
    vcb = v_cmp[:, :nb * NSA_BLOCK].reshape(B, nb, NSA_BLOCK, G, dh)
    kc = jnp.einsum('bnjgd,gj->bngd', kcb, w_ck)
    vc = jnp.einsum('bnjgd,gj->bngd', vcb, w_cv)
    blk = jnp.arange(nb)
    s_c = jnp.einsum('bqgrd,bngd->bgrqn', qg, kc, preferred_element_type=f32)
    dist_c = t[:, None].astype(f32) - (blk * NSA_BLOCK + (NSA_BLOCK - 1) / 2.0)[None, :]
    ok_c = ((blk + 1) * NSA_BLOCK - 1)[None, :] <= t[:, None]
    p_c = masked_softmax(s_c - slopes[None, :, :, None, None] * dist_c, ok_c, axes=-1)
    o_c = jnp.einsum('bgrqn,bngd->bqgrd', p_c, vc.astype(f32))
    nbs = -(-Sk // NSA_BLOCK)
    imp = jnp.pad(jnp.sum(p_c, axis=2), ((0, 0), (0, 0), (0, 0), (0, nbs - nb)))
    cur = t // NSA_BLOCK
    cand = jnp.arange(nbs)
    forced = (cand[None, :] == 0) | (cand[None, :] == cur[:, None]) | (cand[None, :] == cur[:, None] - 1)
    score = jnp.where(cand[None, :] > cur[:, None], -BIG, jnp.where(forced, BIG, imp))
    n_sel = min(NSA_TOPK, nbs)
    _, idx = lax.top_k(score, n_sel)
    valid = idx <= cur[None, None, :, None]
    pad_k = nbs * NSA_BLOCK - Sk

    def to_blocks(a):
        a = jnp.pad(a, ((0, 0), (0, pad_k), (0, 0), (0, 0)))
        return a.reshape(B, nbs, NSA_BLOCK, G, dh).transpose(0, 3, 1, 2, 4)

    ksb, vsb = to_blocks(k_sel), to_blocks(v_sel)
    kw_pad = jnp.pad(k_win, ((0, 0), (WINDOW, 0), (0, 0), (0, 0)))
    vw_pad = jnp.pad(v_win, ((0, 0), (WINDOW, 0), (0, 0), (0, 0)))
    qb_len = math.gcd(Lq, Q_BLOCK)
    nq = Lq // qb_len
    span = qb_len + WINDOW - 1
    bi = jnp.arange(B)[:, None, None, None]
    gi = jnp.arange(G)[None, :, None, None]

    def body(xs):
        qb, ib, vb, i0 = xs
        tb = q0 + i0 + jnp.arange(qb_len)
        kg = ksb[bi, gi, ib]
        vg = vsb[bi, gi, ib]
        pos = ib[..., None] * NSA_BLOCK + jnp.arange(NSA_BLOCK)
        dist = tb[None, None, :, None, None] - pos
        m_s = (dist >= 0) & vb[..., None]
        s = jnp.einsum('bqgrd,bgqnjd->bgrqnj', qb, kg, preferred_element_type=f32)
        s = s - slopes[None, :, :, None, None, None] * dist[:, :, None].astype(f32)
        p = masked_softmax(s, m_s[:, :, None], axes=(-2, -1))
        o_s = jnp.einsum('bgrqnj,bgqnjd->bqgrd', p, vg.astype(f32))
        start = q0 + i0 - w0 + 1
        kwb = lax.dynamic_slice_in_dim(kw_pad, start, span, axis=1)
        vwb = lax.dynamic_slice_in_dim(vw_pad, start, span, axis=1)
        wpos = q0 + i0 - WINDOW + 1 + jnp.arange(span)
        dist_w = tb[:, None] - wpos[None, :]
        m_w = (dist_w >= 0) & (dist_w < WINDOW) & (wpos >= w0)[None, :]
        s_w = jnp.einsum('bqgrd,bkgd->bgrqk', qb, kwb, preferred_element_type=f32)
        p_w = masked_softmax(s_w - slopes[None, :, :, None, None] * dist_w.astype(f32), m_w, axes=-1)
        o_w = jnp.einsum('bgrqk,bkgd->bqgrd', p_w, vwb.astype(f32))
        return o_s, o_w

    xs = (qg.reshape(B, nq, qb_len, G, R, dh).transpose(1, 0, 2, 3, 4, 5),
          idx.reshape(B, G, nq, qb_len, n_sel).transpose(2, 0, 1, 3, 4),
          valid.reshape(B, G, nq, qb_len, n_sel).transpose(2, 0, 1, 3, 4),
          jnp.arange(nq) * qb_len)
    o_s, o_w = lax.map(body, xs)
    o_s = o_s.transpose(1, 0, 2, 3, 4, 5).reshape(B, Lq, G, R, dh)
    o_w = o_w.transpose(1, 0, 2, 3, 4, 5).reshape(B, Lq, G, R, dh)
    gt = gates.reshape(B, Lq, G, R, 3)
    o = gt[..., 0:1] * o_c + gt[..., 1:2] * o_s + gt[..., 2:3] * o_w
    return o.reshape(B, Lq, NSA_WIDTH)

def short_conv(x, buf, w):
    L = x.shape[1]
    xc = jnp.concatenate([buf.astype(x.dtype), x], axis=1)
    y = sum(xc[:, j:j + L] * w[:, j] for j in range(DN_CONV_W))
    return jax.nn.silu(y), xc[:, xc.shape[1] - (DN_CONV_W - 1):]

def gated_delta_chunked(q, k, v, g, beta, s0):
    B, L, H, dk = q.shape
    dv = v.shape[-1]
    C = min(DN_CHUNK, L)
    n = -(-L // C)
    pad = n * C - L
    if pad:
        pw = ((0, 0), (0, pad), (0, 0), (0, 0))
        q, k, v = jnp.pad(q, pw), jnp.pad(k, pw), jnp.pad(v, pw)
        g, beta = jnp.pad(g, pw[:3]), jnp.pad(beta, pw[:3])
    qc, kc, vc = [a.reshape(B, n, C, H, a.shape[-1]).transpose(1, 0, 3, 2, 4) for a in (q, k, v)]
    gc = jnp.cumsum(g.reshape(B, n, C, H).transpose(1, 0, 3, 2), axis=-1)
    bc = beta.reshape(B, n, C, H).transpose(1, 0, 3, 2)
    tri = jnp.tril(jnp.ones((C, C), dtype=bool))
    strict = jnp.tril(jnp.ones((C, C), dtype=bool), -1)
    diff = gc[..., :, None] - gc[..., None, :]
    decay = jnp.where(tri, jnp.exp(jnp.where(tri, diff, 0.0)), 0.0)
    kb = kc * bc[..., None]
    a_mat = jnp.where(strict, jnp.einsum('nbhid,nbhjd->nbhij', kb, kc) * decay, 0.0)
    eye = jnp.eye(C, dtype=a_mat.dtype)
    rhs = jnp.concatenate([vc * bc[..., None], kb * jnp.exp(gc)[..., None]], axis=-1)
    sol = lax.linalg.triangular_solve(a_mat + eye, rhs, left_side=True, lower=True)
    u, w = sol[..., :dv], sol[..., dv:]
    a_qk = jnp.where(tri, jnp.einsum('nbhid,nbhjd->nbhij', qc, kc) * decay, 0.0)

    def step(S, xs):
        q_i, k_i, u_i, w_i, g_i, aqk_i = xs
        v_new = u_i - jnp.einsum('bhck,bhkv->bhcv', w_i, S)
        o_i = (jnp.einsum('bhck,bhkv->bhcv', q_i * jnp.exp(g_i)[..., None], S)
               + jnp.einsum('bhij,bhjv->bhiv', aqk_i, v_new))
        g_last = g_i[..., -1]
        S = (S * jnp.exp(g_last)[..., None, None]
             + jnp.einsum('bhck,bhcv->bhkv', k_i * jnp.exp(g_last[..., None] - g_i)[..., None], v_new))
        return S, o_i

    s_fin, o = lax.scan(step, s0, (qc, kc, u, w, gc, a_qk))
    o = o.transpose(1, 0, 3, 2, 4).reshape(B, n * C, H, dv)[:, :L]
    return o, s_fin

def deltanet_mix(qkv, a, b, z, conv_buf, s0, conv_w, a_log, dt_bias, norm_w):
    B, L, _ = qkv.shape
    f32 = jnp.float32
    y, new_buf = short_conv(qkv, conv_buf, conv_w)
    y = y.astype(f32)
    q = l2norm(y[..., :DN_WIDTH].reshape(B, L, DN_HEADS, DN_DK)) * DN_DK ** -0.5
    k = l2norm(y[..., DN_WIDTH:2 * DN_WIDTH].reshape(B, L, DN_HEADS, DN_DK))
    v = y[..., 2 * DN_WIDTH:].reshape(B, L, DN_HEADS, DN_DV)
    beta = jax.nn.sigmoid(b.astype(f32))
    g = -jnp.exp(a_log.astype(f32)) * jax.nn.softplus(a.astype(f32) + dt_bias.astype(f32))
    o, s_new = gated_delta_chunked(q, k, v, g, beta, s0.astype(f32))
    o = rmsnorm(o, norm_w) * jax.nn.silu(z.astype(f32).reshape(B, L, DN_HEADS, DN_DV))
    return o.reshape(B, L, DN_WIDTH), new_buf, s_new

def complex_affine_combine(e1, e2):
    a1r, a1i, b1r, b1i = e1
    a2r, a2i, b2r, b2i = e2
    return (a2r * a1r - a2i * a1i, a2r * a1i + a2i * a1r,
            a2r * b1r - a2i * b1i + b2r, a2r * b1i + a2i * b1r + b2i)

def s5_mix(u, h0_re, h0_im, lam_re, lam_im, log_step, b_re, b_im, c_re, c_im, d, w_glu):
    B, L, _ = u.shape
    f32 = jnp.float32
    uf = u.astype(f32)
    ug = uf.reshape(B, L, S5_GROUPS, S5_GROUP_CH)
    lr, li = lam_re.astype(f32), lam_im.astype(f32)
    dt = jnp.exp(log_step.astype(f32))[:, None]
    mag = jnp.exp(lr * dt)
    ar, ai = mag * jnp.cos(li * dt), mag * jnp.sin(li * dt)
    den = lr * lr + li * li
    fr = ((ar - 1.0) * lr + ai * li) / den
    fi = (ai * lr - (ar - 1.0) * li) / den
    br, bi = b_re.astype(f32), b_im.astype(f32)
    bbr = fr[..., None] * br - fi[..., None] * bi
    bbi = fr[..., None] * bi + fi[..., None] * br
    bu_r = jnp.einsum('gpc,blgc->blgp', bbr, ug)
    bu_i = jnp.einsum('gpc,blgc->blgp', bbi, ug)
    a_r = jnp.broadcast_to(ar, bu_r.shape)
    a_i = jnp.broadcast_to(ai, bu_i.shape)
    cum_r, cum_i, hs_r, hs_i = lax.associative_scan(complex_affine_combine, (a_r, a_i, bu_r, bu_i), axis=1)
    h0r = h0_re.astype(f32)[:, None]
    h0i = h0_im.astype(f32)[:, None]
    h_r = cum_r * h0r - cum_i * h0i + hs_r
    h_i = cum_r * h0i + cum_i * h0r + hs_i
    y = (jnp.einsum('gcp,blgp->blgc', c_re.astype(f32), h_r)
         - jnp.einsum('gcp,blgp->blgc', c_im.astype(f32), h_i))
    y = y.reshape(B, L, S5_WIDTH) + d.astype(f32) * uf
    gl = jax.nn.gelu(y)
    out = gl * jax.nn.sigmoid(gl @ w_glu.astype(f32))
    return out, h_r[:, -1], h_i[:, -1]

def trunk_layer(x, past_kv, win_buf, conv_buf, dn_s0, s5_re0, s5_im0, p):
    B, L, _ = x.shape
    f32 = jnp.float32
    q0 = past_kv.shape[1]
    w0 = q0 - win_buf.shape[1]
    h = rmsnorm(x, p['ln1'])
    nsa_q, nsa_kv, nsa_gate, dn_qkv, dn_a, dn_b, dn_z, s5_u = split_cols(h @ p['w_in'], SPLIT_WIDTHS)
    kv = nsa_kv.reshape(B, L, N_NSA_KV, NSA_KV_HEADS, HEAD_DIM)
    new_kv = kv[:, :, :4]
    full = jnp.concatenate([past_kv.astype(kv.dtype), new_kv], axis=1)
    wseq = jnp.concatenate([win_buf.astype(kv.dtype), kv[:, :, 4:]], axis=1)
    q = nsa_q.reshape(B, L, NSA_HEADS, HEAD_DIM) * HEAD_DIM ** -0.5
    gates = jax.nn.sigmoid(nsa_gate.astype(f32)).reshape(B, L, NSA_HEADS, 3)
    o_nsa = nsa_attend(q, full[:, :, 0], full[:, :, 1], full[:, :, 2], full[:, :, 3],
                       wseq[:, :, 0], wseq[:, :, 1], gates, p['nsa_wck'], p['nsa_wcv'], q0, w0)
    new_win = wseq[:, wseq.shape[1] - min(WINDOW, q0 + L):]
    o_dn, new_conv, new_dn = deltanet_mix(dn_qkv, dn_a, dn_b, dn_z, conv_buf, dn_s0, p['dn_conv_w'],
                                          p['dn_a_log'], p['dn_dt_bias'], p['dn_norm_w'])
    o_s5, s5_re, s5_im = s5_mix(s5_u, s5_re0, s5_im0, p['s5_lambda_re'], p['s5_lambda_im'], p['s5_log_step'],
                                p['s5_b_re'], p['s5_b_im'], p['s5_c_re'], p['s5_c_im'], p['s5_d'], p['s5_w_glu'])
    mix = jnp.concatenate([o_nsa, o_dn, o_s5], axis=-1).astype(x.dtype)
    x = x + mix @ p['w_out']
    h2 = rmsnorm(x, p['ln2'])
    x = x + jnp.square(jax.nn.relu(h2 @ p['mlp_up'])) @ p['mlp_down']
    return x, (new_kv, new_win, new_conv, new_dn, s5_re, s5_im)

def setup_inputs(seed: int = 0) -> dict:
    key = jax.random.key(seed)
    ks = iter(jax.random.split(key, 48))
    f32 = jnp.float32

    def nrm(shape, scale):
        return jax.random.normal(next(ks), shape, f32) * scale

    def unif(shape, lo, hi):
        return jax.random.uniform(next(ks), shape, f32, lo, hi)

    n_pages = PAST_LEN // PAGE_SIZE
    n_used = DEC_BATCH * n_pages
    n_phys = n_used + (n_used + 3) // 4
    G, dh = NSA_KV_HEADS, HEAD_DIM
    x_prompt = nrm((BATCH, SEQ, D_MODEL), 1.0)
    x_sample = nrm((DEC_BATCH, DEC_SEQ, D_MODEL), 1.0)
    cache_nsa_kv = nrm((DEPTH, n_phys, PAGE_SIZE, 4, G, dh), 1.0)
    cache_win_kv = nrm((DEPTH, DEC_BATCH, min(WINDOW, PAST_LEN), 2, G, dh), 1.0)
    state_dn_conv = nrm((DEPTH, DEC_BATCH, DN_CONV_W - 1, DN_CONV_DIM), 1.0)
    state_dn = nrm((DEPTH, DEC_BATCH, DN_HEADS, DN_DK, DN_DV), 0.3)
    state_s5_re = nrm((DEPTH, DEC_BATCH, S5_GROUPS, S5_STATE), 0.2)
    state_s5_im = nrm((DEPTH, DEC_BATCH, S5_GROUPS, S5_STATE), 0.2)
    page_table = jax.random.permutation(next(ks), n_phys)[:n_used].reshape(DEC_BATCH, n_pages).astype(jnp.int32)
    ln1 = 1.0 + nrm((DEPTH, D_MODEL), 0.02)
    ln2 = 1.0 + nrm((DEPTH, D_MODEL), 0.02)
    ln_f = 1.0 + nrm((D_MODEL,), 0.02)
    w_in = nrm((DEPTH, D_MODEL, IN_WIDTH), D_MODEL ** -0.5)
    w_out = nrm((DEPTH, MIX, D_MODEL), MIX ** -0.5)
    nsa_wck = 1.0 / NSA_BLOCK + nrm((DEPTH, G, NSA_BLOCK), NSA_BLOCK ** -0.5)
    nsa_wcv = 1.0 / NSA_BLOCK + nrm((DEPTH, G, NSA_BLOCK), NSA_BLOCK ** -0.5)
    dn_conv_w = nrm((DEPTH, DN_CONV_DIM, DN_CONV_W), DN_CONV_W ** -0.5)
    dn_a_log = jnp.log(unif((DEPTH, DN_HEADS), 1.0, 16.0))
    dt = jnp.exp(unif((DEPTH, DN_HEADS), math.log(1e-3), math.log(0.1)))
    dn_dt_bias = dt + jnp.log(-jnp.expm1(-dt))
    dn_norm_w = 1.0 + nrm((DEPTH, DN_DV), 0.02)
    s5_lambda_re = -0.5 + nrm((DEPTH, S5_GROUPS, S5_STATE), 0.01)
    s5_lambda_im = math.pi * jnp.arange(S5_STATE, dtype=f32) + nrm((DEPTH, S5_GROUPS, S5_STATE), 0.01)
    s5_log_step = unif((DEPTH, S5_GROUPS), math.log(1e-3), math.log(0.1))
    s5_b_re = nrm((DEPTH, S5_GROUPS, S5_STATE, S5_GROUP_CH), (2 * S5_GROUP_CH) ** -0.5)
    s5_b_im = nrm((DEPTH, S5_GROUPS, S5_STATE, S5_GROUP_CH), (2 * S5_GROUP_CH) ** -0.5)
    s5_c_re = nrm((DEPTH, S5_GROUPS, S5_GROUP_CH, S5_STATE), S5_STATE ** -0.5)
    s5_c_im = nrm((DEPTH, S5_GROUPS, S5_GROUP_CH, S5_STATE), S5_STATE ** -0.5)
    s5_d = nrm((DEPTH, S5_WIDTH), 1.0)
    s5_w_glu = nrm((DEPTH, S5_WIDTH, S5_WIDTH), S5_WIDTH ** -0.5)
    mlp_up = nrm((DEPTH, D_MODEL, D_FF), D_MODEL ** -0.5)
    mlp_down = nrm((DEPTH, D_FF, D_MODEL), D_FF ** -0.5)
    return {'x_prompt': x_prompt, 'x_sample': x_sample, 'cache_nsa_kv': cache_nsa_kv,
            'cache_win_kv': cache_win_kv, 'state_dn_conv': state_dn_conv, 'state_dn': state_dn,
            'state_s5_re': state_s5_re, 'state_s5_im': state_s5_im, 'page_table': page_table,
            'ln1': ln1, 'ln2': ln2, 'ln_f': ln_f, 'w_in': w_in, 'w_out': w_out,
            'nsa_wck': nsa_wck, 'nsa_wcv': nsa_wcv, 'dn_conv_w': dn_conv_w, 'dn_a_log': dn_a_log,
            'dn_dt_bias': dn_dt_bias, 'dn_norm_w': dn_norm_w, 's5_lambda_re': s5_lambda_re,
            's5_lambda_im': s5_lambda_im, 's5_log_step': s5_log_step, 's5_b_re': s5_b_re,
            's5_b_im': s5_b_im, 's5_c_re': s5_c_re, 's5_c_im': s5_c_im, 's5_d': s5_d,
            's5_w_glu': s5_w_glu, 'mlp_up': mlp_up, 'mlp_down': mlp_down}

def reference(x_prompt, x_sample, cache_nsa_kv, cache_win_kv, state_dn_conv, state_dn, state_s5_re,
              state_s5_im, page_table, ln1, ln2, ln_f, w_in, w_out, nsa_wck, nsa_wcv, dn_conv_w,
              dn_a_log, dn_dt_bias, dn_norm_w, s5_lambda_re, s5_lambda_im, s5_log_step, s5_b_re,
              s5_b_im, s5_c_re, s5_c_im, s5_d, s5_w_glu, mlp_up, mlp_down):
    B = x_prompt.shape[0]
    DB = x_sample.shape[0]
    n_pages = page_table.shape[1]
    page = cache_nsa_kv.shape[2]
    G, dh = NSA_KV_HEADS, HEAD_DIM
    f32 = jnp.float32
    xp, xs = x_prompt, x_sample
    outs_p, outs_s = [], []
    for l in range(DEPTH):
        p = {'ln1': ln1[l], 'ln2': ln2[l], 'w_in': w_in[l], 'w_out': w_out[l],
             'nsa_wck': nsa_wck[l], 'nsa_wcv': nsa_wcv[l], 'dn_conv_w': dn_conv_w[l],
             'dn_a_log': dn_a_log[l], 'dn_dt_bias': dn_dt_bias[l], 'dn_norm_w': dn_norm_w[l],
             's5_lambda_re': s5_lambda_re[l], 's5_lambda_im': s5_lambda_im[l],
             's5_log_step': s5_log_step[l], 's5_b_re': s5_b_re[l], 's5_b_im': s5_b_im[l],
             's5_c_re': s5_c_re[l], 's5_c_im': s5_c_im[l], 's5_d': s5_d[l], 's5_w_glu': s5_w_glu[l],
             'mlp_up': mlp_up[l], 'mlp_down': mlp_down[l]}
        xp, st_p = trunk_layer(
            xp, jnp.zeros((B, 0, 4, G, dh), xp.dtype), jnp.zeros((B, 0, 2, G, dh), xp.dtype),
            jnp.zeros((B, DN_CONV_W - 1, DN_CONV_DIM), xp.dtype),
            jnp.zeros((B, DN_HEADS, DN_DK, DN_DV), f32),
            jnp.zeros((B, S5_GROUPS, S5_STATE), f32), jnp.zeros((B, S5_GROUPS, S5_STATE), f32), p)
        past = cache_nsa_kv[l, page_table].reshape(DB, n_pages * page, 4, G, dh)
        xs, st_s = trunk_layer(xs, past, cache_win_kv[l], state_dn_conv[l], state_dn[l],
                               state_s5_re[l], state_s5_im[l], p)
        outs_p.append(st_p)
        outs_s.append(st_s)
    y_prompt = rmsnorm(xp, ln_f)
    y_sample = rmsnorm(xs, ln_f)

    def stk(outs, i):
        return jnp.stack([o[i] for o in outs], axis=0)

    kv_p, kv_s = stk(outs_p, 0), stk(outs_s, 0)
    win_p, win_s = stk(outs_p, 1), stk(outs_s, 1)
    conv_p, conv_s = stk(outs_p, 2), stk(outs_s, 2)
    dn_p, dn_s = stk(outs_p, 3), stk(outs_s, 3)
    s5re_p, s5re_s = stk(outs_p, 4), stk(outs_s, 4)
    s5im_p, s5im_s = stk(outs_p, 5), stk(outs_s, 5)
    return (y_prompt, y_sample, kv_p, kv_s, win_p, win_s, conv_p, conv_s, dn_p, dn_s,
            s5re_p, s5re_s, s5im_p, s5im_s)


_drawn_inputs = setup_inputs


def setup_inputs(seed=0):
    import zlib

    import numpy as np

    out = dict(_drawn_inputs(seed))
    spreads = {}
    factors = {'ln2': 9.615,
     'ln_f': 22.788,
     'dn_norm_w': 22.111,
     's5_lambda_re': 79.292,
     's5_c_re': 12.876,
     's5_c_im': 12.731,
     'nsa_wck': 3.351,
     's5_w_glu': 3.878}
    for name, (base, spread) in spreads.items():
        noise = np.random.default_rng([zlib.crc32(name.encode()), seed]).standard_normal(out[name].shape)
        drawn = base * np.exp(spread * noise) if base else spread * noise
        out[name] = jnp.asarray(drawn.astype(out[name].dtype))
    for name, factor in factors.items():
        out[name] = (out[name] * factor).astype(out[name].dtype)
    return out
```

```python
from contextlib import ExitStack

import numpy as np
import concourse.bass as bass
from concourse import mybir

P = 128
F32 = mybir.dt.float32
F32R = mybir.dt.float32r
I32 = mybir.dt.int32
ALU = mybir.AluOpType
ACT = mybir.ActivationFunctionType
AX = mybir.AxisListType

D = 1024
KT = D // P
SEQ = 1024
NB, NQ = 8, 8
TOK = SEQ + NB * NQ
TILES = SEQ // P + 1
ROWS = [P] * (TILES - 1) + [NB * NQ]
TS = TILES - 1
PADT = TILES * P
GROUPS_N = [(0, 364), (364, 364), (728, 360)]
HD = 64
G, R = 2, 4
PAST = 256
PAGES = 2
WINDOW = 512
KV = 768
KCMP, VCMP, KSEL, VSEL, KWIN, VWIN = (c * P for c in range(6))
SMALL = 24 + 8 + 256
FEAT = 12
PADC = 3 + SEQ + NB * (3 + NQ)
CONVN = PADC - 3
FF = 4096
FG = 256
EPS = 1e-6
NEG = -1e30
MFLOOR = -1e25
NCH = 8
LEVELS = 7
SLEVELS = 3



def constant_tables():
    p = np.arange(P)[:, None]
    f = np.float32
    t = {}
    t["ident"] = np.eye(P, dtype=f)
    t["ones"] = np.ones((P, P), f)
    j = np.arange(1024)[None, :] - 896
    t["dist_sel"] = np.where(j <= p, j - p, NEG).astype(f)
    jw = np.arange(640)[None, :] - 512
    t["dist_win"] = np.where((jw <= p) & (p - jw < WINDOW), jw - p, NEG).astype(f)
    blk = np.arange(16)[None, None, :]
    tok = np.arange(8)[None, :, None] * P + p[:, :, None]
    t["dist_cmp"] = np.where((blk + 1) * 64 - 1 <= tok, blk * 64 + 31.5 - tok, NEG).astype(f).reshape(P, -1)
    q, r, b4 = p % 8, (p // 8) % 4, p // 32
    past = np.arange(PAST)[None, :] - (PAST + q)
    new = np.arange(64)[None, :]
    dist, cmp_ = [], []
    for h in range(2):
        own = (new // 8 == b4 + 4 * h) & (new % 8 <= q)
        dist.append(np.concatenate([past, np.where(own, new % 8 - q, NEG)], 1))
        c = np.arange(32)[None, :]
        cmp_.append(np.where(c // 4 == b4 + 4 * h, (c % 4) * 64 + 31.5 - (PAST + q), NEG))
    t["sdist"] = np.concatenate(dist, 1).astype(f)
    t["sdist_cmp"] = np.concatenate(cmp_, 1).astype(f)
    t["sslope"] = np.concatenate([2.0 ** -(g * 4 + r + 1.0) for g in range(2)], 1).astype(f)
    sel = np.zeros((P, 2, 4, P), f)
    for h in range(2):
        for b in range(4):
            for rr in range(4):
                for qq in range(8):
                    sel[(4 * h + b) * 8 + qq, h, rr, b * 32 + rr * 8 + qq] = 1
    t["gate_sel"] = sel.reshape(P, -1)
    i = np.arange(P)[None, :]
    same = (p // 8 == i // 8) & (p < 64) & (i < 64)
    t["upto"] = (p <= i).astype(f)
    t["upto_s"] = ((p <= i) & same).astype(f)
    t["ones_s"] = same.astype(f)
    t["neg"] = np.where(p <= i, 0, NEG).astype(f)
    t["neg_s"] = np.where((p <= i) & (p // 8 == i // 8), 0, NEG).astype(f)
    t["level"] = np.concatenate([((i >> s) == (p >> s) + 1) & (i >> (s + 1) == p >> (s + 1))
                                 for s in range(LEVELS)], 1).astype(f)
    t["seq_col"] = np.concatenate([np.broadcast_to((np.arange(64)[None, :] // 8) == b, (P, 64))
                                   for b in range(8)], 1).astype(f)
    t["seq_row"] = np.concatenate([(p // 8) == b for b in range(8)], 1).astype(f)
    t["notfirst"] = np.broadcast_to((np.arange(64)[None, :] % 8) != 0, (P, 64)).astype(f)
    return t


CONST_AT = {}


def constants_array():
    t = constant_tables()
    at, cols = 0, []
    for k, v in t.items():
        CONST_AT[k] = (at, v.shape[1])
        at += v.shape[1]
        cols.append(v)
    return np.ascontiguousarray(np.concatenate(cols, 1))


class Link:

    def __init__(self, eng, sem):
        self.eng, self.sem, self.n = eng, sem, 0

    def __call__(self, ins):
        self.n += 1
        ins.then_inc(self.sem, 1)
        self.eng.wait_ge(self.sem, self.n)


class Memory:
    pass



def norm_transpose(nc, m, name, gain, outT, source, load):
    with ExitStack() as ctx:
        sb = lambda n, s: ctx.enter_context(nc.sbuf_tensor(f"{name}_{n}", s, F32))
        sem = m.sem
        if load:
            slots = sb("x", [P, 3, D])
        xn = sb("xn", [P, 2, D])
        whole = sb("whole", [P, 2, KT, P])
        junk = sb("junk", [P, D])
        stat = sb("stat", [P, 4, TILES])
        gainT = sb("gain", [P, KT])
        x_loaded = [sem(f"{name}_x_loaded{i}") for i in range(3)]
        gain_loaded = sem(f"{name}_gain_loaded")
        squared, var_ready, std_ready = sem(f"{name}_squared"), sem(f"{name}_var"), sem(f"{name}_std")
        normed, turned, evacuated = sem(f"{name}_normed"), sem(f"{name}_turned"), sem(f"{name}_evac")
        vec, hi_made, lo_made = sem(f"{name}_vec"), sem(f"{name}_hi_made"), sem(f"{name}_lo_made")
        hiT, loT = outT

        def x_at(t):
            return (slots[:ROWS[t], t % 3, :] if load else source[:ROWS[t], t, :])

        with nc.Block() as block:
            @block.sync
            def _(sp):
                sp.dma_start(gainT[:], gain).then_inc(gain_loaded, 16)
                if load:
                    for t in range(TILES):
                        if t >= 3:
                            sp.wait_ge(normed, t - 2)
                        src = m.x_prompt[t * P:(t + 1) * P, :] if t < TS else m.x_sample
                        sp.dma_start(x_at(t), src).then_inc(x_loaded[t % 3], 16)

            @block.gpsimd
            def _(pool):
                if hiT.shape[2] > TOK:
                    for part in outT:
                        pool.memset(part[:, :, TOK:].bitcast(F32), 0.0)

            @block.scalar
            def _(act):
                def square(t):
                    if load:
                        act.wait_ge(x_loaded[t % 3], 16 * (t // 3 + 1))
                    if t:
                        act.wait_ge(squared, t)
                    act.activation(junk[:ROWS[t], :], x_at(t), ACT.Square,
                                   accum_out=stat[:ROWS[t], 0, t:t + 1]).then_inc(squared, 1)

                def split(t):
                    n = ROWS[t]
                    act.wait_ge(evacuated, 2 * (t + 1))
                    act.activation(hiT[:, :, t * P:t * P + n], whole[:, t % 2, :, :n], ACT.Copy).then_inc(hi_made, 1)
                square(0)
                for t in range(TILES):
                    if t + 1 < TILES:
                        square(t + 1)
                    act.wait_ge(var_ready, t + 1)
                    act.activation(stat[:ROWS[t], 2, t:t + 1], stat[:ROWS[t], 1, t:t + 1],
                                   ACT.Sqrt).then_inc(std_ready, 1)
                    if t >= 2:
                        split(t - 2)
                split(TILES - 2)
                split(TILES - 1)

            @block.vector
            def _(dve):
                link = Link(dve, vec)

                def subtract(t):
                    n = ROWS[t]
                    dve.wait_ge(hi_made, t + 1)
                    dve.tensor_tensor(loT[:, :, t * P:t * P + n], whole[:, t % 2, :, :n], hiT[:, :, t * P:t * P + n],
                                      ALU.subtract).then_inc(lo_made, 1)

                def evacuate(t):
                    dve.wait_ge(turned, t + 1)
                    if t >= 2:
                        dve.wait_ge(lo_made, t - 1)
                    for h in range(2):
                        bank = m.ps[:, (t % 2) * 2 + h, :].rearrange("p (k n) -> p k n", k=4)[:, :, :ROWS[t]]
                        dve.tensor_tensor(whole[:, t % 2, 4 * h:4 * h + 4, :ROWS[t]], bank,
                                          gainT[:, 4 * h:4 * h + 4].unsqueeze(2).to_broadcast([P, 4, ROWS[t]]),
                                          ALU.mult).then_inc(evacuated, 1)
                dve.wait_ge(gain_loaded, 16)
                for t in range(TILES):
                    n = ROWS[t]
                    dve.wait_ge(squared, t + 1)
                    dve.tensor_scalar(stat[:n, 1, t:t + 1], stat[:n, 0, t:t + 1], 1.0 / D, EPS,
                                      ALU.mult, ALU.add).then_inc(var_ready, 1)
                    dve.wait_ge(std_ready, t + 1)
                    link(dve.reciprocal(stat[:n, 3, t:t + 1], stat[:n, 2, t:t + 1]))
                    if t >= 2:
                        dve.wait_ge(turned, t - 1)
                    dve.tensor_scalar(xn[:n, t % 2, :], x_at(t), stat[:n, 3, t:t + 1], None,
                                      ALU.mult).then_inc(normed, 1)
                    if t >= 3:
                        subtract(t - 3)
                    if t:
                        evacuate(t - 1)
                subtract(TILES - 3)
                evacuate(TILES - 1)
                subtract(TILES - 2)
                subtract(TILES - 1)

            @block.tensor
            def _(pe):
                for t in range(TILES):
                    pe.wait_ge(normed, t + 1)
                    if t >= 2:
                        pe.wait_ge(evacuated, 2 * (t - 1))
                    for k in range(KT):
                        last = pe.transpose(m.ps[:, (t % 2) * 2 + k // 4, (k % 4) * P:(k % 4) * P + ROWS[t]],
                                            xn[:ROWS[t], t % 2, k * P:(k + 1) * P],
                                            m.ident[:ROWS[t], :ROWS[t]])
                    last.then_inc(turned, 1)


def triple(pe, out, lhs, rhs, first, last):
    pe.matmul(out, lhs[0], rhs[0], start=first, stop=False)
    pe.matmul(out, lhs[0], rhs[1], start=False, stop=False)
    return pe.matmul(out, lhs[1], rhs[0], start=False, stop=last)



def project(nc, m, name, chunks, widths, units, evacuation, extra):
    with ExitStack() as ctx:
        sem = lambda n: m.sem(f"{name}_{n}")
        NC, W, BANKS = len(chunks), KT * max(widths), 8
        raw = ctx.enter_context(nc.sbuf_tensor(f"{name}_raw", [P, W], F32))
        hi, lo = (ctx.enter_context(nc.sbuf_tensor(f"{name}_{n}", [P, 2, W], F32R)) for n in ("whi", "wlo"))
        w_loaded, hi_made, lo_made, product = (sem(n) for n in ("w_loaded", "hi_made", "lo_made", "product"))
        evac = [sem("evac_act"), sem("evac_dve")]
        ends = [max(u for u, unit in enumerate(units) if unit[0] == c) + 1 for c in range(NC)]
        begins = [0] + ends[:-1]

        def slot(t, c):
            return t[:, c % 2, :KT * widths[c]].rearrange("p (k n) -> p k n", k=KT)

        with nc.Block() as block:
            @block.sync
            def _(sp):
                for c in range(NC):
                    if c:
                        sp.wait_ge(lo_made, c)
                    sp.dma_start(raw[:, :KT * widths[c]], chunks[c]).then_inc(w_loaded, 16)
                extra["sync"](sp, evac)

            @block.gpsimd
            def _(pool):
                extra["gpsimd"](pool)

            @block.scalar
            def _(act):
                def round_weights(c):
                    act.wait_ge(w_loaded, 16 * (c + 1))
                    if c >= 2:
                        act.wait_ge(product, ends[c - 2])
                    n = KT * widths[c]
                    act.activation(hi[:, c % 2, :n], raw[:, :n], ACT.Copy).then_inc(hi_made, 1)
                round_weights(0)
                for u in range(len(units)):
                    if u in begins and begins.index(u) + 1 < NC:
                        round_weights(begins.index(u) + 1)
                    if u % 2 == 0:
                        act.wait_ge(product, u + 1)
                        evacuation(act, True, u).then_inc(evac[0], 1)

            @block.vector
            def _(dve):
                def rest_of_weights(c):
                    dve.wait_ge(hi_made, c + 1)
                    n = KT * widths[c]
                    dve.tensor_tensor(lo[:, c % 2, :n], raw[:, :n], hi[:, c % 2, :n], ALU.subtract).then_inc(lo_made, 1)
                rest_of_weights(0)
                for u in range(len(units)):
                    if u in begins and begins.index(u) + 1 < NC:
                        rest_of_weights(begins.index(u) + 1)
                    if u % 2:
                        dve.wait_ge(product, u + 1)
                        evacuation(dve, False, u).then_inc(evac[1], 1)

            @block.tensor
            def _(pe):
                for u, (c, n) in enumerate(units):
                    if u in begins:
                        pe.wait_ge(lo_made, c + 1)
                    if u >= BANKS:
                        pe.wait_ge(evac[u % 2], (u - BANKS) // 2 + 1)
                    w = (slot(hi, c), slot(lo, c))
                    for k in range(KT):
                        wk = [x[:, k, :] for x in w]
                        if extra["feature"]:
                            o, width = GROUPS_N[n]
                            last = triple(pe, m.ps[:, u % BANKS, :width], wk, [x[:, k, o:o + width] for x in m.hT2],
                                          k == 0, k == KT - 1)
                        else:
                            last = triple(pe, m.ps[:, u % BANKS, :widths[c]],
                                          [x[:, k, n * P:(n + 1) * P] for x in m.hT2], wk, k == 0, k == KT - 1)
                    last.then_inc(product, 1)


def token_projection(nc, m):
    stored, zeroed = m.sem("proj_stored"), m.sem("kv_zeroed")
    units = [(c, t) for c in range(3) for t in range(TILES)]
    widths = [384, 384, SMALL]

    def evacuation(eng, scalar, u):
        c, t = units[u]
        rows = ROWS[t]
        src = m.ps[:rows, u % 8, :widths[c]]
        dst = m.kv[:rows, t, 384 * c:384 * c + 384] if c < 2 else m.small[:rows, t, :]
        return eng.activation(dst, src, ACT.Copy) if scalar else eng.tensor_copy(dst, src)

    def sync(sp, evac):
        sp.wait_ge(evac[0], (len(units) + 1) // 2)
        sp.wait_ge(evac[1], len(units) // 2)
        for t in range(TS):
            sp.dma_start(m.kv_prompt[t * P:(t + 1) * P, :], m.kv[:, t, 0:512]).then_inc(stored, 16)
            if t >= TS // 2:
                sp.dma_start(m.win_prompt[(t - 4) * P:(t - 3) * P, :], m.kv[:, t, 512:768]).then_inc(stored, 16)
        sp.dma_start(m.kv_sample, m.kv[:NB * NQ, TS, 0:512]).then_inc(stored, 16)
        for b in range(NB):
            sp.dma_start(m.win_sample[b, PAST:PAST + NQ, :],
                         m.kv[b * NQ:(b + 1) * NQ, TS, 512:768]).then_inc(stored, 16)
        sp.dma_start(m.win_sample[:, 0:PAST, :], m.cache_win).then_inc(stored, 16)

    def gpsimd(pool):
        pool.memset(m.small[64:128, TS, :], 0.0).then_inc(zeroed, 1)

    project(nc, m, "kvp", m.w_in[FEAT:], widths, units, evacuation,
            {"sync": sync, "gpsimd": gpsimd, "feature": False})


def feature_projection(nc, m):
    with ExitStack() as ctx:
        convbuf = ctx.enter_context(nc.sbuf_tensor("convbuf", [P, 6, NB, 3], F32))
        stored, conv_in, conv_put = m.sem("proj_stored"), m.sem("conv_in"), m.sem("conv_put")
        units = [(c, n) for c in range(FEAT) for n in range(3)]

        def evacuation(eng, scalar, u):
            c, n = units[u]
            o, w = GROUPS_N[n]
            src = m.ps[:, u % 8, :w]
            if c < 4:
                dst = m.qT[:, c, o:o + w]
                if scalar:
                    return eng.activation(dst, src, ACT.Copy, scale=0.125)
                return eng.tensor_scalar(dst, src, 0.125, None, ALU.mult)
            if c >= 10:
                dst = m.uT[:, c - 10, o:o + w]
            elif n < 2:
                dst = m.dnx[:, c - 4, 3 + o:3 + o + w]
            else:
                dst, part = m.dnx[:, c - 4, 3 + o:3 + SEQ], src[:, :SEQ - o]
                if scalar:
                    eng.activation(dst, part, ACT.Copy)
                else:
                    eng.tensor_copy(dst, part)
                dst = m.dnx[:, c - 4, 3 + SEQ:].rearrange("p (b s) -> p b s", b=NB)[:, :, 3:]
                src = src[:, SEQ - o:].rearrange("p (b s) -> p b s", b=NB)
            return eng.activation(dst, src, ACT.Copy) if scalar else eng.tensor_copy(dst, src)

        def sync(sp, evac):
            sp.wait_ge(evac[0], (len(units) + 1) // 2)
            sp.wait_ge(evac[1], len(units) // 2)
            sp.wait_ge(conv_put, 7)
            sp.dma_start(m.conv_prompt, m.dnx[:, :, SEQ:SEQ + 3]).then_inc(stored, 16)
            for f in range(6):
                sp.dma_start(m.conv_sample[:, f],
                             m.dnx[:, f, 3 + SEQ:].rearrange("p (b s) -> p b s", b=NB)[:, :, NQ:NQ + 3]
                             ).then_inc(stored, 16)

        def gpsimd(pool):
            pool.dma_start(convbuf[:], m.state_conv).then_inc(conv_in, 16)
            pool.memset(m.dnx[:, :, 0:3], 0.0).then_inc(conv_put, 1)
            pool.wait_ge(conv_in, 16)
            pool.wait_ge(conv_put, 1)
            for f in range(6):
                pool.tensor_copy(m.dnx[:, f, 3 + SEQ:].rearrange("p (b s) -> p b s", b=NB)[:, :, 0:3],
                                 convbuf[:, f]).then_inc(conv_put, 1)

        project(nc, m, "fp", m.w_in[:FEAT], [P] * FEAT, units, evacuation,
                {"sync": sync, "gpsimd": gpsimd, "feature": True})


STORES_OF_INPUT = TS + TS // 2 + 1 + NB + 1 + 1 + 6



def delta_net(nc, m):
    with ExitStack() as ctx:
        sb = lambda n, s: ctx.enter_context(nc.sbuf_tensor(f"dn_{n}", s, F32))
        sem = lambda n: m.sem(f"dn_{n}")
        H = 4
        NT = TILES
        flat_hT = m.mixT[:].rearrange("p k n -> p (k n)")
        conv = flat_hT[:, :6 * PADC].rearrange("p (f n) -> p f n", f=6)
        convs = sb("convs", [P, 6, NB * NQ])
        names = ["ones", "ones_s", "upto", "upto_s", "neg", "neg_s", "level", "seq_col", "seq_row"]
        C = {n: sb(n, [P, CONST_AT[n][1]]) for n in names}
        convw, alog, dtb, normw = sb("convw", [P, 6, 4]), sb("alog", [P, H]), sb("dtb", [P, H]), sb("normw", [P, HD])
        minus_half = sb("minus_half", [P, NT * H])
        gate = sb("gate", [P, 12, NT, H])
        X, GG, BETA, GC, GL, NGC, EGC, EGL, EDEC, T0, T1, T2 = range(12)
        gm = sb("gm", [64, NB, H])
        egl_s = sb("egl_s", [P, NB, H])
        o_all = sb("o", [P, NT, 256])
        qk = sb("qk", [P, 2, 512])
        sq = sb("sq", [P, 512])
        ssq = sb("ssq", [P, 2, 8])
        rnorm = sb("rnorm", [P, 2, 8])
        kb, kbg, qg = sb("kb", [P, 256]), sb("kbg", [P, 2, 256]), sb("qg", [P, 256])
        kdec, vb = sb("kdec", [P, 2, 256]), sb("vb", [P, 2, 256])
        featT = sb("featT", [P, 2, 8, P])
        decay = sb("decay", [P, H, P])
        AT, aqkT = sb("AT", [P, 2, H, P]), sb("aqkT", [P, 2, H, P])
        B, U, T, TT = (sb(n, [P, 2, H, P]) for n in ("B", "U", "T", "TT"))
        wT = sb("wT", [P, 2, 2, P])
        S = sb("S", [P, 2, P])
        vnew = sb("vnew", [P, 256])

        tables, params = sem("tables"), sem("params")
        conv_made, silu_made = sem("conv_made"), sem("silu_made")
        vec, vec_pool, vec_act = sem("vec"), sem("vec_pool"), sem("vec_act")
        x_ready, ex_ready, lnin, ln_ready, g_ready = (sem(n) for n in ("x_ready", "ex_ready", "lnin", "ln_ready", "g_ready"))
        sums, sums_out, gexp = sem("sums"), sem("sums_out"), sem("gexp")
        raw, qk_out, vb_out = sem("raw"), sem("qk_out"), sem("vb_out")
        ssq_ready, rnorm_ready, normed = sem("ssq_ready"), sem("rnorm_ready"), sem("normed")
        scaled, turned, feat_out = sem("scaled"), sem("turned"), sem("feat_out")
        drow, decay_ready = sem("drow"), sem("decay_ready")
        gram, a_ready = sem("gram"), sem("a_ready")
        b_ready, bt, u_ready, tut, t_ready = sem("b_ready"), sem("bt"), sem("u_ready"), sem("tut"), sem("t_ready")
        wprod, w_ready = sem("wprod"), sem("w_ready")
        vprod, v_ready, oprod, o_out, sprod, s_ready = (sem(n) for n in ("vprod", "v_ready", "oprod", "o_out", "sprod", "s_ready"))
        s_zero, stored, s_in = sem("s_zero"), sem("stored"), sem("s_in")
        osq, orn, fin, fturn, fout, zsilu = (sem(n) for n in ("osq", "orn", "fin", "fturn", "fout", "zsilu"))
        masked, ss_ready = sem("masked"), sem("ss_ready")
        Ss = sb("Ss", [P, NB, 2, P])
        wTm = B[:].rearrange("p a h n -> p (a h n)").rearrange("p (c b n) -> p c b n", c=2, b=NB)
        qgm = U[:].rearrange("p a h n -> p (a h n)").rearrange("p (c b n) -> p c b n", c=2, b=NB)

        def kdecm(b):
            t = (AT if b < 4 else T)[:].rearrange("p a h n -> p (a h n)")
            return t[:64, (b % 4) * 256:(b % 4) * 256 + 256]

        def order(k, s):
            if k == TS:
                return TS * LEVELS + s + 1
            return (k // 2) * 2 * LEVELS + 2 * s + k % 2 + 1

        def order1(k, s):
            if k == TS:
                return TS * (LEVELS - 1) + s
            return (k // 2) * 2 * (LEVELS - 1) + 2 * (s - 1) + k % 2 + 1

        def pairs():
            return [(0, 1), (2, 3), (4, 5), (6, 7), (TS,)]

        def levels(k):
            return SLEVELS if k == TS else LEVELS

        def heads(t):
            return t.rearrange("p (h n) -> p h n", h=H)

        with nc.Block() as block:
            @block.sync
            def _(sp):
                sp.dma_start(convw[:], m.conv_w).then_inc(params, 16)
                sp.dma_start(alog[:], m.a_log).then_inc(params, 16)
                sp.dma_start(dtb[:], m.dt_bias).then_inc(params, 16)
                sp.dma_start(normw[:], m.norm_w).then_inc(params, 16)
                for n in names:
                    at, w = CONST_AT[n]
                    sp.dma_start(C[n][:], m.const[:, at:at + w]).then_inc(tables, 16)
                sp.dma_start(Ss[:], m.state_dn).then_inc(s_in, 16)
                sp.wait_ge(s_ready, TS)
                for h in range(2):
                    half = slice(64 * h, 64 * h + 64)
                    sp.dma_start(m.dn_prompt[half], S[half, :, half]).then_inc(stored, 16)
                sp.wait_ge(ss_ready, H)
                for h in range(2):
                    half = slice(64 * h, 64 * h + 64)
                    for c in range(2):
                        sp.dma_start(m.dn_sample[half, :, c], Ss[half, :, c, half]).then_inc(stored, 16)
                sp.wait_ge(stored, 16 * 6)
                sp.wait_ge(m.sem("proj_stored"), 16 * STORES_OF_INPUT)

            @block.gpsimd
            def _(pool):
                link = Link(pool, vec_pool)
                link(pool.memset(o_all[64:128, TS, :], 0.0))
                link(pool.memset(minus_half[:], -0.5))
                pool.memset(S[:], 0.0).then_inc(s_zero, 1)
                for pair in pairs():
                    for k in pair:
                        n, x = ROWS[k], k % 2
                        bc = lambda c: gate[:n, c, k, :].unsqueeze(2).to_broadcast([n, H, HD])
                        pool.wait_ge(ssq_ready, k + 1)
                        pool.tensor_tensor(rnorm[:n, x, :], ssq[:n, x, :], minus_half[:n, :8], ALU.pow).then_inc(rnorm_ready, 1)
                        pool.wait_ge(normed, k + 1)
                        pool.wait_ge(gexp, 3)
                        if k:
                            pool.wait_ge(turned, k)
                        kn = heads(qk[:n, x, 256:512])
                        pool.tensor_tensor(heads(kb[:n, :]), kn, bc(BETA), ALU.mult).then_inc(scaled, 1)
                        pool.tensor_tensor(heads(qg[:n, :]), heads(qk[:n, x, 0:256]), bc(EGC), ALU.mult).then_inc(scaled, 1)
                        if k >= 2:
                            pool.wait_ge(wprod, k - 1)
                            pool.wait_ge(sprod, k - 1)
                        pool.tensor_tensor(heads(kdec[:n, x, :]), kn, bc(EDEC), ALU.mult).then_inc(scaled, 1)
                        pool.wait_ge(scaled, 4 * k + 1)
                        pool.tensor_tensor(heads(kbg[:n, x, :]), heads(kb[:n, :]), bc(EGC), ALU.mult).then_inc(scaled, 1)
                    for s in range(levels(pair[0])):
                        for k in pair:
                            n, x = ROWS[k], k % 2
                            pool.wait_ge(a_ready, 4 * (k + 1))
                            if s:
                                pool.wait_ge(bt, order(k, s - 1))
                                pool.wait_ge(t_ready, order(k, s - 1))
                            mask = C["level"][:n, s * P:s * P + n].unsqueeze(1).to_broadcast([n, H, n])
                            pool.tensor_tensor(B[:n, x, :, :n], AT[:n, x, :, :n], mask, ALU.mult).then_inc(b_ready, 1)
                pool.wait_ge(osq, 1)
                pool.tensor_tensor(gate[:, T1].rearrange("p t h -> p (t h)"), gate[:, T0].rearrange("p t h -> p (t h)"),
                                   minus_half[:], ALU.pow).then_inc(orn, 1)

            @block.scalar
            def _(act):
                for f in range(6):
                    act.wait_ge(conv_made, f + 1)
                    act.activation(conv[:, f, :SEQ], conv[:, f, :SEQ], ACT.Silu).then_inc(silu_made, 1)
                    act.activation(convs[:, f].rearrange("p (b q) -> p b q", b=NB),
                                   conv[:, f, 3 + SEQ:].rearrange("p (b s) -> p b s", b=NB)[:, :, :NQ],
                                   ACT.Silu).then_inc(silu_made, 1)
                act.wait_ge(x_ready, 1)
                act.activation(gate[:, T1], gate[:, T0], ACT.Exp).then_inc(ex_ready, 1)
                act.activation(gate[:, T2], m.small[:, :, 28:32], ACT.Exp, scale=-1.0).then_inc(ex_ready, 1)
                act.activation(alog[:], alog[:], ACT.Exp).then_inc(ex_ready, 1)
                act.wait_ge(lnin, 1)
                act.activation(gate[:, T1], gate[:, T1], ACT.Ln, bias=1.0).then_inc(ln_ready, 1)
                act.wait_ge(sums_out, 1)
                act.activation(gate[:, EGC], gate[:, GC], ACT.Exp).then_inc(gexp, 1)
                act.activation(gate[:, EGL], gate[:, GL], ACT.Exp).then_inc(gexp, 1)
                act.activation(gate[:, EDEC], gate[:, T0], ACT.Exp).then_inc(gexp, 1)
                act.activation(egl_s[:], m.ps[:, 0, 128:160].rearrange("p (b h) -> p b h", b=NB), ACT.Exp).then_inc(gexp, 1)
                for pair in pairs():
                    for k in pair:
                        n, x = ROWS[k], k % 2
                        act.wait_ge(raw, k + 1)
                        if k:
                            act.wait_ge(ssq_ready, k)
                        if k >= 2:
                            act.wait_ge(scaled, 4 * (k - 1))
                            act.wait_ge(turned, k - 1)
                        act.activation(sq[:n, :], m.ps[:n, 4 * x, :], ACT.Square).then_inc(qk_out, 1)
                        act.activation(qk[:n, x, :], m.ps[:n, 4 * x, :], ACT.Copy).then_inc(qk_out, 1)
                        act.wait_ge(turned, k + 1)
                        if k >= 2:
                            act.wait_ge(oprod, k - 1)
                        for c in range(2):
                            act.activation(featT[:, x, 4 * c:4 * c + 4, :n],
                                           heads(m.ps[:, 4 * x + 2 + c, :])[:, :, :n], ACT.Copy).then_inc(feat_out, 1)
                        act.wait_ge(drow, k + 1)
                        if k:
                            act.wait_ge(a_ready, 4 * k)
                        for h in range(H):
                            act.activation(decay[:n, h, :n], m.ps[:n, 4 * x, h * P:h * P + n], ACT.Exp,
                                           bias=gate[:n, NGC, k, h:h + 1]).then_inc(decay_ready, 1)
                    for s in range(1, levels(pair[0])):
                        for k in pair:
                            n, x = ROWS[k], k % 2
                            act.wait_ge(bt, order(k, s))
                            if s > 1:
                                act.wait_ge(tut, order1(k, s - 1))
                            elif k >= 2:
                                act.wait_ge(tut, order1(k - 2, LEVELS - 1))
                            act.activation(U[:n, x, :, :n], heads(m.ps[:n, 4 * x, :])[:, :, :n], ACT.Copy).then_inc(u_ready, 1)
                    for k in pair:
                        n, x = ROWS[k], k % 2
                        act.wait_ge(wprod, k + 1)
                        for h in range(2):
                            act.activation(wT[64 * h:64 * h + 64, x, :, :n],
                                           heads(m.ps[64 * h:64 * h + 64, 4 * x, :])[:, h::2, :n],
                                           ACT.Copy, scale=-1.0).then_inc(w_ready, 1)
                        act.wait_ge(vprod, k + 1)
                        if k:
                            act.wait_ge(oprod, k)
                        act.activation(vnew[:n, :], m.ps[:n, 4 * x + 1, :256], ACT.Copy).then_inc(v_ready, 1)
                act.activation(m.small[:, :, 32:], m.small[:, :, 32:], ACT.Silu).then_inc(zsilu, 1)
                for k in range(NT):
                    act.wait_ge(fturn, k + 1)
                    act.activation(m.mixT[:, 4:6, k * P:k * P + ROWS[k]],
                                   heads(m.ps[:, k % 2, :])[:, 0:2, :ROWS[k]], ACT.Copy).then_inc(fout, 1)

            @block.vector
            def _(dve):
                link = Link(dve, vec)
                dve.wait_ge(params, 64)
                for j in range(4):
                    for f in range(6):
                        src, w = m.dnx[:, f, j:j + CONVN], convw[:, f, j:j + 1]
                        if j == 0:
                            last = dve.tensor_scalar(conv[:, f, :CONVN], src, w, None, ALU.mult)
                        else:
                            last = dve.scalar_tensor_tensor(conv[:, f, :CONVN], src, w, conv[:, f, :CONVN], ALU.mult, ALU.add)
                        if j == 3:
                            last.then_inc(conv_made, 1)
                        elif f == 5:
                            link(last)
                bcH = lambda t: t[:].unsqueeze(1).to_broadcast([P, NT, H])
                link(dve.tensor_tensor(gate[:, X], m.small[:, :, 24:28], bcH(dtb), ALU.add))
                link(dve.tensor_scalar(gate[:, T1], gate[:, X], -1.0, None, ALU.mult))
                dve.tensor_tensor(gate[:, T0], gate[:, X], gate[:, T1], ALU.min).then_inc(x_ready, 1)
                dve.wait_ge(ex_ready, 3)
                link(dve.tensor_scalar(gate[:, T2], gate[:, T2], 1.0, None, ALU.add))
                dve.reciprocal(gate[:, BETA], gate[:, T2]).then_inc(lnin, 1)
                dve.wait_ge(ln_ready, 1)
                link(dve.tensor_scalar(gate[:, X], gate[:, X], 0.0, None, ALU.max))
                link(dve.tensor_tensor(gate[:, X], gate[:, X], gate[:, T1], ALU.add))
                link(dve.tensor_tensor(gate[:, X], gate[:, X], bcH(alog), ALU.mult))
                link(dve.tensor_scalar(gate[:, GG], gate[:, X], -1.0, None, ALU.mult))
                dve.wait_ge(tables, 16 * len(names))
                dve.tensor_tensor(gm[:], gate[:64, GG, TS, :].unsqueeze(1).to_broadcast([64, NB, H]),
                                  C["seq_row"][:64, :].unsqueeze(2).to_broadcast([64, NB, H]), ALU.mult).then_inc(g_ready, 1)
                dve.wait_ge(sums, 1)
                link(dve.tensor_copy(gate[:, GC], m.ps[:, 0, 0:36].rearrange("p (t h) -> p t h", t=NT)))
                link(dve.tensor_copy(gate[:, GL], m.ps[:, 0, 64:100].rearrange("p (t h) -> p t h", t=NT)))
                link(dve.tensor_scalar(gate[:, NGC], gate[:, GC], -1.0, None, ALU.mult))
                dve.tensor_tensor(gate[:, T0], gate[:, GL], gate[:, GC], ALU.subtract).then_inc(sums_out, 1)
                for pair in pairs():
                    for k in pair:
                        n, x = ROWS[k], k % 2
                        dve.wait_ge(raw, k + 1)
                        if k >= 2:
                            dve.wait_ge(vprod, k - 1)
                        dve.tensor_tensor(heads(vb[:n, x, :]), heads(m.ps[:n, 4 * x + 1, 0:256]),
                                          gate[:n, BETA, k, :].unsqueeze(2).to_broadcast([n, H, HD]),
                                          ALU.mult).then_inc(vb_out, 1)
                        dve.wait_ge(qk_out, 2 * k + 2)
                        link(dve.tensor_reduce(ssq[:n, x, :], sq[:n, :].rearrange("p (h d) -> p h d", h=8), AX.X, ALU.add))
                        link(dve.tensor_scalar(ssq[:n, x, :], ssq[:n, x, :], 1e-6, None, ALU.add))
                        dve.tensor_scalar(ssq[:n, x, 0:4], ssq[:n, x, 0:4], 64.0, None, ALU.mult).then_inc(ssq_ready, 1)
                        dve.wait_ge(rnorm_ready, k + 1)
                        v = qk[:n, x, :].rearrange("p (h d) -> p h d", h=8)
                        dve.tensor_tensor(v, v, rnorm[:n, x, :].unsqueeze(2).to_broadcast([n, 8, HD]),
                                          ALU.mult).then_inc(normed, 1)
                        dve.wait_ge(gram, k + 1)
                        dve.wait_ge(decay_ready, 4 * (k + 1))
                        for h in range(2):
                            bank = heads(m.ps[:n, 4 * x + (1, 2)[h], :])
                            dve.tensor_tensor(AT[:n, x, h::2, :n], bank[:, 0:2, :n], decay[:n, h::2, :n], ALU.mult).then_inc(a_ready, 1)
                            dve.tensor_tensor(aqkT[:n, x, h::2, :n], bank[:, 2:4, :n], decay[:n, h::2, :n], ALU.mult).then_inc(a_ready, 1)
                    for s in range(levels(pair[0])):
                        for k in pair:
                            n, x = ROWS[k], k % 2
                            if s == 0:
                                eye = m.ident[:n, :n].unsqueeze(1).to_broadcast([n, H, n])
                                dve.wait_ge(b_ready, order(k, 0))
                                link(dve.tensor_tensor(TT[:n, x, :, :n], eye, B[:n, x, :, :n], ALU.subtract))
                                dve.wait_ge(bt, order(k, 0))
                                dve.tensor_tensor(T[:n, x, :, :n], eye, heads(m.ps[:n, 4 * x, :])[:, :, :n],
                                                  ALU.subtract).then_inc(t_ready, 1)
                                continue
                            dve.wait_ge(tut, order1(k, s))
                            if s < levels(k) - 1:
                                link(dve.tensor_tensor(T[:n, x, :, :n], T[:n, x, :, :n],
                                                       heads(m.ps[:n, 4 * x + 1, :])[:, :, :n], ALU.subtract))
                            dve.tensor_tensor(TT[:n, x, :, :n], TT[:n, x, :, :n],
                                              heads(m.ps[:n, 4 * x + 3, :])[:, :, :n], ALU.subtract).then_inc(t_ready, 1)
                    for k in pair:
                        if k == TS:
                            continue
                        x = k % 2
                        dve.wait_ge(sprod, k + 1)
                        for h in range(H):
                            half = slice(64 * (h % 2), 64 * (h % 2) + 64)
                            blk = S[half, h // 2, half]
                            last = dve.scalar_tensor_tensor(blk, blk, gate[half, EGL, k, h:h + 1],
                                                            m.ps[half, 4 * x + 3, (h // 2) * P + 64 * (h % 2):(h // 2) * P + 64 * (h % 2) + 64],
                                                            ALU.mult, ALU.add)
                        last.then_inc(s_ready, 1)
                        dve.wait_ge(oprod, k + 1)
                        dve.tensor_copy(o_all[:, k, :], m.ps[:, 4 * x + 2, :256]).then_inc(o_out, 1)
                n = NB * NQ
                dve.wait_ge(w_ready, 2 * NT)
                col = C["seq_col"][:].rearrange("p (b n) -> p b n", b=NB)
                for c in range(2):
                    dve.tensor_tensor(wTm[:, c], wT[:, 0, c, :n].unsqueeze(1).to_broadcast([P, NB, n]), col, ALU.mult)
                    dve.tensor_tensor(qgm[:, c], featT[:, 0, 6 + c, :n].unsqueeze(1).to_broadcast([P, NB, n]), col, ALU.mult)
                for b in range(NB):
                    last = dve.tensor_scalar(kdecm(b), kdec[:n, 0, :], C["seq_row"][:n, b:b + 1], None, ALU.mult)
                last.then_inc(masked, 1)
                dve.wait_ge(sprod, NT)
                for h in range(H):
                    half = slice(64 * (h % 2), 64 * (h % 2) + 64)
                    blk = Ss[half, :, h // 2, half]
                    link(dve.tensor_tensor(blk, blk, egl_s[half, :, h:h + 1].to_broadcast([64, NB, 64]), ALU.mult))
                    upd = m.ps[half, 4:8, :].rearrange("p a n -> p (a n)").rearrange("p (b c n) -> p b c n", b=NB, c=2)
                    dve.tensor_tensor(blk, blk, upd[:, :, h // 2, half], ALU.add).then_inc(ss_ready, 1)
                dve.wait_ge(oprod, NT)
                dve.tensor_copy(o_all[:n, TS, :], m.ps[:n, 2, :256]).then_inc(o_out, 1)
                dve.wait_ge(o_out, NT)
                dve.wait_ge(vec_pool, 2)
                flat = o_all[:].rearrange("p t (h d) -> p (t h) d", h=H)
                squares = flat_hT[:, :NT * 256]
                link(dve.tensor_tensor(squares, o_all[:].rearrange("p t n -> p (t n)"), o_all[:].rearrange("p t n -> p (t n)"), ALU.mult))
                link(dve.tensor_reduce(gate[:, T0].rearrange("p t h -> p (t h)"), squares.rearrange("p (a d) -> p a d", d=HD), AX.X, ALU.add))
                dve.tensor_scalar(gate[:, T0], gate[:, T0], 1.0 / HD, EPS, ALU.mult, ALU.add).then_inc(osq, 1)
                link(dve.tensor_tensor(flat, flat, normw[:].unsqueeze(1).to_broadcast([P, NT * H, HD]), ALU.mult))
                dve.wait_ge(orn, 1)
                link(dve.tensor_tensor(flat, flat, gate[:, T1].rearrange("p t h -> p (t h)").unsqueeze(2).to_broadcast([P, NT * H, HD]), ALU.mult))
                dve.wait_ge(zsilu, 1)
                dve.tensor_tensor(o_all[:], o_all[:], m.small[:, :, 32:], ALU.mult).then_inc(fin, 1)

            @block.tensor
            def _(pe):
                pe.wait_ge(tables, 16 * len(names))
                pe.wait_ge(g_ready, 1)
                g = gate[:, GG, 0:TS, :].rearrange("p t h -> p (t h)")
                bank = m.ps[:, 0, :]
                pe.matmul(bank[:, 0:32], C["upto"][:], g, start=True, stop=True)
                pe.matmul(bank[:, 32:36], C["upto_s"][:64, :], gate[:64, GG, TS, :], start=True, stop=True)
                pe.matmul(bank[:, 64:96], C["ones"][:], g, start=True, stop=True)
                pe.matmul(bank[:, 96:100], C["ones_s"][:64, :], gate[:64, GG, TS, :], start=True, stop=True)
                pe.matmul(bank[:, 128:160], C["ones"][:64, :], gm[:].rearrange("p b h -> p (b h)"),
                          start=True, stop=True).then_inc(sums, 1)
                pe.wait_ge(silu_made, 12)
                pe.wait_ge(gexp, 4)
                for pair in pairs():
                    for k in pair:
                        n, x = ROWS[k], k % 2
                        if k >= 2:
                            pe.wait_ge(v_ready, k - 1)
                            pe.wait_ge(o_out, k - 1)
                            pe.wait_ge(s_ready, k - 1)
                            pe.wait_ge(w_ready, 2 * (k - 1))
                        for f in range(6):
                            if k < TS:
                                src = conv[:, f, k * P:(k + 1) * P]
                            else:
                                src = convs[:, f, :]
                            last = pe.transpose(m.ps[:n, 4 * x + f // 4, (f % 4) * P:(f % 4) * P + P], src, m.ident[:])
                        last.then_inc(raw, 1)
                        pe.wait_ge(normed, k + 1)
                        pe.wait_ge(scaled, 4 * k + 2)
                        for c, src in enumerate((qk[:n, x, 0:128], qk[:n, x, 128:256], qk[:n, x, 256:384], qk[:n, x, 384:512],
                                                 kb[:n, 0:128], kb[:n, 128:256], qg[:n, 0:128], qg[:n, 128:256])):
                            last = pe.transpose(m.ps[:, 4 * x + 2 + c // 4, (c % 4) * P:(c % 4) * P + n], src, m.ident[:n, :n])
                        last.then_inc(turned, 1)
                        pe.wait_ge(qk_out, 2 * k + 2)
                        for h in range(H):
                            row = m.ps[:n, 4 * x, h * P:h * P + n]
                            pe.matmul(row, gate[:n, GG, k, h:h + 1].to_broadcast([n, n]),
                                      C["upto" if k < TS else "upto_s"][:n, :n], start=True, stop=False)
                            last = pe.matmul(row, m.ident[:n, :n], C["neg" if k < TS else "neg_s"][:n, :n], start=False, stop=True)
                        last.then_inc(drow, 1)
                        pe.wait_ge(feat_out, 2 * k + 2)
                        pe.wait_ge(vb_out, k + 1)
                        for h in (0, 2, 1, 3):
                            half = slice(64 * (h % 2), 64 * (h % 2) + 64)
                            bank = m.ps[:n, 4 * x + (1, 2)[h % 2], :]
                            kT = featT[half, x, 2 + h // 2, :n]
                            pe.matmul(bank[:, (h // 2) * P:(h // 2) * P + n], kT, featT[half, x, 4 + h // 2, :n], start=True, stop=True)
                            last = pe.matmul(bank[:, (2 + h // 2) * P:(2 + h // 2) * P + n], kT, featT[half, x, h // 2, :n], start=True, stop=True)
                        last.then_inc(gram, 1)
                    for s in range(levels(pair[0])):
                        for k in pair:
                            n, x = ROWS[k], k % 2
                            pe.wait_ge(b_ready, order(k, s))
                            if s:
                                pe.wait_ge(t_ready, order(k, s - 1))
                            else:
                                pe.wait_ge(a_ready, 4 * (k + 1))
                                pe.wait_ge(decay_ready, 4 * (k + 1))
                            for h in range(H):
                                last = pe.matmul(m.ps[:n, 4 * x, h * P:h * P + n], B[:n, x, h, :n],
                                                 T[:n, x, h, :n] if s else m.ident[:n, :n], start=True, stop=True)
                            last.then_inc(bt, 1)
                        if s == 0:
                            continue
                        for k in pair:
                            n, x = ROWS[k], k % 2
                            pe.wait_ge(u_ready, order1(k, s))
                            for h in range(H):
                                if s < levels(k) - 1:
                                    pe.matmul(m.ps[:n, 4 * x + 1, h * P:h * P + n], TT[:n, x, h, :n], U[:n, x, h, :n], start=True, stop=True)
                                last = pe.matmul(m.ps[:n, 4 * x + 3, h * P:h * P + n], U[:n, x, h, :n], TT[:n, x, h, :n], start=True, stop=True)
                            last.then_inc(tut, 1)
                    for k in pair:
                        n, x = ROWS[k], k % 2
                        pe.wait_ge(t_ready, order(k, levels(k) - 1))
                        pe.wait_ge(scaled, 4 * k + 4)
                        for h in range(H):
                            last = pe.matmul(m.ps[:, 4 * x, h * P:h * P + n], kbg[:n, x, (h // 2) * P:(h // 2) * P + P],
                                             TT[:n, x, h, :n], start=True, stop=True)
                        last.then_inc(wprod, 1)
                        if k == TS:
                            n = NB * NQ
                            vbank, obank = m.ps[:n, 1, :], m.ps[:n, 2, :]
                            pe.wait_ge(masked, 1)
                            pe.wait_ge(s_in, 16)
                            for h in range(H):
                                pe.matmul(vbank[:, h * HD:(h + 1) * HD], TT[:n, x, h, :n], vb[:n, x, h * HD:(h + 1) * HD],
                                          start=h == 0, stop=False, skip_group_check=True)
                            for b in range(NB):
                                for c in range(2):
                                    last = pe.matmul(vbank[:, c * P:(c + 1) * P], wTm[:, c, b, :], Ss[:, b, c, :],
                                                     start=False, stop=b == NB - 1, skip_group_check=True)
                            last.then_inc(vprod, 1)
                            for b in range(NB):
                                for c in range(2):
                                    pe.matmul(obank[:, c * P:(c + 1) * P], qgm[:, c, b, :], Ss[:, b, c, :],
                                              start=b + c == 0, stop=False, skip_group_check=True)
                            pe.wait_ge(v_ready, NT)
                            pe.wait_ge(v_ready, TS)
                            pe.wait_ge(o_out, TS)
                            pe.wait_ge(s_ready, TS)
                            for b in range(NB):
                                for c in range(2):
                                    last = pe.matmul(m.ps[:, 4 + b // 2, (b % 2) * 256 + c * P:(b % 2) * 256 + (c + 1) * P],
                                                     kdecm(b)[:, c * P:(c + 1) * P], vnew[:n, c * P:(c + 1) * P],
                                                     start=True, stop=True)
                            last.then_inc(sprod, 1)
                            for h in range(H):
                                last = pe.matmul(obank[:, h * HD:(h + 1) * HD], aqkT[:n, x, h, :n], vnew[:n, h * HD:(h + 1) * HD],
                                                 start=False, stop=h == 3, skip_group_check=True)
                            last.then_inc(oprod, 1)
                            continue
                        pe.wait_ge(w_ready, 2 * (k + 1))
                        if k:
                            pe.wait_ge(s_ready, k)
                        else:
                            pe.wait_ge(s_zero, 1)
                        vbank, obank, sbank = (m.ps[:, 4 * x + c, :] for c in (1, 2, 3))
                        for h in range(H):
                            pe.matmul(vbank[:, h * HD:(h + 1) * HD], TT[:, x, h, :], vb[:, x, h * HD:(h + 1) * HD],
                                      start=h == 0, stop=False, skip_group_check=True)
                        for c in range(2):
                            last = pe.matmul(vbank[:, c * P:(c + 1) * P], wT[:, x, c, :], S[:, c, :],
                                             start=False, stop=c == 1, skip_group_check=True)
                        last.then_inc(vprod, 1)
                        for c in range(2):
                            pe.matmul(obank[:, c * P:(c + 1) * P], featT[:, x, 6 + c, :], S[:, c, :],
                                      start=c == 0, stop=False, skip_group_check=True)
                        pe.wait_ge(v_ready, k + 1)
                        for c in range(2):
                            last = pe.matmul(sbank[:, c * P:(c + 1) * P], kdec[:, x, c * P:(c + 1) * P],
                                             vnew[:, c * P:(c + 1) * P], start=True, stop=True)
                        last.then_inc(sprod, 1)
                        for h in range(H):
                            last = pe.matmul(obank[:, h * HD:(h + 1) * HD], aqkT[:, x, h, :], vnew[:, h * HD:(h + 1) * HD],
                                             start=False, stop=h == 3, skip_group_check=True)
                        last.then_inc(oprod, 1)
                pe.wait_ge(fin, 1)
                for k in range(NT):
                    if k >= 2:
                        pe.wait_ge(fout, k - 1)
                    for c in range(2):
                        last = pe.transpose(m.ps[:, k % 2, c * P:c * P + ROWS[k]], o_all[:ROWS[k], k, c * P:(c + 1) * P],
                                            m.ident[:ROWS[k], :ROWS[k]])
                    last.then_inc(fturn, 1)



def key_prep(nc, m):
    with ExitStack() as ctx:
        sb = lambda n, s: ctx.enter_context(nc.sbuf_tensor(f"prep_{n}", s, F32))
        sem = lambda n: m.sem(f"prep_{n}")
        loaded, turned, pooled, out, gates = sem("loaded"), sem("turned"), sem("pooled"), sem("out"), sem("gates")
        jobs = [(KSEL, m.kselT, (0, 1, 2, 3)), (KSEL, m.kselT, (4, 5, 6, 7)),
                (KWIN, m.kwinT, (0, 1, 2, 3)), (KWIN, m.kwinT, (4, 5, 6, 7))]
        with nc.Block() as block:
            @block.sync
            def _(sp):
                sp.dma_start(m.wck[:], m.a["wck"]).then_inc(loaded, 16)
                sp.dma_start(m.wcv[:], m.a["wcv"]).then_inc(loaded, 16)
                sp.wait_ge(loaded, 32)

            @block.tensor
            def _(pe):
                for j, (col, _, tiles) in enumerate(jobs):
                    for c, t in enumerate(tiles):
                        last = pe.transpose(m.ps[:, j, c * P:(c + 1) * P], m.kv[:, t, col:col + P], m.ident[:])
                    last.then_inc(turned, 1)
                for c, col in enumerate((KSEL, KWIN)):
                    last = pe.transpose(m.ps[:, 4, c * P:c * P + 64], m.kv[:64, TS, col:col + P], m.ident[:64, :64])
                last.then_inc(turned, 1)
                pe.wait_ge(loaded, 32)
                for t in range(TS):
                    pe.matmul(m.ps[:, 5, 4 * t:4 * t + 4], m.kv[:, t, KCMP:KCMP + P], m.wck[:], start=True, stop=True)
                for g in range(G):
                    for t in range(TS):
                        last = pe.matmul(m.ps[:16, 6, g * HD:(g + 1) * HD], m.wcv[:, g, 30 - 2 * t:46 - 2 * t],
                                         m.kv[:, t, VCMP + g * HD:VCMP + (g + 1) * HD], start=t == 0, stop=t == TS - 1)
                last.then_inc(pooled, 1)

            @block.scalar
            def _(act):
                act.activation(m.small[:, :, 0:24], m.small[:, :, 0:24], ACT.Sigmoid).then_inc(gates, 1)
                for j, (_, dst, tiles) in enumerate(jobs):
                    act.wait_ge(turned, j + 1)
                    act.activation(dst[:, tiles[0] * P:tiles[0] * P + 512], m.ps[:, j, :], ACT.Copy).then_inc(out, 1)

            @block.vector
            def _(dve):
                dve.wait_ge(turned, 5)
                for c, dst in enumerate((m.kselT, m.kwinT)):
                    dve.tensor_copy(dst[:, SEQ:TOK], m.ps[:, 4, c * P:c * P + 64]).then_inc(out, 1)
                dve.wait_ge(pooled, 1)
                for g in range(G):
                    half = slice(64 * g, 64 * g + 64)
                    src = m.ps[half, 5, 0:32].rearrange("p (t g b) -> p t g b", t=TS, g=G)[:, :, g, :]
                    dve.tensor_copy(m.kcT[half, :].rearrange("p (t b) -> p t b", t=TS), src).then_inc(out, 1)
                dve.tensor_copy(m.vc[:], m.ps[:16, 6, 0:P]).then_inc(out, 1)


def prompt_attention(nc, m):
    with ExitStack() as ctx:
        sb = lambda n, s: ctx.enter_context(nc.sbuf_tensor(f"pa_{n}", s, F32))
        sem = lambda n: m.sem(f"pa_{n}")
        SLOTS = 8
        WIN_AT, CMP_AT, WIDTH = SEQ, SEQ + 640, SEQ + 640 + 16
        probs = sb("probs", [P, SLOTS, WIDTH])
        dsel, dwin, dcmp = sb("dsel", [P, 1024]), sb("dwin", [P, 640]), sb("dcmp", [P, 128])
        mx, nm, rs, fac = (sb(n, [P, SLOTS, 3]) for n in ("mx", "nm", "rs", "fac"))
        PTN = 4
        PT = sb("PT", [P, PTN, 512])
        (loaded, score_ready, score_out, nm_ready, exp_done, scaled, turned, pt_ready, pv_step, o_out, vec) = (
            sem(n) for n in ("loaded", "score_ready", "score_out", "nm_ready", "exp_done", "scaled", "turned",
                             "pt_ready", "pv_step", "o_out", "vec"))
        units = [(i, g) for i in range(TS) for g in range(G)]
        RING = 4

        def window(i):
            f = max(0, i - WINDOW // P)
            return f, i - f + 1

        def pieces(i):
            out = [(o, min(512, (i + 1) * P - o), m.kselT, o, dsel[:, 1024 - (i + 1) * P + o:])
                   for o in range(0, (i + 1) * P, 512)]
            f, nw = window(i)
            out += [(WIN_AT + o, min(512, nw * P - o), m.kwinT, f * P + o, dwin[:, (f - i) * P + 512 + o:])
                    for o in range(0, nw * P, 512)]
            return out + [(CMP_AT, 16, m.kcT, 0, dcmp[:, 16 * i:])]

        def branches(i):
            return [(0, (i + 1) * P), (WIN_AT, window(i)[1] * P), (CMP_AT, 16)]

        def steps(n):
            i, g = units[n]
            f, nw = window(i)
            v = slice(g * HD, (g + 1) * HD)
            out = [(P * t, P, m.kv[:, t, VSEL:VSEL + P][:, v]) for t in range(i + 1)]
            out += [(WIN_AT + P * t, P, m.kv[:, f + t, VWIN:VWIN + P][:, v]) for t in range(nw)]
            return out + [(CMP_AT, 16, m.vc[:, v])]

        first_step = [0]
        for n in range(len(units)):
            first_step.append(first_step[-1] + len(steps(n)))

        def part(n, r):
            k = len(steps(n))
            return range(k * r // R, k * (r + 1) // R)

        with nc.Block() as block:
            @block.sync
            def _(sp):
                for name, dst in (("dist_sel", dsel), ("dist_win", dwin), ("dist_cmp", dcmp)):
                    at, w = CONST_AT[name]
                    sp.dma_start(dst[:], m.const[:, at:at + w]).then_inc(loaded, 16)
                sp.wait_ge(loaded, 48)

            @block.tensor
            def _(pe):
                count = [0]

                def scores(n, r):
                    i, g = units[n]
                    half = slice(64 * g, 64 * g + 64)
                    for _, w, keys, k0, _ in pieces(i):
                        c = count[0]
                        if c >= RING:
                            pe.wait_ge(score_out, c - RING + 1)
                        pe.matmul(m.ps[:, c % RING, :w], m.qT[half, r, i * P:(i + 1) * P], keys[half, k0:k0 + w],
                                  start=True, stop=True).then_inc(score_ready, 1)
                        count[0] += 1

                def multiply(n, s):
                    st = first_step[n] + s
                    _, k, values = steps(n)[s]
                    half = slice(64 * units[n][1], 64 * units[n][1] + 64)
                    if s == 0 and n >= 2:
                        pe.wait_ge(o_out, n - 1)
                    pe.wait_ge(pt_ready, st + 1)
                    pe.matmul(m.ps[half, 6 + n % 2, :], values, PT[:k, st % PTN, :], start=s == 0,
                              stop=s == len(steps(n)) - 1).then_inc(pv_step, 1)

                def turn(n, r):
                    if r == 0:
                        pe.wait_ge(scaled, R * (n + 1))
                    for s in part(n, r):
                        col, k, _ = steps(n)[s]
                        st = first_step[n] + s
                        if st >= 2:
                            pe.wait_ge(pt_ready, st - 1)
                        for h in range(R):
                            last = pe.transpose(m.ps[:k, 4 + st % 2, h * P:(h + 1) * P],
                                                probs[:, (R * n + h) % SLOTS, col:col + k], m.ident[:])
                        last.then_inc(turned, 1)
                        if s:
                            multiply(n, s - 1)
                    if r == R - 1:
                        multiply(n, len(steps(n)) - 1)

                pe.wait_ge(loaded, 48)
                for n in range(len(units) + 1):
                    for r in range(R):
                        if n < len(units):
                            scores(n, r)
                        if n:
                            turn(n - 1, r)

            @block.vector
            def _(dve):
                link = Link(dve, vec)
                count = [0]
                dve.wait_ge(loaded, 48)

                def rows(e):
                    n, r = e // R, e % R
                    i, g = units[n]
                    x = e % SLOTS
                    if n >= 2 and r == 0:
                        dve.wait_ge(turned, first_step[n - 1])
                    for col, w, _, _, table in pieces(i):
                        dve.wait_ge(score_ready, count[0] + 1)
                        last = dve.scalar_tensor_tensor(probs[:, x, col:col + w], table[:, :w], 2.0 ** -(4 * g + r + 1),
                                                        m.ps[:, count[0] % RING, :w], ALU.mult, ALU.add)
                        last.then_inc(score_out, 1)
                        count[0] += 1
                    dve.wait_ge(score_out, count[0])
                    for b, (o, w) in enumerate(branches(i)):
                        last = dve.tensor_reduce(mx[:, x, b:b + 1], probs[:, x, o:o + w], AX.X, ALU.max)
                    link(last)
                    dve.tensor_scalar(nm[:, x, :], mx[:, x, :], MFLOOR, -1.0, ALU.max, ALU.mult).then_inc(nm_ready, 1)

                def scale(e):
                    n, r = e // R, e % R
                    i, g = units[n]
                    x = e % SLOTS
                    dve.wait_ge(exp_done, e + 1)
                    link(dve.tensor_scalar(rs[:, x, :], rs[:, x, :], 1e-30, None, ALU.max))
                    link(dve.reciprocal(fac[:, x, :], rs[:, x, :]))
                    h = 4 * g + r
                    link(dve.tensor_tensor(fac[:, x, 0:2], fac[:, x, 0:2], m.small[:, i, 3 * h + 1:3 * h + 3], ALU.mult))
                    link(dve.tensor_tensor(fac[:, x, 2:3], fac[:, x, 2:3], m.small[:, i, 3 * h:3 * h + 1], ALU.mult))
                    for b, (o, w) in enumerate(branches(i)):
                        last = dve.tensor_scalar(probs[:, x, o:o + w], probs[:, x, o:o + w], fac[:, x, b:b + 1], None, ALU.mult)
                    last.then_inc(scaled, 1)

                E = R * len(units)
                for e in range(E + 1):
                    if e < E:
                        rows(e)
                    if e:
                        scale(e - 1)

            @block.scalar
            def _(act):
                def exps(e):
                    i, _ = units[e // R]
                    x = e % SLOTS
                    act.wait_ge(nm_ready, e + 1)
                    for b, (o, w) in enumerate(branches(i)):
                        last = act.activation(probs[:, x, o:o + w], probs[:, x, o:o + w], ACT.Exp, bias=nm[:, x, b:b + 1],
                                              accum_out=rs[:, x, b:b + 1])
                    last.then_inc(exp_done, 1)

                def copies(n, r):
                    for s in part(n, r):
                        st = first_step[n] + s
                        k = steps(n)[s][1]
                        act.wait_ge(turned, st + 1)
                        if st >= PTN:
                            act.wait_ge(pv_step, st - PTN + 1)
                        act.activation(PT[:k, st % PTN, :], m.ps[:k, 4 + st % 2, :], ACT.Copy).then_inc(pt_ready, 1)
                    if r == R - 1:
                        i, g = units[n]
                        half = slice(64 * g, 64 * g + 64)
                        act.wait_ge(pv_step, first_step[n + 1])
                        act.activation(m.mixT[half, 0:4, i * P:(i + 1) * P],
                                       m.ps[half, 6 + n % 2, :].rearrange("p (h n) -> p h n", h=R), ACT.Copy).then_inc(o_out, 1)

                for n in range(len(units) + 1):
                    for r in range(R):
                        if n:
                            copies(n - 1, r)
                        if n < len(units):
                            exps(R * n + r)


def sample_attention(nc, m):
    with ExitStack() as ctx:
        sb = lambda n, s: ctx.enter_context(nc.sbuf_tensor(f"sa_{n}", s, F32))
        sem = lambda n: m.sem(f"sa_{n}")
        ck = sb("ck", [P, NB * PAGES, 512])
        cw = sb("cw", [P, NB * PAGES, 256])
        kT = sb("kT", [P, 2, NB * PAGES * P])
        pages = ctx.enter_context(nc.sbuf_tensor("sa_pages", [1, NB * PAGES], I32))
        dist, dcmp, slope = sb("dist", [P, 2, 320]), sb("dcmp", [P, 2, 32]), sb("slope", [P, 2])
        gsel = sb("gsel", [P, 2, R, P])
        qS = sb("qS", [P, NB, R, NQ])
        kcT, vc = sb("kcT", [P, 32]), sb("vc", [32, P])
        gates = sb("gates", [P, 2, 6])
        NEW = 64
        WIDTH = 2 * (PAST + NEW) + 32
        probs = sb("probs", [P, WIDTH])
        mx, nm, rs, fac = (sb(n, [P, 4, 3]) for n in ("mx", "nm", "rs", "fac"))
        PT = sb("PT", [P, 7, P])
        BR = [(0, PAST + NEW), (PAST + NEW, PAST + NEW), (2 * (PAST + NEW), 32)]
        items = [(g, h) for h in range(2) for g in range(G)]
        (consts, pg, cached, turned, t_out, pooled, pool_out, gate_prod, gate_out, sc, sc_out, nm_ready, exp_done,
         scaled, p_turned, p_out, pv, o_out, vec, q_out) = (sem(n) for n in (
             "consts", "pg", "cached", "turned", "t_out", "pooled", "pool_out", "gate_prod", "gate_out", "sc", "sc_out",
             "nm_ready", "exp_done", "scaled", "p_turned", "p_out", "pv", "o_out", "vec", "q_out"))
        jobs = [(which, j) for which in range(2) for j in range(4)]
        with nc.Block() as block:
            @block.sync
            def _(sp):
                sp.dma_start(pages[:], m.a["page_table"]).then_inc(pg, 16)
                sp.dma_start(cw[:], m.cache_win.rearrange("b (a p) n -> p (b a) n", p=P)).then_inc(cached, 16)
                for name, dst in (("sdist", dist[:].rearrange("p h n -> p (h n)")), ("sdist_cmp", dcmp[:].rearrange("p h n -> p (h n)")),
                                  ("sslope", slope[:]), ("gate_sel", gsel[:].rearrange("p h r n -> p (h r n)"))):
                    at, w = CONST_AT[name]
                    sp.dma_start(dst, m.const[:, at:at + w]).then_inc(consts, 16)
                sp.wait_ge(pg, 16)
                for j in range(NB * PAGES):
                    page = sp.value_load(pages[0:1, j:j + 1], min_val=0, max_val=m.a["cache_nsa"].shape[0] - 1)
                    sp.dma_start(ck[:, j, :], m.a["cache_nsa"][bass.DynSlice(page, 1)].rearrange("a p n -> p (a n)")
                                 ).then_inc(cached, 16)
                sp.wait_ge(cached, 16 * 17)

            @block.tensor
            def _(pe):
                pe.wait_ge(cached, 16 * 17)
                pe.wait_ge(consts, 64)
                for j, (which, a) in enumerate(jobs):
                    if j >= 4:
                        pe.wait_ge(t_out, j - 3)
                    for c in range(4):
                        src = ck[:, 4 * a + c, 256:384] if which == 0 else cw[:, 4 * a + c, 0:128]
                        last = pe.transpose(m.ps[:, j % 4, c * P:(c + 1) * P], src, m.ident[:])
                    last.then_inc(turned, 1)
                for j in range(16):
                    pe.matmul(m.ps[:, 4, 4 * j:4 * j + 4], ck[:, j, 0:128], m.wck[:], start=True, stop=True)
                for g in range(G):
                    for j in range(16):
                        last = pe.matmul(m.ps[:32, 5, g * HD:(g + 1) * HD], m.wcv[:, g, 30 - 2 * j:62 - 2 * j],
                                         ck[:, j, 128 + g * HD:128 + (g + 1) * HD], start=j == 0, stop=j == 15)
                last.then_inc(pooled, 1)
                gt = m.small[:64, TS, 0:24].rearrange("p (g r c) -> p g r c", g=G, r=R)
                for h in range(2):
                    for r in range(R):
                        last = pe.matmul(m.ps[:, 6 + h, 0:6], gsel[:64, h, r, :], gt[:, :, r, :], start=r == 0, stop=r == R - 1)
                last.then_inc(gate_prod, 1)
                pe.wait_ge(t_out, 8)
                pe.wait_ge(q_out, R)
                pe.wait_ge(pool_out, 3)
                pe.wait_ge(gate_out, 1)
                for it, (g, h) in enumerate(items):
                    half = slice(64 * g, 64 * g + 64)
                    if it:
                        pe.wait_ge(sc_out, it)
                    for b in range(4):
                        rows = slice(32 * b, 32 * b + 32)
                        seq = 4 * h + b
                        q = qS[half, seq].rearrange("p r q -> p (r q)")
                        pe.matmul(m.ps[rows, 0, 0:PAST], q, kT[half, 0, seq * PAST:(seq + 1) * PAST], start=True, stop=True)
                        pe.matmul(m.ps[rows, 0, PAST:PAST + NEW], q, m.kselT[half, SEQ:TOK], start=True, stop=True)
                        pe.matmul(m.ps[rows, 1, 0:PAST], q, kT[half, 1, seq * PAST:(seq + 1) * PAST], start=True, stop=True)
                        pe.matmul(m.ps[rows, 1, PAST:PAST + NEW], q, m.kwinT[half, SEQ:TOK], start=True, stop=True)
                        last = pe.matmul(m.ps[rows, 2, 0:32], q, kcT[half, :], start=True, stop=True)
                    last.then_inc(sc, 1)
                    pe.wait_ge(scaled, it + 1)
                    if it:
                        pe.wait_ge(p_out, 3 * it)
                    for c, o in enumerate((0, P, 320, 320 + P)):
                        pe.transpose(m.ps[:, 6, c * P:(c + 1) * P], probs[:, o:o + P], m.ident[:])
                    for c, o in enumerate((PAST, 320 + PAST)):
                        pe.transpose(m.ps[:64, 7, c * P:(c + 1) * P], probs[:, o:o + NEW], m.ident[:])
                    pe.transpose(m.ps[:32, 7, 2 * P:3 * P], probs[:, 640:672], m.ident[:]).then_inc(p_turned, 1)
                    pe.wait_ge(p_out, 3 * (it + 1))
                    if it >= 2:
                        pe.wait_ge(o_out, it - 1)
                    acc = m.ps[half, 3 + it % 2, 0:P]
                    v = lambda t: t[:, g * HD:(g + 1) * HD]
                    args = dict(stop=False, skip_group_check=True)
                    pe.matmul(acc, v(m.kv[:64, TS, VSEL:VSEL + P]), PT[:64, 4, :], start=True, **args)
                    pe.matmul(acc, v(m.kv[:64, TS, VWIN:VWIN + P]), PT[:64, 5, :], start=False, **args)
                    pe.matmul(acc, v(vc[:, :]), PT[:32, 6, :], start=False, **args)
                    for b in range(4):
                        rows = slice(32 * b, 32 * b + 32)
                        for a in range(PAGES):
                            j = (4 * h + b) * PAGES + a
                            pe.matmul(acc[:, rows], v(ck[:, j, 384:512]), PT[:, a, rows], start=False, **args)
                            last = pe.matmul(acc[:, rows], v(cw[:, j, 128:256]), PT[:, 2 + a, rows], start=False,
                                             stop=b == 3 and a == 1, skip_group_check=True)
                    last.then_inc(pv, 1)

            @block.scalar
            def _(act):
                for r in range(R):
                    act.activation(qS[:, :, r, :], m.qT[:, r, SEQ:TOK].rearrange("p (b q) -> p b q", b=NB),
                                   ACT.Copy).then_inc(q_out, 1)
                for j, (which, a) in enumerate(jobs):
                    act.wait_ge(turned, j + 1)
                    act.activation(kT[:, which, 512 * a:512 * a + 512], m.ps[:, j % 4, :], ACT.Copy).then_inc(t_out, 1)
                for it, (g, h) in enumerate(items):
                    act.wait_ge(nm_ready, it + 1)
                    for b, (o, w) in enumerate(BR):
                        last = act.activation(probs[:, o:o + w], probs[:, o:o + w], ACT.Exp, bias=nm[:, it, b:b + 1],
                                              accum_out=rs[:, it, b:b + 1])
                    last.then_inc(exp_done, 1)
                    act.wait_ge(p_turned, it + 1)
                    if it:
                        act.wait_ge(pv, it)
                    act.activation(PT[:, 0:4, :], m.ps[:, 6, :].rearrange("p (c n) -> p c n", c=4), ACT.Copy).then_inc(p_out, 1)
                    act.activation(PT[:64, 4:6, :], m.ps[:64, 7, 0:256].rearrange("p (c n) -> p c n", c=2), ACT.Copy).then_inc(p_out, 1)
                    act.activation(PT[:32, 6, :], m.ps[:32, 7, 256:384], ACT.Copy).then_inc(p_out, 1)
                    act.wait_ge(pv, it + 1)
                    half = slice(64 * g, 64 * g + 64)
                    dst = m.mixT[half, 0:4, SEQ + 32 * h:SEQ + 32 * h + 32].rearrange("p r (b q) -> p r b q", b=4)
                    src = m.ps[half, 3 + it % 2, 0:P].rearrange("p (b r q) -> p r b q", b=4, r=R)
                    for r in range(R):
                        last = act.activation(dst[:, r], src[:, r], ACT.Copy)
                    last.then_inc(o_out, 1)

            @block.vector
            def _(dve):
                link = Link(dve, vec)
                dve.wait_ge(pooled, 1)
                for g in range(G):
                    half = slice(64 * g, 64 * g + 64)
                    src = m.ps[half, 4, 0:64].rearrange("p (j g b) -> p j g b", j=16, g=G)[:, :, g, :]
                    dve.tensor_copy(kcT[half, :].rearrange("p (j b) -> p j b", j=16), src).then_inc(pool_out, 1)
                dve.tensor_copy(vc[:], m.ps[:32, 5, 0:P]).then_inc(pool_out, 1)
                dve.wait_ge(gate_prod, 1)
                dve.tensor_copy(gates[:], m.ps[:, 6:8, 0:6]).then_inc(gate_out, 1)
                dve.wait_ge(gate_out, 1)
                dve.wait_ge(consts, 64)
                for it, (g, h) in enumerate(items):
                    dve.wait_ge(sc, it + 1)
                    if it:
                        dve.wait_ge(p_turned, it)
                    for b, (o, w) in enumerate(BR):
                        table = dist[:, h, :] if b < 2 else dcmp[:, h, :]
                        last = dve.scalar_tensor_tensor(probs[:, o:o + w], table, slope[:, g:g + 1], m.ps[:, b, 0:w],
                                                        ALU.mult, ALU.add)
                    last.then_inc(sc_out, 1)
                    dve.wait_ge(sc_out, it + 1)
                    for b, (o, w) in enumerate(BR):
                        last = dve.tensor_reduce(mx[:, it, b:b + 1], probs[:, o:o + w], AX.X, ALU.max)
                    link(last)
                    dve.tensor_scalar(nm[:, it, :], mx[:, it, :], MFLOOR, -1.0, ALU.max, ALU.mult).then_inc(nm_ready, 1)
                    dve.wait_ge(exp_done, it + 1)
                    link(dve.tensor_scalar(rs[:, it, :], rs[:, it, :], 1e-30, None, ALU.max))
                    link(dve.reciprocal(fac[:, it, :], rs[:, it, :]))
                    for b, c in enumerate((1, 2, 0)):
                        last = dve.tensor_tensor(fac[:, it, b:b + 1], fac[:, it, b:b + 1], gates[:, h, 3 * g + c:3 * g + c + 1], ALU.mult)
                    link(last)
                    for b, (o, w) in enumerate(BR):
                        last = dve.tensor_scalar(probs[:, o:o + w], probs[:, o:o + w], fac[:, it, b:b + 1], None, ALU.mult)
                    last.then_inc(scaled, 1)


def attention(nc, m):
    with ExitStack() as held:
        hold = lambda n, s: held.enter_context(nc.sbuf_tensor(n, s, F32))
        m.kselT, m.kwinT = hold("kselT", [P, TOK]), hold("kwinT", [P, TOK])
        m.kcT, m.vc = hold("kcT", [P, 16]), hold("vc", [16, P])
        m.wck, m.wcv = hold("wck", [P, 4]), hold("wcv", [P, 2, 62])
        key_prep(nc, m)
        prompt_attention(nc, m)
        sample_attention(nc, m)



def output_projection(nc, m):
    with ExitStack() as ctx:
        sb = lambda n, s: ctx.enter_context(nc.sbuf_tensor(f"out_{n}_sb", s, F32))
        sem = lambda n: m.sem(f"out_{n}")
        W, xs = sb("w", [P, KT, D]), sb("x", [P, 3, D])
        w_loaded, product, added = sem("w_loaded"), sem("product"), sem("added")
        x_loaded = [sem(f"x_loaded{i}") for i in range(3)]
        with nc.Block() as block:
            @block.sync
            def _(sp):
                sp.dma_start(W[:].rearrange("p k n -> p (k n)"), m.a["w_out"]).then_inc(w_loaded, 16)
                for t in range(TILES):
                    if t >= 3:
                        sp.wait_ge(added, 2 * (t - 2))
                    src = m.x_prompt[t * P:(t + 1) * P, :] if t < TS else m.x_sample
                    sp.dma_start(xs[:ROWS[t], t % 3, :], src).then_inc(x_loaded[t % 3], 16)

            @block.tensor
            def _(pe):
                pe.wait_ge(w_loaded, 16)
                for u in range(2 * TILES):
                    t, h = u // 2, u % 2
                    if u >= 8:
                        pe.wait_ge(added, u - 7)
                    for k in range(KT):
                        last = pe.matmul(m.ps[:ROWS[t], u % 8, :], m.mixT[:, k, t * P:t * P + ROWS[t]],
                                         W[:, k, 512 * h:512 * h + 512], start=k == 0, stop=k == KT - 1)
                    last.then_inc(product, 1)

            @block.vector
            def _(dve):
                for u in range(2 * TILES):
                    t, h = u // 2, u % 2
                    n = ROWS[t]
                    if h == 0:
                        dve.wait_ge(x_loaded[t % 3], 16 * (t // 3 + 1))
                    dve.wait_ge(product, u + 1)
                    dve.tensor_tensor(m.x2[:n, t, 512 * h:512 * h + 512], xs[:n, t % 3, 512 * h:512 * h + 512],
                                      m.ps[:n, u % 8, :], ALU.add).then_inc(added, 1)


def mlp_products(nc, m):
    with ExitStack() as ctx:
        sb = lambda n, s, dt=F32R: ctx.enter_context(nc.sbuf_tensor(f"mlp_{n}", s, dt))
        sem = lambda n: m.sem(f"mlp_{n}")
        NG, FT = FF // FG, FG // P
        KINDS = ("up", "down")
        WN = KT * FG
        assert WN == FT * D
        raw = {k: sb("raw_" + k, [P, WN], F32) for k in KINDS}
        hi = {k: sb("hi_" + k, [P, WN]) for k in KINDS}
        lo = {k: sb("lo_" + k, [P, WN]) for k in KINDS}
        RT = 2
        rect = sb("rect", [P, RT, 512], F32)
        hid = [sb(n, [P, 2, FT, PADT]) for n in ("hid_hi", "hid_lo")]
        loaded = {k: sem(k + "_loaded") for k in KINDS}
        hi_made = {k: sem(k + "_hi_made") for k in KINDS}
        lo_made = {k: sem(k + "_lo_made") for k in KINDS}
        (product, rectified, squared, hid_hi, hid_lo, added) = (
            sem(n) for n in ("product", "rectified", "squared", "hid_hi", "hid_lo", "added"))
        padded = sem("padded")
        UPS, DOWNS = 3 * FT, 2 * TILES
        phases = [("up", 0)]
        for g in range(NG):
            phases += [("up", g + 1)] * (g + 1 < NG) + [("down", g)]
        units = []
        for kind, g in phases:
            units += [(kind, g, a, b) for a in range(FT if kind == "up" else TILES) for b in range(3 if kind == "up" else 2)]
        rank, seen = [], {"up": 0, "down": 0}
        for kind, *_ in units:
            seen[kind] += 1
            rank.append(seen[kind])
        ends = {}
        for u, (kind, g, _, _) in enumerate(units):
            ends[kind, g] = u + 1
        w_of = {"up": lambda t: t[:].rearrange("p (k n) -> p k n", k=KT),
                "down": lambda t: t[:].rearrange("p (f n) -> p f n", f=FT)}
        with nc.Block() as block:
            @block.sync
            def _(sp):
                for kind, g in phases:
                    if g:
                        sp.wait_ge(lo_made[kind], g)
                    src = m.a["w_" + kind][g].rearrange("p a n -> p (a n)")
                    sp.dma_start(raw[kind][:], src).then_inc(loaded[kind], 16)

            @block.scalar
            def _(act):
                def round_weights(kind, g):
                    act.wait_ge(loaded[kind], 16 * (g + 1))
                    if g:
                        act.wait_ge(product, ends[kind, g - 1])
                    act.activation(hi[kind][:], raw[kind][:], ACT.Copy).then_inc(hi_made[kind], 1)

                def round_hidden(u):
                    _, g, a, b = units[u]
                    o, w = GROUPS_N[b]
                    act.wait_ge(squared, rank[u])
                    act.activation(hid[0][:, g % 2, a, o:o + w], rect[:, (rank[u] - 1) % RT, :w], ACT.Copy).then_inc(hid_hi, 1)

                round_weights("up", 0)
                waiting = None
                for u, (kind, g, a, b) in enumerate(units):
                    if kind == "down":
                        if waiting is not None:
                            round_hidden(waiting)
                            waiting = None
                        if (a, b) == (0, 0) and g + 2 < NG:
                            round_weights("up", g + 2)
                        if (a, b) == (0, 0) and g == NG - 1:
                            round_weights("down", g)
                        continue
                    o, w = GROUPS_N[b]
                    if (a, b) == (0, 0):
                        if g:
                            round_weights("down", g - 1)
                        if g >= 2:
                            act.wait_ge(product, ends["down", g - 2])
                    act.wait_ge(product, u + 1)
                    if rank[u] > RT:
                        act.wait_ge(hid_lo, rank[u] - RT)
                    act.activation(rect[:, (rank[u] - 1) % RT, :w], m.ps[:, u % 8, :w], ACT.Relu).then_inc(rectified, 1)
                    if waiting is not None:
                        round_hidden(waiting)
                    waiting = u
                    if g == 0 and (a, b) == (FT - 1, 2):
                        round_hidden(waiting)
                        waiting = None
                        round_weights("up", 1)

            @block.gpsimd
            def _(pool):
                for part in hid:
                    pool.memset(part[:, :, :, TOK:].bitcast(F32), 0.0).then_inc(padded, 1)
                for u, (kind, g, a, b) in enumerate(units):
                    if kind == "up":
                        w = GROUPS_N[b][1]
                        pool.wait_ge(rectified, rank[u])
                        part = rect[:, (rank[u] - 1) % RT, :w]
                        pool.tensor_tensor(part, part, part, ALU.mult).then_inc(squared, 1)

            @block.vector
            def _(dve):
                def rest_of_weights(kind, g):
                    dve.wait_ge(hi_made[kind], g + 1)
                    dve.tensor_tensor(lo[kind][:], raw[kind][:], hi[kind][:], ALU.subtract).then_inc(lo_made[kind], 1)

                rest_of_weights("up", 0)
                for u, (kind, g, a, b) in enumerate(units):
                    if kind == "up":
                        o, w = GROUPS_N[b]
                        if (a, b) == (0, 0) and g:
                            rest_of_weights("down", g - 1)
                        dve.wait_ge(hid_hi, rank[u])
                        dve.tensor_tensor(hid[1][:, g % 2, a, o:o + w], rect[:, (rank[u] - 1) % RT, :w],
                                          hid[0][:, g % 2, a, o:o + w], ALU.subtract).then_inc(hid_lo, 1)
                        if g == 0 and (a, b) == (FT - 1, 2):
                            rest_of_weights("up", 1)
                        continue
                    if (a, b) == (0, 0) and g + 2 < NG:
                        rest_of_weights("up", g + 2)
                    if (a, b) == (0, 0) and g == NG - 1:
                        rest_of_weights("down", g)
                    n = ROWS[a]
                    dve.wait_ge(product, u + 1)
                    if g:
                        dve.wait_ge(added, DOWNS * (g - 1) + 2 * a + b + 1)
                    part = m.x2[:n, a, 512 * b:512 * b + 512]
                    dve.tensor_tensor(part, part, m.ps[:n, u % 8, :], ALU.add).then_inc(added, 1)

            @block.tensor
            def _(pe):
                for u, (kind, g, a, b) in enumerate(units):
                    x = g % 2
                    if (a, b) == (0, 0):
                        pe.wait_ge(lo_made[kind], g + 1)
                        if kind == "down":
                            pe.wait_ge(hid_lo, UPS * (g + 1))
                            pe.wait_ge(padded, 2)
                    if u >= 8:
                        pe.wait_ge(rectified if units[u - 8][0] == "up" else added, rank[u - 8])
                    w2 = [w_of[kind](t[kind]) for t in (hi, lo)]
                    if kind == "up":
                        o, w = GROUPS_N[b]
                        for k in range(KT):
                            last = triple(pe, m.ps[:, u % 8, :w], [t[:, k, a * P:(a + 1) * P] for t in w2],
                                          [t[:, k, o:o + w] for t in m.h2], k == 0, k == KT - 1)
                    else:
                        for f in range(FT):
                            last = triple(pe, m.ps[:, u % 8, :], [t[:, x, f, a * P:(a + 1) * P] for t in hid],
                                          [t[:, f, 512 * b:512 * b + 512] for t in w2], f == 0, f == FT - 1)
                    last.then_inc(product, 1)


def final_norm(nc, m):
    with ExitStack() as ctx:
        sb = lambda n, s: ctx.enter_context(nc.sbuf_tensor(f"fin_{n}", s, F32))
        sem = lambda n: m.sem(f"fin_{n}")
        gain, junk, y = sb("gain", [P, D]), sb("junk", [P, D]), sb("y", [P, TILES, D])
        stat = sb("stat", [P, 4, TILES])
        loaded, squared, var_ready, std_ready, vec, y_ready, stored = (
            sem(n) for n in ("loaded", "squared", "var", "std", "vec", "y_ready", "stored"))
        with nc.Block() as block:
            @block.sync
            def _(sp):
                sp.dma_start(gain[:], m.a["ln_f"]).then_inc(loaded, 16)
                for t in range(TILES):
                    sp.wait_ge(y_ready, t + 1)
                    dst = m.o["y_p"][t * P:(t + 1) * P, :] if t < TS else m.o["y_s"]
                    sp.dma_start(dst, y[:ROWS[t], t, :]).then_inc(stored, 16)
                sp.wait_ge(stored, 16 * TILES)

            @block.scalar
            def _(act):
                def square(t):
                    if t:
                        act.wait_ge(squared, t)
                    act.activation(junk[:ROWS[t], :], m.x2[:ROWS[t], t, :], ACT.Square,
                                   accum_out=stat[:ROWS[t], 0, t:t + 1]).then_inc(squared, 1)
                square(0)
                for t in range(TILES):
                    if t + 1 < TILES:
                        square(t + 1)
                    act.wait_ge(var_ready, t + 1)
                    act.activation(stat[:ROWS[t], 2, t:t + 1], stat[:ROWS[t], 1, t:t + 1], ACT.Sqrt).then_inc(std_ready, 1)

            @block.vector
            def _(dve):
                link = Link(dve, vec)
                dve.wait_ge(loaded, 16)
                for t in range(TILES):
                    n = ROWS[t]
                    dve.wait_ge(squared, t + 1)
                    dve.tensor_scalar(stat[:n, 1, t:t + 1], stat[:n, 0, t:t + 1], 1.0 / D, EPS, ALU.mult, ALU.add).then_inc(var_ready, 1)
                    dve.wait_ge(std_ready, t + 1)
                    link(dve.reciprocal(stat[:n, 3, t:t + 1], stat[:n, 2, t:t + 1]))
                    dve.scalar_tensor_tensor(y[:n, t, :], m.x2[:n, t, :], stat[:n, 3, t:t + 1], gain[:n, :],
                                             ALU.mult, ALU.mult).then_inc(y_ready, 1)


def mlp(nc, m):
    with ExitStack() as normed:
        m.h2 = [normed.enter_context(nc.sbuf_tensor(n, [P, KT, TOK], F32R)) for n in ("h2_hi", "h2_lo")]
        norm_transpose(nc, m, "ln2", m.a["ln2"], m.h2, m.x2, False)
        mlp_products(nc, m)
    final_norm(nc, m)



def s5(nc, m):
    with ExitStack() as ctx:
        sb = lambda n, s: ctx.enter_context(nc.sbuf_tensor(f"s5_{n}", s, F32))
        sem = lambda n: m.sem(f"s5_{n}")
        M = 8
        CH = NCH + 1
        W = [P] * NCH + [NB * NQ]
        par = sb("par", [P, 3, M])
        dvec, wglu = sb("d", [P, 2]), sb("wglu", [P, 2, 256])
        bpad, cpad = sb("bpad", [P, 2, M, P]), sb("cpad", [P, 2, M, P])
        h0 = sb("h0", [P, 2, M, NB])
        notfirst = sb("notfirst", [P, 64])
        v = sb("v", [P, 24, M])
        bbT = sb("bbT", [P, 2, M, P])
        cs = sb("cs", [P, 2, M, P])
        css = sb("css", [P, 2, M, NB, NQ])
        mags = sb("mags", [P, M, 64])
        magp = sb("magp", [P, M, P])
        bu = sb("bu", [P, 2, M, P])
        rot, rot_p = sb("rot", [P, 2, M, P]), sb("rot_p", [P, 2, M, P])
        h = sb("h", [P, 2, M, P])
        glb, sgb = (sb(n, [P, 2, TOK]) for n in ("gelu", "sigm"))
        gl = lambda o, w: glb[:, :, o:o + w]
        sg = lambda o, w: sgb[:, :, o:o + w]
        fin_p, fin_s = sb("fin_p", [P, M, 2]), sb("fin_s", [P, M, 2, NB])
        loaded = sem("loaded")
        vec = sem("vec")
        (e1, e2, trig_in, trig, bb_made, bbT_turned, bbT_out, neg_made) = (
            sem(n) for n in ("e1", "e2", "trig_in", "trig", "bb_made", "bbT_turned", "bbT_out", "neg_made"))
        (bu_prod, bu_out, pin, vin, scanned, pout, h_ready, yprod, y_out, fin_ready, stored) = (
            sem(n) for n in ("bu_prod", "bu_out", "pin", "vin", "scanned", "pout", "h_ready", "yprod", "y_out", "fin_ready", "stored"))
        (gelu_made, glu, sig_made, mix_made) = (sem(n) for n in ("gelu_made", "glu", "sig_made", "mix_made"))
        LR, LI, LS = range(3)

        def phase(ri, c):
            if c < NCH:
                return cs[:, ri]
            return css[:, ri].rearrange("p m b q -> p m (b q)")
        (DT, MAG, TH, K, RS, RC, COS, SIN, AR, AI, DEN, FR, FI, T0, T1, T2) = range(16)

        with nc.Block() as block:
            @block.sync
            def _(sp):
                at, w = CONST_AT["notfirst"]
                for dst, src in ((par, m.a["s5_par"]), (dvec, m.a["s5_d"]), (bpad, m.a["s5_b"]), (cpad, m.a["s5_c"]),
                                 (h0, m.a["s5_h0"]), (wglu, m.a["w_glu"]), (notfirst, m.const[:, at:at + w])):
                    sp.dma_start(dst[:], src).then_inc(loaded, 16)
                sp.wait_ge(fin_ready, 2)
                sp.dma_start(m.o["s5_p"], fin_p[:]).then_inc(stored, 16)
                sp.dma_start(m.o["s5_s"], fin_s[:]).then_inc(stored, 16)
                sp.wait_ge(stored, 32)

            @block.gpsimd
            def _(pool):
                pool.wait_ge(trig, 3)
                for c in range(CH):
                    n = W[c]
                    pool.wait_ge(bu_out, 2 * (c + 1))
                    if c:
                        pool.wait_ge(h_ready, c)
                    pool.tensor_tensor(rot_p[:, 0, :, :n], bu[:, 0, :, :n], phase(1, c), ALU.mult).then_inc(pin, 1)
                    pool.tensor_tensor(rot_p[:, 1, :, :n], bu[:, 1, :, :n], phase(0, c), ALU.mult).then_inc(pin, 1)
                    pool.wait_ge(scanned, c + 1)
                    pool.tensor_tensor(rot_p[:, 0, :, :n], rot[:, 0, :, :n], phase(1, c), ALU.mult).then_inc(pout, 1)
                    pool.tensor_tensor(rot_p[:, 1, :, :n], rot[:, 1, :, :n], phase(0, c), ALU.mult).then_inc(pout, 1)

            @block.scalar
            def _(act):
                act.wait_ge(loaded, 16 * 7)
                act.activation(v[:, DT], par[:, LS], ACT.Exp).then_inc(e1, 1)
                act.activation(cpad[:, 1], cpad[:, 1], ACT.Copy, scale=-1.0).then_inc(neg_made, 1)
                act.wait_ge(e2, 1)
                act.activation(v[:, MAG], v[:, T0], ACT.Exp).then_inc(e1, 1)
                act.wait_ge(trig_in, 1)
                act.activation(v[:, COS], v[:, RC], ACT.Sin).then_inc(trig, 1)
                act.activation(v[:, SIN], v[:, RS], ACT.Sin).then_inc(trig, 1)
                for ri in range(2):
                    act.wait_ge(bbT_turned, ri + 1)
                    act.activation(bbT[:, ri].rearrange("p m n -> p (m n)"),
                                   m.ps[:, 2 * ri:2 * ri + 2, :].rearrange("p a n -> p (a n)"), ACT.Copy).then_inc(bbT_out, 1)
                for c in range(CH):
                    n = W[c]
                    act.wait_ge(bu_prod, c + 1)
                    if c == 0:
                        act.wait_ge(trig, 3)
                    else:
                        act.wait_ge(pin, 2 * c)
                        act.wait_ge(vin, c)
                    for ri in range(2):
                        act.activation(bu[:, ri, :, :n], m.ps[:, 2 * ri:2 * ri + 2, :].rearrange("p a (q n) -> p (a q) n", n=P)[:, :, :n],
                                       ACT.Copy).then_inc(bu_out, 1)
                    if c >= NCH - 1:
                        act.wait_ge(h_ready, c + 1)
                        if c == NCH - 1:
                            act.activation(fin_p[:], h[:, :, :, P - 1].rearrange("p r m -> p m r"), ACT.Copy).then_inc(fin_ready, 1)
                        else:
                            for ri in range(2):
                                last = act.activation(fin_s[:, :, ri], h[:, ri, :, NQ - 1:NB * NQ:NQ], ACT.Copy)
                            last.then_inc(fin_ready, 1)
                for g, (o, w) in enumerate(GROUPS_N):
                    act.wait_ge(y_out, 2 * CH)
                    act.wait_ge(vin, CH)
                    act.activation(gl(o, w), m.mixT[:, 6:8, o:o + w], ACT.Gelu_apprx_tanh).then_inc(gelu_made, 1)
                for g, (o, w) in enumerate(GROUPS_N):
                    act.wait_ge(glu, g + 1)
                    act.activation(sg(o, w), m.ps[:, 4 + 2 * (g % 2):6 + 2 * (g % 2), :w], ACT.Sigmoid).then_inc(sig_made, 1)

            @block.vector
            def _(dve):
                link = Link(dve, vec)
                tt = dve.tensor_tensor
                dve.wait_ge(e1, 1)
                tt(v[:, T0], par[:, LR], v[:, DT], ALU.mult).then_inc(e2, 1)
                link(tt(v[:, TH], par[:, LI], v[:, DT], ALU.mult))
                link(dve.tensor_scalar(v[:, K], v[:, TH], 1.0 / (2 * np.pi), 12582912.0, ALU.mult, ALU.add))
                link(dve.tensor_scalar(v[:, K], v[:, K], 12582912.0, None, ALU.subtract))
                c1 = 6.28125
                c2 = float(np.float32(2 * np.pi - c1))
                c3 = 2 * np.pi - c1 - c2
                link(dve.scalar_tensor_tensor(v[:, T1], v[:, K], -c1, v[:, TH], ALU.mult, ALU.add))
                link(dve.scalar_tensor_tensor(v[:, T1], v[:, K], -c2, v[:, T1], ALU.mult, ALU.add))
                link(dve.scalar_tensor_tensor(v[:, T1], v[:, K], -c3, v[:, T1], ALU.mult, ALU.add))
                pi = 3.1415925
                link(dve.tensor_scalar(v[:, RS], v[:, T1], pi, -pi, ALU.min, ALU.max))
                link(dve.tensor_scalar(v[:, T1], v[:, T1], np.pi / 2, None, ALU.add))
                link(dve.tensor_scalar(v[:, T2], v[:, T1], np.pi, -2 * np.pi, ALU.is_gt, ALU.mult))
                link(tt(v[:, T1], v[:, T1], v[:, T2], ALU.add))
                dve.tensor_scalar(v[:, RC], v[:, T1], pi, -pi, ALU.min, ALU.max).then_inc(trig_in, 1)
                dve.wait_ge(trig, 2)
                dve.wait_ge(e1, 2)
                link(tt(v[:, AR], v[:, MAG], v[:, COS], ALU.mult))
                link(tt(v[:, AI], v[:, MAG], v[:, SIN], ALU.mult))
                link(dve.tensor_scalar(v[:, AR], v[:, AR], 1.0, None, ALU.subtract))
                link(tt(v[:, T0], par[:, LR], par[:, LR], ALU.mult))
                link(tt(v[:, T1], par[:, LI], par[:, LI], ALU.mult))
                link(tt(v[:, T0], v[:, T0], v[:, T1], ALU.add))
                link(dve.reciprocal(v[:, DEN], v[:, T0]))
                link(tt(v[:, T0], v[:, AR], par[:, LR], ALU.mult))
                link(tt(v[:, T1], v[:, AI], par[:, LI], ALU.mult))
                link(tt(v[:, T0], v[:, T0], v[:, T1], ALU.add))
                link(tt(v[:, FR], v[:, T0], v[:, DEN], ALU.mult))
                link(tt(v[:, T0], v[:, AI], par[:, LR], ALU.mult))
                link(tt(v[:, T1], v[:, AR], par[:, LI], ALU.mult))
                link(tt(v[:, T0], v[:, T0], v[:, T1], ALU.subtract))
                link(tt(v[:, FI], v[:, T0], v[:, DEN], ALU.mult))
                over = lambda c, n: v[:, c].unsqueeze(2).to_broadcast([P, M, n])
                dve.wait_ge(loaded, 16 * 7)
                for ri, (x, y, op) in enumerate(((0, 1, ALU.subtract), (1, 0, ALU.add))):
                    link(tt(rot[:, ri], bpad[:, x], over(FR, P), ALU.mult))
                    link(tt(h[:, ri], bpad[:, y], over(FI, P), ALU.mult))
                    tt(rot[:, ri], rot[:, ri], h[:, ri], op).then_inc(bb_made, 1)
                link(dve.tensor_copy(cs[:, 0, :, 0:1], v[:, COS].unsqueeze(2)))
                link(dve.tensor_copy(cs[:, 1, :, 0:1], v[:, SIN].unsqueeze(2)))
                n = 1
                while n < P:
                    cn = cs[:, 0, :, n - 1:n].to_broadcast([P, M, n])
                    sn = cs[:, 1, :, n - 1:n].to_broadcast([P, M, n])
                    tt(h[:, 0, :, :n], cs[:, 0, :, :n], cn, ALU.mult)
                    tt(h[:, 1, :, :n], cs[:, 1, :, :n], cn, ALU.mult)
                    tt(magp[:, :, :n], cs[:, 1, :, :n], sn, ALU.mult)
                    link(tt(bu[:, 0, :, :n], cs[:, 0, :, :n], sn, ALU.mult))
                    tt(cs[:, 0, :, n:2 * n], h[:, 0, :, :n], magp[:, :, :n], ALU.subtract)
                    last = tt(cs[:, 1, :, n:2 * n], h[:, 1, :, :n], bu[:, 0, :, :n], ALU.add)
                    link(last)
                    n *= 2
                for ri in range(2):
                    dve.tensor_copy(css[:, ri], cs[:, ri, :, :NQ].unsqueeze(2).to_broadcast([P, M, NB, NQ]))
                dve.tensor_copy(magp[:], over(MAG, P))
                tt(mags[:], over(MAG, 64), notfirst[:].unsqueeze(1).to_broadcast([P, M, 64]), ALU.mult)
                for ri in range(2):
                    last = tt(h0[:, ri], h0[:, ri], over(MAG, NB), ALU.mult)
                last.then_inc(trig, 1)
                dve.wait_ge(trig, 3)
                dve.wait_ge(bbT_out, 2)

                def rotate_in(c):
                    n = W[c]
                    dve.wait_ge(bu_out, 2 * (c + 1))
                    tt(rot[:, 0, :, :n], bu[:, 0, :, :n], phase(0, c), ALU.mult)
                    link(tt(rot[:, 1, :, :n], bu[:, 1, :, :n], phase(1, c), ALU.mult))
                    link(tt(rot[:, 0, :, :n], rot[:, 0, :, :n], rot[:, 1, :, :n], ALU.add))
                    dve.wait_ge(pin, 2 * (c + 1))
                    tt(rot[:, 1, :, :n], rot_p[:, 1, :, :n], rot_p[:, 0, :, :n], ALU.subtract).then_inc(vin, 1)
                    dve.wait_ge(vin, c + 1)

                def y_out_of(c):
                    n = W[c]
                    dve.wait_ge(yprod, c + 1)
                    for ct in range(2):
                        dve.scalar_tensor_tensor(m.mixT[:, 6 + ct, c * P:c * P + n], m.uT[:, ct, c * P:c * P + n], dvec[:, ct:ct + 1],
                                                 m.ps[:, 4 + c % 2, ct * P:ct * P + n], ALU.mult, ALU.add).then_inc(y_out, 1)

                for c in range(CH):
                    n = W[c]
                    rotate_in(c)
                    if c == NCH:
                        first = rot[:, :, :, 0:64:NQ]
                        for ri in range(2):
                            last = tt(first[:, ri], first[:, ri], h0[:, ri], ALU.add)
                        link(last)
                    for ri in range(2):
                        for mm in range(M):
                            data0 = magp[:, mm, :] if c < NCH else mags[:, mm, :]
                            init = h[:, ri, mm, P - 1:P] if 0 < c < NCH else 0.0
                            last = dve.tensor_tensor_scan(rot[:, ri, mm, :n], data0[:, :n], rot[:, ri, mm, :n], init,
                                                          ALU.mult, ALU.add)
                    last.then_inc(scanned, 1)
                    dve.wait_ge(scanned, c + 1)
                    if c:
                        dve.wait_ge(yprod, c)
                    if c == NCH:
                        dve.wait_ge(fin_ready, 1)
                    tt(h[:, 0, :, :n], rot[:, 0, :, :n], phase(0, c), ALU.mult)
                    link(tt(h[:, 1, :, :n], rot[:, 1, :, :n], phase(1, c), ALU.mult))
                    link(tt(h[:, 0, :, :n], h[:, 0, :, :n], h[:, 1, :, :n], ALU.subtract))
                    dve.wait_ge(pout, 2 * (c + 1))
                    tt(h[:, 1, :, :n], rot_p[:, 0, :, :n], rot_p[:, 1, :, :n], ALU.add).then_inc(h_ready, 1)
                    dve.wait_ge(h_ready, c + 1)
                    if c:
                        y_out_of(c - 1)
                y_out_of(CH - 1)
                for g, (o, w) in enumerate(GROUPS_N):
                    dve.wait_ge(sig_made, g + 1)
                    tt(m.mixT[:, 6:8, o:o + w], gl(o, w), sg(o, w), ALU.mult).then_inc(mix_made, 1)

            @block.tensor
            def _(pe):
                pe.wait_ge(loaded, 16 * 7)
                for ri in range(2):
                    pe.wait_ge(bb_made, ri + 1)
                    for mm in range(M):
                        last = pe.transpose(m.ps[:, 2 * ri + mm // 4, (mm % 4) * P:(mm % 4) * P + P], rot[:, ri, mm, :], m.ident[:])
                    last.then_inc(bbT_turned, 1)
                pe.wait_ge(bbT_out, 2)
                pe.wait_ge(neg_made, 1)

                def bu_products(c):
                    n = W[c]
                    if c:
                        pe.wait_ge(bu_out, 2 * c)
                    for ri in range(2):
                        for mm in range(M):
                            last = pe.matmul(m.ps[:, 2 * ri + mm // 4, (mm % 4) * P:(mm % 4) * P + n], bbT[:, ri, mm, :],
                                             m.uT[:, mm // 4, c * P:c * P + n], start=True, stop=True)
                    last.then_inc(bu_prod, 1)

                bu_products(0)
                for c in range(CH):
                    n = W[c]
                    if c + 1 < CH:
                        bu_products(c + 1)
                    pe.wait_ge(h_ready, c + 1)
                    if c >= 2:
                        pe.wait_ge(y_out, 2 * (c - 1))
                    for ct in range(2):
                        for i in range(8):
                            mm, ri = 4 * ct + i // 2, i % 2
                            last = pe.matmul(m.ps[:, 4 + c % 2, ct * P:ct * P + n], cpad[:, ri, mm, :], h[:, ri, mm, :n],
                                             start=i == 0, stop=i == 7)
                    last.then_inc(yprod, 1)
                for g, (o, w) in enumerate(GROUPS_N):
                    pe.wait_ge(gelu_made, g + 1)
                    pe.wait_ge(y_out, 2 * CH)
                    if g >= 2:
                        pe.wait_ge(sig_made, g - 1)
                    for co in range(2):
                        for kt in range(2):
                            last = pe.matmul(m.ps[:, 4 + 2 * (g % 2) + co, :w], wglu[:, kt, co * P:co * P + P], gl(o, w)[:, kt, :],
                                             start=kt == 0, stop=kt == 1)
                    last.then_inc(glu, 1)



def hymba_layer(nc, a, o, stages):
    m = Memory()
    with ExitStack() as ctx:
        live = []
        stored = {n: nc.alloc_semaphore(n) for n in ("proj_stored", "dn_stored", "s5_stored", "fin_stored")}

        def sem(name):
            if name in stored:
                return stored[name]
            live.append(nc.alloc_semaphore(name))
            return live[-1]

        def recycle_semaphores():
            nc.clear_and_free_semaphores(live)
            live.clear()
            nc.all_engine_barrier()

        m.sem = sem
        keep = lambda n, s: ctx.enter_context(nc.sbuf_tensor(n, s, F32))
        m.ps = ctx.enter_context(nc.psum_tensor("ps", [P, 8, 512], F32))
        m.const = a["const"]
        m.x_prompt, m.x_sample = a["x_prompt"], a["x_sample"]
        m.w_in = [a["w_feat"][c] for c in range(FEAT)] + [a["w_kv"][0], a["w_kv"][1], a["w_small"]]
        m.cache_win, m.state_conv, m.state_dn = a["cache_win"], a["state_conv"], a["state_dn"]
        m.conv_w, m.a_log, m.dt_bias, m.norm_w = a["conv_w"], a["a_log"], a["dt_bias"], a["norm_w"]
        m.kv_prompt, m.kv_sample, m.win_prompt, m.win_sample = o["kv_p"], o["kv_s"], o["win_p"], o["win_s"]
        m.conv_prompt, m.conv_sample = o["conv_p"], o["conv_s"]
        m.dn_prompt, m.dn_sample = o["dn_p"], o["dn_s"]
        m.a, m.o = a, o
        m.ident = keep("ident", [P, P])
        ident_loaded = m.sem("ident_loaded")
        with nc.Block() as block:
            @block.sync
            def _(sp):
                at, w = CONST_AT["ident"]
                sp.dma_start(m.ident[:], m.const[:, at:at + w]).then_inc(ident_loaded, 16)
                sp.wait_ge(ident_loaded, 16)
        right = lambda stack, n, s, dt=F32: stack.enter_context(nc.sbuf_tensor(n, s, dt, side="right"))
        with ExitStack() as mixers:
            hold = lambda n, s: mixers.enter_context(nc.sbuf_tensor(n, s, F32))
            delta = mixers.enter_context(ExitStack())
            m.dnx = right(delta, "dnx", [P, 6, PADC])
            with ExitStack() as normed:
                m.hT2 = [right(normed, n, [P, KT, PADT], F32R) for n in ("h_hi", "h_lo")]
                norm_transpose(nc, m, "ln1", a["ln1"], m.hT2, None, True)
                m.kv = hold("kv", [P, TILES, KV])
                m.small = hold("small", [P, TILES, SMALL])
                token_projection(nc, m)
                m.qT = hold("qT", [P, 4, TOK])
                m.uT = hold("uT", [P, 2, TOK])
                feature_projection(nc, m)
            m.mixT = hold("mixT", [P, KT, TOK])
            if "dn" in stages:
                delta_net(nc, m)
            delta.close()
            recycle_semaphores()
            if "s5" in stages:
                s5(nc, m)
            if "attn" in stages:
                attention(nc, m)
                recycle_semaphores()
                m.x2 = right(ctx, "x2", [P, TILES, D])
                output_projection(nc, m)
        if "mlp" in stages:
            mlp(nc, m)
        nc.clear_and_free_semaphores(live)



STAGES = ("dn","s5","attn","mlp")


def host_inputs(i):
    f = np.float32
    w = i["w_in"][0]
    kt = lambda x: np.ascontiguousarray(x.reshape(KT, P, -1).transpose(1, 0, 2).reshape(P, -1))
    feat = [np.concatenate([w[:, h * HD:(h + 1) * HD], w[:, (h + 4) * HD:(h + 5) * HD]], 1) for h in range(4)]
    feat += [w[:, 1304 + c * P:1304 + (c + 1) * P] for c in range(6)]
    feat += [w[:, 2336 + c * P:2336 + (c + 1) * P] for c in range(2)]
    a = {
        "const": constants_array(),
        "x_prompt": i["x_prompt"][0], "x_sample": i["x_sample"].reshape(NB * NQ, D),
        "ln1": i["ln1"][0].reshape(KT, P).T,
        "w_feat": np.stack([kt(x) for x in feat]),
        "w_kv": np.stack([kt(w[:, 512:896]), kt(w[:, 896:1280])]),
        "w_small": kt(np.concatenate([w[:, 1280:1304], w[:, 2072:2336]], 1)),
        "cache_win": i["cache_win_kv"][0].reshape(NB, PAST, 256),
        "state_conv": i["state_dn_conv"][0].reshape(NB, 3, 6, P).transpose(3, 2, 0, 1),
        "conv_w": i["dn_conv_w"][0].reshape(6, P, 4).transpose(1, 0, 2),
        "a_log": np.broadcast_to(i["dn_a_log"][0], (P, 4)), "dt_bias": np.broadcast_to(i["dn_dt_bias"][0], (P, 4)),
        "norm_w": np.broadcast_to(i["dn_norm_w"][0], (P, HD)),
    }
    s = np.zeros((2, HD, NB, 2, 2, HD), f)
    dn = i["state_dn"][0].reshape(NB, 2, 2, HD, HD)
    for h in range(2):
        s[h, :, :, :, h] = dn[:, :, h].transpose(2, 0, 1, 3)
    state = lambda x: x.reshape(-1, 8, P).transpose(2, 0, 1)
    a["s5_par"] = state(np.stack([i["s5_lambda_re"][0], i["s5_lambda_im"][0],
                                  np.broadcast_to(i["s5_log_step"][0][:, None], (16, 64))]))
    a["s5_d"] = i["s5_d"][0].reshape(2, P).T
    a["w_glu"] = i["s5_w_glu"][0].reshape(2, P, 256).transpose(1, 0, 2)
    b, c = np.zeros((P, 2, 8, P), f), np.zeros((P, 2, 8, P), f)
    for g in range(16):
        rows, ch = slice((g % 2) * 64, (g % 2) * 64 + 64), slice((g % 8) * 16, (g % 8) * 16 + 16)
        for ri, part in enumerate(("re", "im")):
            b[rows, ri, g // 2, ch] = i["s5_b_" + part][0, g]
            c[rows, ri, g // 2, ch] = i["s5_c_" + part][0, g].T
    a["s5_b"], a["s5_c"] = b, c
    a["s5_h0"] = np.stack([i["state_s5_" + part][0].reshape(NB, 8, P).transpose(2, 1, 0) for part in ("re", "im")], 1)
    wck, wcv = np.zeros((P, 2, 2), f), np.zeros((P, 2, 62), f)
    for blk in range(2):
        wck[64 * blk:64 * blk + 64, :, blk] = i["nsa_wck"][0].T
        wcv[64 * blk:64 * blk + 64, :, 30 + blk] = i["nsa_wcv"][0].T
    a["wck"], a["wcv"] = wck.reshape(P, 4), wcv
    a["page_table"] = i["page_table"].reshape(1, NB * PAGES)
    a["cache_nsa"] = i["cache_nsa_kv"][0].reshape(-1, P, 512)
    a["ln2"] = i["ln2"][0].reshape(KT, P).T
    a["ln_f"] = np.broadcast_to(i["ln_f"], (P, D))
    wo = i["w_out"][0]
    heads = np.concatenate([np.concatenate([wo[h * HD:(h + 1) * HD], wo[(h + 4) * HD:(h + 5) * HD]], 0) for h in range(4)], 0)
    a["w_out"] = kt(np.concatenate([heads, wo[512:]], 0))
    a["w_up"] = i["mlp_up"][0].reshape(KT, P, FF // FG, FG).transpose(2, 1, 0, 3)
    a["w_down"] = i["mlp_down"][0].reshape(FF // FG, FG // P, P, D).transpose(0, 2, 1, 3)
    a["state_dn"] = s.reshape(P, NB, 2, P)
    return a


OUTS = {"y_p": (SEQ, D), "y_s": (NB * NQ, D), "kv_p": (SEQ, 512), "kv_s": (NB * NQ, 512),
        "win_p": (512, 256), "win_s": (NB, PAST + NQ, 256), "conv_p": (P, 6, 3), "conv_s": (P, 6, NB, 3),
        "dn_p": (P, 2, HD), "dn_s": (P, NB, 2, HD), "s5_p": (P, 8, 2), "s5_s": (P, 8, 2, NB)}


def host_outputs(r):
    dn_s = r["dn_s"].reshape(2, HD, NB, 2, HD).transpose(2, 3, 0, 1, 4).reshape(1, NB, 4, HD, HD)
    dn_p = r["dn_p"].reshape(2, HD, 2, HD).transpose(2, 0, 1, 3).reshape(1, 1, 4, HD, HD)
    s5_p = r["s5_p"].transpose(2, 1, 0).reshape(2, 1, 1, 16, 64)
    s5_s = r["s5_s"].transpose(2, 3, 1, 0).reshape(2, 1, NB, 16, 64)
    return (r["y_p"].reshape(1, SEQ, D), r["y_s"].reshape(NB, NQ, D),
            r["kv_p"].reshape(1, 1, SEQ, 4, 2, HD), r["kv_s"].reshape(1, NB, NQ, 4, 2, HD),
            r["win_p"].reshape(1, 1, 512, 2, 2, HD), r["win_s"].reshape(1, NB, PAST + NQ, 2, 2, HD),
            r["conv_p"].transpose(2, 1, 0).reshape(1, 1, 3, KV), r["conv_s"].transpose(2, 3, 1, 0).reshape(1, NB, 3, KV),
            dn_p, dn_s, s5_p[0], s5_s[0], s5_p[1], s5_s[1])


def kernel(**inputs):
    import concourse.bacc as bacc
    from concourse.bass_utils import run_bass_kernel_spmd

    nc = bacc.Bacc("TRN2", target_bir_lowering=False, num_devices=1)
    arrays, a, o = {}, {}, {}
    for name, x in host_inputs({k: np.asarray(v) for k, v in inputs.items()}).items():
        x = np.ascontiguousarray(x)
        arrays["in_" + name] = x
        a[name] = nc.dram_tensor("in_" + name, x.shape, mybir.dt.from_np(x.dtype), kind="ExternalInput").ap()
    for name, shape in OUTS.items():
        o[name] = nc.dram_tensor("out_" + name, shape, F32, kind="ExternalOutput").ap()
    hymba_layer(nc, a, o, STAGES)
    r = run_bass_kernel_spmd(nc, [arrays], core_ids=[0])
    return tuple(np.ascontiguousarray(x) for x in host_outputs({n: np.asarray(r.results[0]["out_" + n]) for n in OUTS}))
```

```python
from contextlib import ExitStack

import numpy as np
import concourse.bass as bass
from concourse import mybir

P = 128
F32 = mybir.dt.float32
F32R = mybir.dt.float32r
I32 = mybir.dt.int32
ALU = mybir.AluOpType
ACT = mybir.ActivationFunctionType
AX = mybir.AxisListType

D = 1024
KT = D // P
SEQ = 1024
NB, NQ = 8, 8
TOK = SEQ + NB * NQ
TILES = SEQ // P + 1
ROWS = [P] * (TILES - 1) + [NB * NQ]
TS = TILES - 1
PADT = TILES * P
GROUPS_N = [(0, 364), (364, 364), (728, 360)]
HD = 64
G, R = 2, 4
PAST = 256
PAGES = 2
WINDOW = 512
KV = 768
KCMP, VCMP, KSEL, VSEL, KWIN, VWIN = (c * P for c in range(6))
SMALL = 24 + 8 + 256
TOKEN_CHUNKS = 4
FEAT = 12
PADC = 3 + SEQ + NB * (3 + NQ)
CONVN = PADC - 3
OUT_CHUNKS = 4
FF = 4096
FG = 256
EPS = 1e-6
NEG = -1e30
MFLOOR = -1e25
NCH = 8
LEVELS = 7
SLEVELS = 3



def constant_tables():
    p = np.arange(P)[:, None]
    f = np.float32
    t = {}
    t["ident"] = np.eye(P, dtype=f)
    t["ones"] = np.ones((P, P), f)
    j = np.arange(1024)[None, :] - 896
    t["dist_sel"] = np.where(j <= p, j - p, NEG).astype(f)
    jw = np.arange(640)[None, :] - 512
    t["dist_win"] = np.where((jw <= p) & (p - jw < WINDOW), jw - p, NEG).astype(f)
    blk = np.arange(16)[None, None, :]
    tok = np.arange(8)[None, :, None] * P + p[:, :, None]
    t["dist_cmp"] = np.where((blk + 1) * 64 - 1 <= tok, blk * 64 + 31.5 - tok, NEG).astype(f).reshape(P, -1)
    q, r, b4 = p % 8, (p // 8) % 4, p // 32
    past = np.arange(PAST)[None, :] - (PAST + q)
    new = np.arange(64)[None, :]
    dist, cmp_ = [], []
    for h in range(2):
        own = (new // 8 == b4 + 4 * h) & (new % 8 <= q)
        dist.append(np.concatenate([past, np.where(own, new % 8 - q, NEG)], 1))
        c = np.arange(32)[None, :]
        cmp_.append(np.where(c // 4 == b4 + 4 * h, (c % 4) * 64 + 31.5 - (PAST + q), NEG))
    t["sdist"] = np.concatenate(dist, 1).astype(f)
    t["sdist_cmp"] = np.concatenate(cmp_, 1).astype(f)
    t["sslope"] = np.concatenate([2.0 ** -(g * 4 + r + 1.0) for g in range(2)], 1).astype(f)
    sel = np.zeros((P, 2, 4, P), f)
    for h in range(2):
        for b in range(4):
            for rr in range(4):
                for qq in range(8):
                    sel[(4 * h + b) * 8 + qq, h, rr, b * 32 + rr * 8 + qq] = 1
    t["gate_sel"] = sel.reshape(P, -1)
    i = np.arange(P)[None, :]
    same = (p // 8 == i // 8) & (p < 64) & (i < 64)
    t["upto"] = (p <= i).astype(f)
    t["upto_s"] = ((p <= i) & same).astype(f)
    t["ones_s"] = same.astype(f)
    t["neg"] = np.where(p <= i, 0, NEG).astype(f)
    t["neg_s"] = np.where((p <= i) & (p // 8 == i // 8), 0, NEG).astype(f)
    t["level"] = np.concatenate([((i >> s) == (p >> s) + 1) & (i >> (s + 1) == p >> (s + 1))
                                 for s in range(LEVELS)], 1).astype(f)
    t["seq_col"] = np.concatenate([np.broadcast_to((np.arange(64)[None, :] // 8) == b, (P, 64))
                                   for b in range(8)], 1).astype(f)
    t["seq_row"] = np.concatenate([(p // 8) == b for b in range(8)], 1).astype(f)
    t["notfirst"] = np.broadcast_to((np.arange(64)[None, :] % 8) != 0, (P, 64)).astype(f)
    return t


CONST_AT = {}


def constants_array():
    t = constant_tables()
    at, cols = 0, []
    for k, v in t.items():
        CONST_AT[k] = (at, v.shape[1])
        at += v.shape[1]
        cols.append(v)
    return np.ascontiguousarray(np.concatenate(cols, 1))


class Link:

    def __init__(self, eng, sem):
        self.eng, self.sem, self.n = eng, sem, 0

    def __call__(self, ins):
        self.n += 1
        ins.then_inc(self.sem, 1)
        self.eng.wait_ge(self.sem, self.n)


class Memory:
    pass



def norm_transpose(nc, m, name, gain, outT, source, load):
    with ExitStack() as ctx:
        sb = lambda n, s: ctx.enter_context(nc.sbuf_tensor(f"{name}_{n}", s, F32))
        sem = m.sem
        if load:
            slots = sb("x", [P, 3, D])
        xn = sb("xn", [P, 2, D])
        whole = sb("whole", [P, 2, KT, P])
        junk = sb("junk", [P, D])
        stat = sb("stat", [P, 4, TILES])
        gainT = sb("gain", [P, KT])
        x_loaded = [sem(f"{name}_x_loaded{i}") for i in range(3)]
        gain_loaded = sem(f"{name}_gain_loaded")
        squared, var_ready, std_ready = sem(f"{name}_squared"), sem(f"{name}_var"), sem(f"{name}_std")
        normed, turned, evacuated = sem(f"{name}_normed"), sem(f"{name}_turned"), sem(f"{name}_evac")
        vec, hi_made, lo_made = sem(f"{name}_vec"), sem(f"{name}_hi_made"), sem(f"{name}_lo_made")
        hiT, loT = outT

        def x_at(t):
            return (slots[:ROWS[t], t % 3, :] if load else source[:ROWS[t], t, :])

        with nc.Block() as block:
            @block.sync
            def _(sp):
                sp.dma_start(gainT[:], gain).then_inc(gain_loaded, 16)
                if load:
                    for t in range(TILES):
                        if t >= 3:
                            sp.wait_ge(normed, t - 2)
                        src = m.x_prompt[t * P:(t + 1) * P, :] if t < TS else m.x_sample
                        sp.dma_start(x_at(t), src).then_inc(x_loaded[t % 3], 16)

            @block.gpsimd
            def _(pool):
                if hiT.shape[2] > TOK:
                    for part in outT:
                        pool.memset(part[:, :, TOK:].bitcast(F32), 0.0)

            @block.scalar
            def _(act):
                def square(t):
                    if load:
                        act.wait_ge(x_loaded[t % 3], 16 * (t // 3 + 1))
                    if t:
                        act.wait_ge(squared, t)
                    act.activation(junk[:ROWS[t], :], x_at(t), ACT.Square,
                                   accum_out=stat[:ROWS[t], 0, t:t + 1]).then_inc(squared, 1)

                def split(t):
                    n = ROWS[t]
                    act.wait_ge(evacuated, 2 * (t + 1))
                    act.activation(hiT[:, :, t * P:t * P + n], whole[:, t % 2, :, :n], ACT.Copy).then_inc(hi_made, 1)
                square(0)
                for t in range(TILES):
                    if t + 1 < TILES:
                        square(t + 1)
                    act.wait_ge(var_ready, t + 1)
                    act.activation(stat[:ROWS[t], 2, t:t + 1], stat[:ROWS[t], 1, t:t + 1],
                                   ACT.Sqrt).then_inc(std_ready, 1)
                    if t >= 2:
                        split(t - 2)
                split(TILES - 2)
                split(TILES - 1)

            @block.vector
            def _(dve):
                link = Link(dve, vec)

                def subtract(t):
                    n = ROWS[t]
                    dve.wait_ge(hi_made, t + 1)
                    dve.tensor_tensor(loT[:, :, t * P:t * P + n], whole[:, t % 2, :, :n], hiT[:, :, t * P:t * P + n],
                                      ALU.subtract).then_inc(lo_made, 1)

                def evacuate(t):
                    dve.wait_ge(turned, t + 1)
                    if t >= 2:
                        dve.wait_ge(lo_made, t - 1)
                    for h in range(2):
                        bank = m.ps[:, (t % 2) * 2 + h, :].rearrange("p (k n) -> p k n", k=4)[:, :, :ROWS[t]]
                        dve.tensor_tensor(whole[:, t % 2, 4 * h:4 * h + 4, :ROWS[t]], bank,
                                          gainT[:, 4 * h:4 * h + 4].unsqueeze(2).to_broadcast([P, 4, ROWS[t]]),
                                          ALU.mult).then_inc(evacuated, 1)
                dve.wait_ge(gain_loaded, 16)
                for t in range(TILES):
                    n = ROWS[t]
                    dve.wait_ge(squared, t + 1)
                    dve.tensor_scalar(stat[:n, 1, t:t + 1], stat[:n, 0, t:t + 1], 1.0 / D, EPS,
                                      ALU.mult, ALU.add).then_inc(var_ready, 1)
                    dve.wait_ge(std_ready, t + 1)
                    link(dve.reciprocal(stat[:n, 3, t:t + 1], stat[:n, 2, t:t + 1]))
                    if t >= 2:
                        dve.wait_ge(turned, t - 1)
                    dve.tensor_scalar(xn[:n, t % 2, :], x_at(t), stat[:n, 3, t:t + 1], None,
                                      ALU.mult).then_inc(normed, 1)
                    if t >= 3:
                        subtract(t - 3)
                    if t:
                        evacuate(t - 1)
                subtract(TILES - 3)
                evacuate(TILES - 1)
                subtract(TILES - 2)
                subtract(TILES - 1)

            @block.tensor
            def _(pe):
                for t in range(TILES):
                    pe.wait_ge(normed, t + 1)
                    if t >= 2:
                        pe.wait_ge(evacuated, 2 * (t - 1))
                    for k in range(KT):
                        last = pe.transpose(m.ps[:, (t % 2) * 2 + k // 4, (k % 4) * P:(k % 4) * P + ROWS[t]],
                                            xn[:ROWS[t], t % 2, k * P:(k + 1) * P],
                                            m.ident[:ROWS[t], :ROWS[t]])
                    last.then_inc(turned, 1)


def triple(pe, out, lhs, rhs, first, last):
    pe.matmul(out, lhs[0], rhs[0], start=first, stop=False)
    pe.matmul(out, lhs[0], rhs[1], start=False, stop=False)
    return pe.matmul(out, lhs[1], rhs[0], start=False, stop=last)



def no_steps(*_):
    pass


def project(nc, m, name, chunks, widths, units, evacuation, feature, banks=range(8), side=None, evac=None,
            preload=None, out_by_dve=False):
    side = side or {}
    with ExitStack() as ctx:
        sem = lambda n: m.sem(f"{name}_{n}")
        NC, W, BANKS = len(chunks), KT * max(widths), len(banks)
        if preload is None:
            preload = ctx.enter_context(nc.sbuf_tensor(f"{name}_raw", [P, W], F32)), sem("w_loaded")
            loads = range(NC)
        else:
            loads = range(1, NC)
        raw, w_loaded = preload
        hi, lo = (ctx.enter_context(nc.sbuf_tensor(f"{name}_{n}", [P, 2, W], F32R)) for n in ("whi", "wlo"))
        hi_made, lo_made, product = (sem(n) for n in ("hi_made", "lo_made", "product"))
        evac = evac or [sem("evac_act"), sem("evac_dve")]
        ends = [max(u for u, unit in enumerate(units) if unit[0] == c) + 1 for c in range(NC)]
        begins = [0] + ends[:-1]

        def out_by(u):
            return (1, u + 1) if out_by_dve else (u % 2, u // 2 + 1)

        def slot(t, c):
            return t[:, c % 2, :KT * widths[c]].rearrange("p (k n) -> p k n", k=KT)

        with nc.Block() as block:
            @block.sync
            def _(sp):
                side.get("sync_first", no_steps)(sp, evac)
                for c in loads:
                    if c:
                        sp.wait_ge(lo_made, c)
                    sp.dma_start(raw[:, :KT * widths[c]], chunks[c]).then_inc(w_loaded, 16)
                side.get("sync", no_steps)(sp, evac)

            @block.gpsimd
            def _(pool):
                side.get("gpsimd", no_steps)(pool, evac)

            @block.scalar
            def _(act):
                def round_weights(c):
                    act.wait_ge(w_loaded, 16 * (c + 1))
                    if c >= 2:
                        act.wait_ge(product, ends[c - 2])
                    n = KT * widths[c]
                    act.activation(hi[:, c % 2, :n], raw[:, :n], ACT.Copy).then_inc(hi_made, 1)
                round_weights(0)
                side.get("scalar_first", no_steps)(act, evac)
                for u in range(len(units)):
                    if u in begins and begins.index(u) + 1 < NC:
                        round_weights(begins.index(u) + 1)
                    if out_by(u)[0] == 0:
                        act.wait_ge(product, u + 1)
                        evacuation(act, True, u).then_inc(evac[0], 1)
                    side.get("scalar", no_steps)(act, u)
                side.get("stores", no_steps)(act, evac)

            @block.vector
            def _(dve):
                def rest_of_weights(c):
                    dve.wait_ge(hi_made, c + 1)
                    n = KT * widths[c]
                    dve.tensor_tensor(lo[:, c % 2, :n], raw[:, :n], hi[:, c % 2, :n], ALU.subtract).then_inc(lo_made, 1)
                rest_of_weights(0)
                side.get("vector_first", no_steps)(dve, evac)
                for u in range(len(units)):
                    if u in begins and begins.index(u) + 1 < NC:
                        rest_of_weights(begins.index(u) + 1)
                    if out_by(u)[0]:
                        dve.wait_ge(product, u + 1)
                        evacuation(dve, False, u).then_inc(evac[1], 1)
                    side.get("vector", no_steps)(dve, u)

            @block.tensor
            def _(pe):
                side.get("tensor_first", no_steps)(pe, evac)
                for u, (c, n) in enumerate(units):
                    if u in begins:
                        pe.wait_ge(lo_made, c + 1)
                    if u >= BANKS:
                        pe.wait_ge(evac[out_by(u - BANKS)[0]], out_by(u - BANKS)[1])
                    w = (slot(hi, c), slot(lo, c))
                    bank = m.ps[:, banks[u % BANKS], :]
                    for k in range(KT):
                        wk = [x[:, k, :] for x in w]
                        if feature:
                            o, width = GROUPS_N[n]
                            last = triple(pe, bank[:, :width], wk, [x[:, k, o:o + width] for x in m.hT2],
                                          k == 0, k == KT - 1)
                        else:
                            last = triple(pe, bank[:, :widths[c]],
                                          [x[:, k, n * P:(n + 1) * P] for x in m.hT2], wk, k == 0, k == KT - 1)
                    last.then_inc(product, 1)
                    side.get("tensor", no_steps)(pe, u)


def token_projection(nc, m, tokens):
    stored, zeroed = m.sem("proj_stored"), m.sem("kv_zeroed")
    units = [(c, t) for c in range(TOKEN_CHUNKS) for t in range(TILES)]
    width = (KV + SMALL) // TOKEN_CHUNKS

    def evacuation(eng, scalar, u):
        c, t = units[u]
        rows = ROWS[t]
        src, dst = m.ps[:rows, u % 8, :width], tokens[:rows, t, width * c:width * (c + 1)]
        return eng.activation(dst, src, ACT.Copy) if scalar else eng.tensor_copy(dst, src)

    def stores(sp, evac):
        sp.wait_ge(evac[0], (len(units) + 1) // 2)
        sp.wait_ge(evac[1], len(units) // 2)
        for t in range(TS):
            sp.dma_start(m.kv_prompt[t * P:(t + 1) * P, :], m.kv[:, t, 0:512]).then_inc(stored, 16)
            if t >= TS // 2:
                sp.dma_start(m.win_prompt[(t - 4) * P:(t - 3) * P, :], m.kv[:, t, 512:768]).then_inc(stored, 16)
        sp.dma_start(m.kv_sample, m.kv[:NB * NQ, TS, 0:512]).then_inc(stored, 16)
        for b in range(NB):
            sp.dma_start(m.win_sample[b, PAST:PAST + NQ, :],
                         m.kv[b * NQ:(b + 1) * NQ, TS, 512:768]).then_inc(stored, 16)
        sp.dma_start(m.win_sample[:, 0:PAST, :], m.cache_win).then_inc(stored, 16)

    def gpsimd(pool, _):
        pool.memset(m.small[64:128, TS, :], 0.0).then_inc(zeroed, 1)

    project(nc, m, "kvp", m.w_in[FEAT:], [width] * TOKEN_CHUNKS, units, evacuation, False, side={"stores": stores, "gpsimd": gpsimd},
            preload=m.token_raw)


def query_projection(nc, m):
    with ExitStack() as ctx:
        units = [(c, n) for c in range(4) for n in range(3)]
        convw = ctx.enter_context(nc.sbuf_tensor("convw", [P, 6, 4], F32))
        conv = m.mixT[:, 0:6, :]
        loaded, tap, conv_made, silu_made = (m.sem(f"conv_{n}") for n in ("loaded", "tap", "made", "silu"))

        def evacuation(eng, scalar, u):
            c, n = units[u]
            o, w = GROUPS_N[n]
            src, dst = m.ps[:, u % 8, :w], m.qT[:, c, o:o + w]
            if scalar:
                return eng.activation(dst, src, ACT.Copy, scale=0.125)
            return eng.tensor_scalar(dst, src, 0.125, None, ALU.mult)

        def load(pool, _):
            pool.dma_start(convw[:], m.conv_w).then_inc(loaded, 16)

        def load_next(sp, _):
            sp.dma_start(m.token_raw[0], m.w_in[FEAT]).then_inc(m.token_raw[1], 16)

        def vector(dve, u):
            if u % 2 == 0:
                return
            f = u // 2
            if f == 0:
                dve.wait_ge(loaded, 16)
            for j in range(4):
                src, w = m.dnx[:, f, j:j + CONVN], convw[:, f, j:j + 1]
                if j == 0:
                    dve.tensor_scalar(conv[:, f, :CONVN], src, w, None, ALU.mult).then_inc(tap, 1)
                else:
                    last = dve.scalar_tensor_tensor(conv[:, f, :CONVN], src, w, conv[:, f, :CONVN], ALU.mult, ALU.add)
                    last.then_inc(conv_made if j == 3 else tap, 1)
                if j < 3:
                    dve.wait_ge(tap, 3 * f + j + 1)

        def silu(act, f):
            act.wait_ge(conv_made, f + 1)
            act.activation(conv[:, f, :SEQ], conv[:, f, :SEQ], ACT.Silu).then_inc(silu_made, 1)
            act.activation(m.convs[:, f].rearrange("p (b q) -> p b q", b=NB),
                           conv[:, f, 3 + SEQ:].rearrange("p (b s) -> p b s", b=NB)[:, :, :NQ],
                           ACT.Silu).then_inc(silu_made, 1)

        def scalar(act, u):
            if u % 2 and u > 1:
                silu(act, u // 2 - 1)
            if u == len(units) - 1:
                silu(act, 5)

        project(nc, m, "qp", m.w_in[:4], [P] * 4, units, evacuation, True,
                side={"gpsimd": load, "sync": load_next, "vector": vector, "scalar": scalar})


def feature_and_s5(nc, m):
    with ExitStack() as ctx:
        convbuf = ctx.enter_context(nc.sbuf_tensor("convbuf", [P, 6, NB, 3], F32))
        stored, conv_in, conv_put = m.sem("proj_stored"), m.sem("conv_in"), m.sem("conv_put")
        units = [(c, n) for c in range(8) for n in range(3)]
        banks = [5, 6, 7]
        evac = [m.sem("fp_evac_act"), m.sem("fp_evac_dve")]
        s5 = S5(nc, m, ctx, evac)

        def evacuation(eng, scalar, u):
            c, n = units[u]
            o, w = GROUPS_N[n]
            src = m.ps[:, banks[u % 3], :w]
            if c < 2:
                dst = m.uT[:, c, o:o + w]
            elif n < 2:
                dst = m.dnx[:, c - 2, 3 + o:3 + o + w]
            else:
                dst, part = m.dnx[:, c - 2, 3 + o:3 + SEQ], src[:, :SEQ - o]
                if scalar:
                    eng.activation(dst, part, ACT.Copy)
                else:
                    eng.tensor_copy(dst, part)
                dst = m.dnx[:, c - 2, 3 + SEQ:].rearrange("p (b s) -> p b s", b=NB)[:, :, 3:]
                src = src[:, SEQ - o:].rearrange("p (b s) -> p b s", b=NB)
            return eng.activation(dst, src, ACT.Copy) if scalar else eng.tensor_copy(dst, src)

        def stores(sp, evac):
            sp.wait_ge(evac[0], (len(units) + 1) // 2)
            sp.wait_ge(evac[1], len(units) // 2)
            sp.wait_ge(conv_put, 7)
            sp.dma_start(m.conv_prompt, m.dnx[:, :, SEQ:SEQ + 3]).then_inc(stored, 16)
            for f in range(6):
                sp.dma_start(m.conv_sample[:, f],
                             m.dnx[:, f, 3 + SEQ:].rearrange("p (b s) -> p b s", b=NB)[:, :, NQ:NQ + 3]
                             ).then_inc(stored, 16)
            s5.store(sp)
            sp.wait_ge(stored, 16 * 7)

        def gpsimd(pool, _):
            pool.dma_start(convbuf[:], m.state_conv).then_inc(conv_in, 16)
            s5.load(pool)
            pool.memset(m.dnx[:, :, 0:3], 0.0).then_inc(conv_put, 1)
            pool.wait_ge(conv_in, 16)
            pool.wait_ge(conv_put, 1)
            for f in range(6):
                pool.tensor_copy(m.dnx[:, f, 3 + SEQ:].rearrange("p (b s) -> p b s", b=NB)[:, :, 0:3],
                                 convbuf[:, f]).then_inc(conv_put, 1)
            s5.pool(pool)

        project(nc, m, "fp", m.w_in[10:FEAT] + m.w_in[4:10], [P] * 8, units, evacuation, True, banks,
                {"sync": stores, "gpsimd": gpsimd, "scalar": s5.scalar, "vector": s5.vector, "tensor": s5.tensor}, evac)


STORES_OF_INPUT = TS + TS // 2 + 1 + NB + 1 + 1 + 6



class S5:
    M = 8
    CH = NCH + 1
    W = [P] * NCH + [NB * NQ]
    LR, LI, LS = range(3)
    (DT, MAG, TH, K, RS, RC, COS, SIN, AR, AI, DEN, FR, FI, T0, T1, T2) = range(16)

    def __init__(self, nc, m, stack, u_out):
        self.m, self.u_out = m, u_out
        M = self.M
        sb = lambda n, s: stack.enter_context(nc.sbuf_tensor(f"s5_{n}", s, F32))
        flat = m.mixT[:].rearrange("p k n -> p (k n)")
        parts = lambda i: flat[:, i * 2 * M * P:(i + 1) * 2 * M * P].rearrange("p (r m n) -> p r m n", r=2, m=M)
        self.bu, self.rot, self.rot_p = parts(0), parts(1), parts(2)
        self.bpad = self.bu
        self.mags = flat[:, 6 * M * P:6 * M * P + 64 * M].rearrange("p (m n) -> p m n", m=M)
        self.gelu, self.sigm = m.mixT[:, 0:2, :], m.mixT[:, 2:4, :]
        self.par = sb("par", [P, 3, M])
        self.dvec, self.wglu = sb("d", [P, 2]), sb("wglu", [P, 2, 256])
        self.cpad = sb("cpad", [P, 2, M, P])
        self.h0 = sb("h0", [P, 2, M, NB])
        self.notfirst = sb("notfirst", [P, 64])
        self.v = sb("v", [P, 16, M])
        self.bbT = sb("bbT", [P, 2, M, P])
        self.cs = sb("cs", [P, 2, M, P])
        self.magp = sb("magp", [P, M, P])
        self.h = sb("h", [P, 2, M, P])
        self.fin_p, self.fin_s = sb("fin_p", [P, M, 2]), sb("fin_s", [P, M, 2, NB])
        sem = lambda n: m.sem(f"s5_{n}")
        self.loaded, self.vec, self.e1, self.e2 = (sem(n) for n in ("loaded", "vec", "e1", "e2"))
        self.trig_in, self.trig, self.bb_made, self.bbT_turned = (sem(n) for n in ("trig_in", "trig", "bb_made", "bbT_turned"))
        self.bbT_out, self.neg_made, self.bu_prod, self.bu_out = (sem(n) for n in ("bbT_out", "neg_made", "bu_prod", "bu_out"))
        self.pin, self.vin, self.scanned, self.pout = (sem(n) for n in ("pin", "vin", "scanned", "pout"))
        self.h_ready, self.yprod, self.y_out, self.fin_ready = (sem(n) for n in ("h_ready", "yprod", "y_out", "fin_ready"))
        self.stored, self.gelu_made, self.glu, self.sig_made = (sem(n) for n in ("stored", "gelu_made", "glu", "sig_made"))
        self.mix_made = sem("mix_made")

    def shape(self, x, c):
        if c < NCH:
            return x
        return x[:, :, :NB * NQ].rearrange("p m (b q) -> p m b q", b=NB)

    def phase(self, ri, c):
        if c < NCH:
            return self.cs[:, ri]
        return self.cs[:, ri, :, :NQ].unsqueeze(2).to_broadcast([P, self.M, NB, NQ])

    def load(self, pool):
        m = self.m
        at, w = CONST_AT["notfirst"]
        for dst, src in ((self.par[:], m.a["s5_par"]), (self.bpad, m.a["s5_b"]), (self.cpad[:], m.a["s5_c"]),
                         (self.dvec[:], m.a["s5_d"]), (self.h0[:], m.a["s5_h0"]), (self.wglu[:], m.a["w_glu"]),
                         (self.notfirst[:], m.const[:, at:at + w])):
            pool.dma_start(dst, src).then_inc(self.loaded, 16)

    def store(self, sp):
        sp.wait_ge(self.fin_ready, 2)
        sp.dma_start(self.m.o["s5_p"], self.fin_p[:]).then_inc(self.stored, 16)
        sp.dma_start(self.m.o["s5_s"], self.fin_s[:]).then_inc(self.stored, 16)
        sp.wait_ge(self.stored, 32)


    def pool(self, pool):
        bu, rot, rot_p, at = self.bu, self.rot, self.rot_p, self.shape
        pool.wait_ge(self.trig, 3)
        for c in range(self.CH):
            pool.wait_ge(self.bu_out, 2 * (c + 1))
            if c:
                pool.wait_ge(self.h_ready, c)
            for ri in range(2):
                pool.tensor_tensor(at(rot_p[:, ri], c), at(bu[:, ri], c), self.phase(1 - ri, c), ALU.mult).then_inc(self.pin, 1)
            pool.wait_ge(self.scanned, c + 1)
            for ri in range(2):
                pool.tensor_tensor(at(rot_p[:, ri], c), at(rot[:, ri], c), self.phase(1 - ri, c), ALU.mult).then_inc(self.pout, 1)


    def scalar(self, act, u):
        v, m = self.v, self.m
        if u == 0:
            act.wait_ge(self.loaded, 16 * 7)
            act.activation(v[:, self.DT], self.par[:, self.LS], ACT.Exp).then_inc(self.e1, 1)
            act.activation(self.cpad[:, 1], self.cpad[:, 1], ACT.Copy, scale=-1.0).then_inc(self.neg_made, 1)
        if u == 1:
            act.wait_ge(self.e2, 1)
            act.activation(v[:, self.MAG], v[:, self.T0], ACT.Exp).then_inc(self.e1, 1)
        if u == 2:
            act.wait_ge(self.trig_in, 1)
            act.activation(v[:, self.COS], v[:, self.RC], ACT.Sin).then_inc(self.trig, 1)
            act.activation(v[:, self.SIN], v[:, self.RS], ACT.Sin).then_inc(self.trig, 1)
        if u == 5:
            for ri in range(2):
                act.wait_ge(self.bbT_turned, ri + 1)
                act.activation(self.bbT[:, ri].rearrange("p m n -> p (m n)"),
                               m.ps[:, 2 * ri:2 * ri + 2, :].rearrange("p a n -> p (a n)"), ACT.Copy).then_inc(self.bbT_out, 1)
        c = (u - 5) // 2
        if u >= 5 and u % 2 and c < self.CH:
            n = self.W[c]
            act.wait_ge(self.bu_prod, c + 1)
            if c == 0:
                act.wait_ge(self.trig, 3)
            else:
                act.wait_ge(self.pin, 2 * c)
                act.wait_ge(self.vin, c)
            for ri in range(2):
                act.activation(self.bu[:, ri, :, :n],
                               m.ps[:, 2 * ri:2 * ri + 2, :].rearrange("p a (q n) -> p (a q) n", n=P)[:, :, :n],
                               ACT.Copy).then_inc(self.bu_out, 1)
        if u == 20:
            act.wait_ge(self.h_ready, NCH)
            act.activation(self.fin_p[:], self.h[:, :, :, P - 1].rearrange("p r m -> p m r"), ACT.Copy).then_inc(self.fin_ready, 1)
        if u == 22:
            act.wait_ge(self.h_ready, self.CH)
            for ri in range(2):
                last = act.activation(self.fin_s[:, :, ri], self.h[:, ri, :, NQ - 1:NB * NQ:NQ], ACT.Copy)
            last.then_inc(self.fin_ready, 1)
        if u == 23:
            act.wait_ge(self.y_out, 2 * self.CH)
            act.wait_ge(self.vin, self.CH)
            for o, w in GROUPS_N:
                act.activation(self.gelu[:, :, o:o + w], m.mixT[:, 6:8, o:o + w], ACT.Gelu_apprx_tanh).then_inc(self.gelu_made, 1)
            for g, (o, w) in enumerate(GROUPS_N):
                act.wait_ge(self.glu, g + 1)
                act.activation(self.sigm[:, :, o:o + w], m.ps[:, 2 * (g % 2):2 * (g % 2) + 2, :w], ACT.Sigmoid).then_inc(self.sig_made, 1)


    def vector(self, dve, u):
        if u == 0:
            self.link = Link(dve, self.vec)
        if u == 1:
            self.angles(dve)
        if u == 3:
            self.input_matrix(dve)
        if u == 5:
            self.tables(dve)
        c = (u - 5) // 2
        if u >= 5 and u % 2 and c < self.CH:
            self.chunk(dve, c)
        if u == 23:
            self.y_out_of(dve, self.CH - 1)
            for g, (o, w) in enumerate(GROUPS_N):
                dve.wait_ge(self.sig_made, g + 1)
                dve.tensor_tensor(self.m.mixT[:, 6:8, o:o + w], self.gelu[:, :, o:o + w], self.sigm[:, :, o:o + w],
                                  ALU.mult).then_inc(self.mix_made, 1)

    def angles(self, dve):
        v, par, tt, link = self.v, self.par, dve.tensor_tensor, self.link
        DT, TH, K, RS, RC, T0, T1, T2 = (self.DT, self.TH, self.K, self.RS, self.RC, self.T0, self.T1, self.T2)
        dve.wait_ge(self.e1, 1)
        tt(v[:, T0], par[:, self.LR], v[:, DT], ALU.mult).then_inc(self.e2, 1)
        link(tt(v[:, TH], par[:, self.LI], v[:, DT], ALU.mult))
        link(dve.tensor_scalar(v[:, K], v[:, TH], 1.0 / (2 * np.pi), 12582912.0, ALU.mult, ALU.add))
        link(dve.tensor_scalar(v[:, K], v[:, K], 12582912.0, None, ALU.subtract))
        c1 = 6.28125
        c2 = float(np.float32(2 * np.pi - c1))
        c3 = 2 * np.pi - c1 - c2
        link(dve.scalar_tensor_tensor(v[:, T1], v[:, K], -c1, v[:, TH], ALU.mult, ALU.add))
        link(dve.scalar_tensor_tensor(v[:, T1], v[:, K], -c2, v[:, T1], ALU.mult, ALU.add))
        link(dve.scalar_tensor_tensor(v[:, T1], v[:, K], -c3, v[:, T1], ALU.mult, ALU.add))
        pi = 3.1415925
        link(dve.tensor_scalar(v[:, RS], v[:, T1], pi, -pi, ALU.min, ALU.max))
        link(dve.tensor_scalar(v[:, T1], v[:, T1], np.pi / 2, None, ALU.add))
        link(dve.tensor_scalar(v[:, T2], v[:, T1], np.pi, -2 * np.pi, ALU.is_gt, ALU.mult))
        link(tt(v[:, T1], v[:, T1], v[:, T2], ALU.add))
        dve.tensor_scalar(v[:, RC], v[:, T1], pi, -pi, ALU.min, ALU.max).then_inc(self.trig_in, 1)

    def over(self, c, n):
        return self.v[:, c].unsqueeze(2).to_broadcast([P, self.M, n])

    def input_matrix(self, dve):
        v, par, tt, link, h, rot = self.v, self.par, dve.tensor_tensor, self.link, self.h, self.rot
        LR, LI, AR, AI, DEN, FR, FI, T0, T1 = (self.LR, self.LI, self.AR, self.AI, self.DEN, self.FR, self.FI, self.T0, self.T1)
        dve.wait_ge(self.trig, 2)
        dve.wait_ge(self.e1, 2)
        link(tt(v[:, AR], v[:, self.MAG], v[:, self.COS], ALU.mult))
        link(tt(v[:, AI], v[:, self.MAG], v[:, self.SIN], ALU.mult))
        link(dve.tensor_scalar(v[:, AR], v[:, AR], 1.0, None, ALU.subtract))
        link(tt(v[:, T0], par[:, LR], par[:, LR], ALU.mult))
        link(tt(v[:, T1], par[:, LI], par[:, LI], ALU.mult))
        link(tt(v[:, T0], v[:, T0], v[:, T1], ALU.add))
        link(dve.reciprocal(v[:, DEN], v[:, T0]))
        link(tt(v[:, T0], v[:, AR], par[:, LR], ALU.mult))
        link(tt(v[:, T1], v[:, AI], par[:, LI], ALU.mult))
        link(tt(v[:, T0], v[:, T0], v[:, T1], ALU.add))
        link(tt(v[:, FR], v[:, T0], v[:, DEN], ALU.mult))
        link(tt(v[:, T0], v[:, AI], par[:, LR], ALU.mult))
        link(tt(v[:, T1], v[:, AR], par[:, LI], ALU.mult))
        link(tt(v[:, T0], v[:, T0], v[:, T1], ALU.subtract))
        link(tt(v[:, FI], v[:, T0], v[:, DEN], ALU.mult))
        dve.wait_ge(self.loaded, 16 * 7)
        for ri, (x, y, op) in enumerate(((0, 1, ALU.subtract), (1, 0, ALU.add))):
            link(tt(rot[:, ri], self.bpad[:, x], self.over(FR, P), ALU.mult))
            link(tt(h[:, ri], self.bpad[:, y], self.over(FI, P), ALU.mult))
            tt(rot[:, ri], rot[:, ri], h[:, ri], op).then_inc(self.bb_made, 1)

    def tables(self, dve):
        v, tt, link, h, cs, bu, magp = self.v, dve.tensor_tensor, self.link, self.h, self.cs, self.bu, self.magp
        M, MAG = self.M, self.MAG
        dve.wait_ge(self.bb_made, 2)
        link(dve.tensor_copy(cs[:, 0, :, 0:1], v[:, self.COS].unsqueeze(2)))
        link(dve.tensor_copy(cs[:, 1, :, 0:1], v[:, self.SIN].unsqueeze(2)))
        n = 1
        while n < P:
            cn = cs[:, 0, :, n - 1:n].to_broadcast([P, M, n])
            sn = cs[:, 1, :, n - 1:n].to_broadcast([P, M, n])
            tt(h[:, 0, :, :n], cs[:, 0, :, :n], cn, ALU.mult)
            tt(h[:, 1, :, :n], cs[:, 1, :, :n], cn, ALU.mult)
            tt(magp[:, :, :n], cs[:, 1, :, :n], sn, ALU.mult)
            link(tt(bu[:, 0, :, :n], cs[:, 0, :, :n], sn, ALU.mult))
            tt(cs[:, 0, :, n:2 * n], h[:, 0, :, :n], magp[:, :, :n], ALU.subtract)
            link(tt(cs[:, 1, :, n:2 * n], h[:, 1, :, :n], bu[:, 0, :, :n], ALU.add))
            n *= 2
        dve.tensor_copy(magp[:], self.over(MAG, P))
        tt(self.mags, self.over(MAG, 64), self.notfirst[:].unsqueeze(1).to_broadcast([P, M, 64]), ALU.mult)
        for ri in range(2):
            last = tt(self.h0[:, ri], self.h0[:, ri], self.over(MAG, NB), ALU.mult)
        last.then_inc(self.trig, 1)
        dve.wait_ge(self.trig, 3)
        dve.wait_ge(self.bbT_out, 2)

    def y_out_of(self, dve, c):
        m, n = self.m, self.W[c]
        dve.wait_ge(self.yprod, c + 1)
        for ct in range(2):
            dve.scalar_tensor_tensor(m.mixT[:, 6 + ct, c * P:c * P + n], m.uT[:, ct, c * P:c * P + n], self.dvec[:, ct:ct + 1],
                                     m.ps[:, 4, ct * P:ct * P + n], ALU.mult, ALU.add).then_inc(self.y_out, 1)

    def chunk(self, dve, c):
        tt, link, n = dve.tensor_tensor, self.link, self.W[c]
        bu, rot, rot_p, h, at = self.bu, self.rot, self.rot_p, self.h, self.shape
        dve.wait_ge(self.bu_out, 2 * (c + 1))
        tt(at(rot[:, 0], c), at(bu[:, 0], c), self.phase(0, c), ALU.mult)
        link(tt(at(rot[:, 1], c), at(bu[:, 1], c), self.phase(1, c), ALU.mult))
        link(tt(rot[:, 0, :, :n], rot[:, 0, :, :n], rot[:, 1, :, :n], ALU.add))
        dve.wait_ge(self.pin, 2 * (c + 1))
        tt(rot[:, 1, :, :n], rot_p[:, 1, :, :n], rot_p[:, 0, :, :n], ALU.subtract).then_inc(self.vin, 1)
        dve.wait_ge(self.vin, c + 1)
        if c == NCH:
            first = rot[:, :, :, 0:64:NQ]
            for ri in range(2):
                last = tt(first[:, ri], first[:, ri], self.h0[:, ri], ALU.add)
            link(last)
        for ri in range(2):
            for mm in range(self.M):
                data0 = self.magp[:, mm, :] if c < NCH else self.mags[:, mm, :]
                init = h[:, ri, mm, P - 1:P] if 0 < c < NCH else 0.0
                last = dve.tensor_tensor_scan(rot[:, ri, mm, :n], data0[:, :n], rot[:, ri, mm, :n], init,
                                              ALU.mult, ALU.add)
        last.then_inc(self.scanned, 1)
        dve.wait_ge(self.scanned, c + 1)
        if c:
            dve.wait_ge(self.yprod, c)
        if c == NCH:
            dve.wait_ge(self.fin_ready, 1)
        tt(at(h[:, 0], c), at(rot[:, 0], c), self.phase(0, c), ALU.mult)
        link(tt(at(h[:, 1], c), at(rot[:, 1], c), self.phase(1, c), ALU.mult))
        link(tt(h[:, 0, :, :n], h[:, 0, :, :n], h[:, 1, :, :n], ALU.subtract))
        dve.wait_ge(self.pout, 2 * (c + 1))
        tt(h[:, 1, :, :n], rot_p[:, 0, :, :n], rot_p[:, 1, :, :n], ALU.add).then_inc(self.h_ready, 1)
        dve.wait_ge(self.h_ready, c + 1)
        if c:
            self.y_out_of(dve, c - 1)


    def tensor(self, pe, u):
        m, M, rot = self.m, self.M, self.rot
        if u == 5:
            for ri in range(2):
                pe.wait_ge(self.bb_made, ri + 1)
                for mm in range(M):
                    last = pe.transpose(m.ps[:, 2 * ri + mm // 4, (mm % 4) * P:(mm % 4) * P + P], rot[:, ri, mm, :], m.ident[:])
                last.then_inc(self.bbT_turned, 1)
            pe.wait_ge(self.bbT_out, 2)
            pe.wait_ge(self.neg_made, 1)
            pe.wait_ge(self.u_out[0], 3)
            pe.wait_ge(self.u_out[1], 3)
            self.bu_products(pe, 0)
        c = (u - 6) // 2
        if u >= 6 and u % 2 == 0 and c + 1 < self.CH:
            self.bu_products(pe, c + 1)
        if u >= 7 and u % 2:
            self.y_products(pe, c)
        if u == 23:
            for g, (o, w) in enumerate(GROUPS_N):
                pe.wait_ge(self.gelu_made, g + 1)
                if g >= 2:
                    pe.wait_ge(self.sig_made, g - 1)
                for co in range(2):
                    for kt in range(2):
                        last = pe.matmul(m.ps[:, 2 * (g % 2) + co, :w], self.wglu[:, kt, co * P:co * P + P],
                                         self.gelu[:, kt, o:o + w], start=kt == 0, stop=kt == 1)
                last.then_inc(self.glu, 1)

    def bu_products(self, pe, c):
        n = self.W[c]
        if c:
            pe.wait_ge(self.bu_out, 2 * c)
        for ri in range(2):
            for mm in range(self.M):
                last = pe.matmul(self.m.ps[:, 2 * ri + mm // 4, (mm % 4) * P:(mm % 4) * P + n], self.bbT[:, ri, mm, :],
                                 self.m.uT[:, mm // 4, c * P:c * P + n], start=True, stop=True)
        last.then_inc(self.bu_prod, 1)

    def y_products(self, pe, c):
        n = self.W[c]
        pe.wait_ge(self.h_ready, c + 1)
        if c:
            pe.wait_ge(self.y_out, 2 * c)
        for ct in range(2):
            for i in range(8):
                mm, ri = 4 * ct + i // 2, i % 2
                last = pe.matmul(self.m.ps[:, 4, ct * P:ct * P + n], self.cpad[:, ri, mm, :], self.h[:, ri, mm, :n],
                                 start=i == 0, stop=i == 7)
        last.then_inc(self.yprod, 1)



def delta_net(nc, m):
    with ExitStack() as ctx:
        sb = lambda n, s: ctx.enter_context(nc.sbuf_tensor(f"dn_{n}", s, F32))
        sem = lambda n: m.sem(f"dn_{n}")
        H = 4
        NT = TILES
        flat_hT = m.mixT[:].rearrange("p k n -> p (k n)")
        conv, convs = m.mixT[:, 0:6, :], m.convs
        names = ["ones", "ones_s", "upto", "upto_s", "neg", "neg_s", "level", "seq_col", "seq_row"]
        C = {n: sb(n, [P, CONST_AT[n][1]]) for n in names}
        alog, dtb, normw = sb("alog", [P, H]), sb("dtb", [P, H]), sb("normw", [P, HD])
        minus_half = sb("minus_half", [P, NT * H])
        gate = sb("gate", [P, 12, NT, H])
        X, GG, BETA, GC, GL, NGC, EGC, EGL, EDEC, T0, T1, T2 = range(12)
        gm = sb("gm", [64, NB, H])
        egl_s = sb("egl_s", [P, NB, H])
        o_all = sb("o", [P, NT, 256])
        qk = sb("qk", [P, 2, 512])
        sq = sb("sq", [P, 512])
        ssq = sb("ssq", [P, 2, 8])
        rnorm = sb("rnorm", [P, 2, 8])
        kb, kbg, qg = sb("kb", [P, 256]), sb("kbg", [P, 2, 256]), sb("qg", [P, 256])
        kdec, vb = sb("kdec", [P, 2, 256]), sb("vb", [P, 2, 256])
        featT = sb("featT", [P, 2, 8, P])
        decay = sb("decay", [P, H, P])
        AT, aqkT = sb("AT", [P, 2, H, P]), sb("aqkT", [P, 2, H, P])
        B, U, T, TT = (sb(n, [P, 2, H, P]) for n in ("B", "U", "T", "TT"))
        wT = sb("wT", [P, 2, 2, P])
        S = sb("S", [P, 2, P])
        vnew = sb("vnew", [P, 256])

        pages = ctx.enter_context(nc.sbuf_tensor("pages", [1, NB * PAGES], I32))
        tables, params, pages_loaded = sem("tables"), sem("params"), sem("pages_loaded")
        vec, vec_pool, vec_act = sem("vec"), sem("vec_pool"), sem("vec_act")
        x_ready, ex_ready, lnin, ln_ready, g_ready = (sem(n) for n in ("x_ready", "ex_ready", "lnin", "ln_ready", "g_ready"))
        sums, sums_out, gexp = sem("sums"), sem("sums_out"), sem("gexp")
        raw, qk_out, vb_out = sem("raw"), sem("qk_out"), sem("vb_out")
        ssq_ready, rnorm_ready, normed = sem("ssq_ready"), sem("rnorm_ready"), sem("normed")
        scaled, turned, feat_out = sem("scaled"), sem("turned"), sem("feat_out")
        drow, decay_ready = sem("drow"), sem("decay_ready")
        gram, a_ready = sem("gram"), sem("a_ready")
        b_ready, bt, u_ready, tut, t_ready = sem("b_ready"), sem("bt"), sem("u_ready"), sem("tut"), sem("t_ready")
        wprod, w_ready = sem("wprod"), sem("w_ready")
        vprod, v_ready, oprod, o_out, sprod, s_ready = (sem(n) for n in ("vprod", "v_ready", "oprod", "o_out", "sprod", "s_ready"))
        s_zero, stored, s_in = sem("s_zero"), sem("stored"), sem("s_in")
        osq, orn, fin, fturn, fout, zsilu = (sem(n) for n in ("osq", "orn", "fin", "fturn", "fout", "zsilu"))
        masked, ss_ready = sem("masked"), sem("ss_ready")
        Ss = sb("Ss", [P, NB, 2, P])
        wTm = B[:].rearrange("p a h n -> p (a h n)").rearrange("p (c b n) -> p c b n", c=2, b=NB)
        qgm = U[:].rearrange("p a h n -> p (a h n)").rearrange("p (c b n) -> p c b n", c=2, b=NB)

        def kdecm(b):
            t = (AT if b < 4 else T)[:].rearrange("p a h n -> p (a h n)")
            return t[:64, (b % 4) * 256:(b % 4) * 256 + 256]

        def order(k, s):
            if k == TS:
                return TS * LEVELS + s + 1
            return (k // 2) * 2 * LEVELS + 2 * s + k % 2 + 1

        def order1(k, s):
            if k == TS:
                return TS * (LEVELS - 1) + s
            return (k // 2) * 2 * (LEVELS - 1) + 2 * (s - 1) + k % 2 + 1

        def pairs():
            return [(0, 1), (2, 3), (4, 5), (6, 7), (TS,)]

        def levels(k):
            return SLEVELS if k == TS else LEVELS

        def heads(t):
            return t.rearrange("p (h n) -> p h n", h=H)

        with nc.Block() as block:
            @block.sync
            def _(sp):
                sp.dma_start(alog[:], m.a_log).then_inc(params, 16)
                sp.dma_start(dtb[:], m.dt_bias).then_inc(params, 16)
                sp.dma_start(normw[:], m.norm_w).then_inc(params, 16)
                for n in names:
                    at, w = CONST_AT[n]
                    sp.dma_start(C[n][:], m.const[:, at:at + w]).then_inc(tables, 16)
                sp.dma_start(Ss[:], m.state_dn).then_inc(s_in, 16)
                caches_loaded = m.sem("caches_loaded")
                sp.dma_start(pages[:], m.a["page_table"]).then_inc(pages_loaded, 16)
                sp.wait_ge(pages_loaded, 16)
                for j in range(NB * PAGES):
                    page = sp.value_load(pages[0:1, j:j + 1], min_val=0, max_val=m.a["cache_nsa"].shape[0] - 1)
                    sp.dma_start(m.ck[:, j, :], m.a["cache_nsa"][bass.DynSlice(page, 1)].rearrange("a p n -> p (a n)")
                                 ).then_inc(caches_loaded, 16)
                sp.wait_ge(s_ready, TS)
                for h in range(2):
                    half = slice(64 * h, 64 * h + 64)
                    sp.dma_start(m.dn_prompt[half], S[half, :, half]).then_inc(stored, 16)
                sp.wait_ge(ss_ready, H)
                for h in range(2):
                    half = slice(64 * h, 64 * h + 64)
                    for c in range(2):
                        sp.dma_start(m.dn_sample[half, :, c], Ss[half, :, c, half]).then_inc(stored, 16)
                sp.wait_ge(stored, 16 * 6)
                sp.wait_ge(m.sem("proj_stored"), 16 * STORES_OF_INPUT)

            @block.gpsimd
            def _(pool):
                link = Link(pool, vec_pool)
                link(pool.memset(o_all[64:128, TS, :], 0.0))
                link(pool.memset(minus_half[:], -0.5))
                pool.memset(S[:], 0.0).then_inc(s_zero, 1)
                for pair in pairs():
                    for k in pair:
                        n, x = ROWS[k], k % 2
                        bc = lambda c: gate[:n, c, k, :].unsqueeze(2).to_broadcast([n, H, HD])
                        pool.wait_ge(ssq_ready, k + 1)
                        pool.tensor_tensor(rnorm[:n, x, :], ssq[:n, x, :], minus_half[:n, :8], ALU.pow).then_inc(rnorm_ready, 1)
                        pool.wait_ge(normed, k + 1)
                        pool.wait_ge(gexp, 3)
                        if k:
                            pool.wait_ge(turned, k)
                        kn = heads(qk[:n, x, 256:512])
                        pool.tensor_tensor(heads(kb[:n, :]), kn, bc(BETA), ALU.mult).then_inc(scaled, 1)
                        pool.tensor_tensor(heads(qg[:n, :]), heads(qk[:n, x, 0:256]), bc(EGC), ALU.mult).then_inc(scaled, 1)
                        if k >= 2:
                            pool.wait_ge(wprod, k - 1)
                            pool.wait_ge(sprod, k - 1)
                        pool.tensor_tensor(heads(kdec[:n, x, :]), kn, bc(EDEC), ALU.mult).then_inc(scaled, 1)
                        pool.wait_ge(scaled, 4 * k + 1)
                        pool.tensor_tensor(heads(kbg[:n, x, :]), heads(kb[:n, :]), bc(EGC), ALU.mult).then_inc(scaled, 1)
                    for s in range(levels(pair[0])):
                        for k in pair:
                            n, x = ROWS[k], k % 2
                            pool.wait_ge(a_ready, 4 * (k + 1))
                            if s:
                                pool.wait_ge(bt, order(k, s - 1))
                                pool.wait_ge(t_ready, order(k, s - 1))
                            mask = C["level"][:n, s * P:s * P + n].unsqueeze(1).to_broadcast([n, H, n])
                            pool.tensor_tensor(B[:n, x, :, :n], AT[:n, x, :, :n], mask, ALU.mult).then_inc(b_ready, 1)
                pool.wait_ge(osq, 1)
                pool.tensor_tensor(gate[:, T1].rearrange("p t h -> p (t h)"), gate[:, T0].rearrange("p t h -> p (t h)"),
                                   minus_half[:], ALU.pow).then_inc(orn, 1)

            @block.scalar
            def _(act):
                act.wait_ge(x_ready, 1)
                act.activation(gate[:, T1], gate[:, T0], ACT.Exp).then_inc(ex_ready, 1)
                act.activation(gate[:, T2], m.small[:, :, 28:32], ACT.Exp, scale=-1.0).then_inc(ex_ready, 1)
                act.activation(alog[:], alog[:], ACT.Exp).then_inc(ex_ready, 1)
                act.wait_ge(lnin, 1)
                act.activation(gate[:, T1], gate[:, T1], ACT.Ln, bias=1.0).then_inc(ln_ready, 1)
                act.wait_ge(sums_out, 1)
                act.activation(gate[:, EGC], gate[:, GC], ACT.Exp).then_inc(gexp, 1)
                act.activation(gate[:, EGL], gate[:, GL], ACT.Exp).then_inc(gexp, 1)
                act.activation(gate[:, EDEC], gate[:, T0], ACT.Exp).then_inc(gexp, 1)
                act.activation(egl_s[:], m.ps[:, 0, 128:160].rearrange("p (b h) -> p b h", b=NB), ACT.Exp).then_inc(gexp, 1)
                for pair in pairs():
                    for k in pair:
                        n, x = ROWS[k], k % 2
                        act.wait_ge(raw, k + 1)
                        if k:
                            act.wait_ge(ssq_ready, k)
                        if k >= 2:
                            act.wait_ge(scaled, 4 * (k - 1))
                            act.wait_ge(turned, k - 1)
                        act.activation(sq[:n, :], m.ps[:n, 4 * x, :], ACT.Square).then_inc(qk_out, 1)
                        act.activation(qk[:n, x, :], m.ps[:n, 4 * x, :], ACT.Copy).then_inc(qk_out, 1)
                        act.wait_ge(turned, k + 1)
                        if k >= 2:
                            act.wait_ge(oprod, k - 1)
                        for c in range(2):
                            act.activation(featT[:, x, 4 * c:4 * c + 4, :n],
                                           heads(m.ps[:, 4 * x + 2 + c, :])[:, :, :n], ACT.Copy).then_inc(feat_out, 1)
                        act.wait_ge(drow, k + 1)
                        if k:
                            act.wait_ge(a_ready, 4 * k)
                        for h in range(H):
                            act.activation(decay[:n, h, :n], m.ps[:n, 4 * x, h * P:h * P + n], ACT.Exp,
                                           bias=gate[:n, NGC, k, h:h + 1]).then_inc(decay_ready, 1)
                    for s in range(1, levels(pair[0])):
                        for k in pair:
                            n, x = ROWS[k], k % 2
                            act.wait_ge(bt, order(k, s))
                            if s > 1:
                                act.wait_ge(tut, order1(k, s - 1))
                            elif k >= 2:
                                act.wait_ge(tut, order1(k - 2, LEVELS - 1))
                            act.activation(U[:n, x, :, :n], heads(m.ps[:n, 4 * x, :])[:, :, :n], ACT.Copy).then_inc(u_ready, 1)
                    for k in pair:
                        n, x = ROWS[k], k % 2
                        act.wait_ge(wprod, k + 1)
                        for h in range(2):
                            act.activation(wT[64 * h:64 * h + 64, x, :, :n],
                                           heads(m.ps[64 * h:64 * h + 64, 4 * x, :])[:, h::2, :n],
                                           ACT.Copy, scale=-1.0).then_inc(w_ready, 1)
                        act.wait_ge(vprod, k + 1)
                        if k:
                            act.wait_ge(oprod, k)
                        act.activation(vnew[:n, :], m.ps[:n, 4 * x + 1, :256], ACT.Copy).then_inc(v_ready, 1)
                act.activation(m.small[:, :, 32:], m.small[:, :, 32:], ACT.Silu).then_inc(zsilu, 1)
                for k in range(NT):
                    act.wait_ge(fturn, k + 1)
                    act.activation(m.mixT[:, 4:6, k * P:k * P + ROWS[k]],
                                   heads(m.ps[:, k % 2, :])[:, 0:2, :ROWS[k]], ACT.Copy).then_inc(fout, 1)

            @block.vector
            def _(dve):
                link = Link(dve, vec)
                dve.wait_ge(params, 48)
                bcH = lambda t: t[:].unsqueeze(1).to_broadcast([P, NT, H])
                link(dve.tensor_tensor(gate[:, X], m.small[:, :, 24:28], bcH(dtb), ALU.add))
                link(dve.tensor_scalar(gate[:, T1], gate[:, X], -1.0, None, ALU.mult))
                dve.tensor_tensor(gate[:, T0], gate[:, X], gate[:, T1], ALU.min).then_inc(x_ready, 1)
                dve.wait_ge(ex_ready, 3)
                link(dve.tensor_scalar(gate[:, T2], gate[:, T2], 1.0, None, ALU.add))
                dve.reciprocal(gate[:, BETA], gate[:, T2]).then_inc(lnin, 1)
                dve.wait_ge(ln_ready, 1)
                link(dve.tensor_scalar(gate[:, X], gate[:, X], 0.0, None, ALU.max))
                link(dve.tensor_tensor(gate[:, X], gate[:, X], gate[:, T1], ALU.add))
                link(dve.tensor_tensor(gate[:, X], gate[:, X], bcH(alog), ALU.mult))
                link(dve.tensor_scalar(gate[:, GG], gate[:, X], -1.0, None, ALU.mult))
                dve.wait_ge(tables, 16 * len(names))
                dve.tensor_tensor(gm[:], gate[:64, GG, TS, :].unsqueeze(1).to_broadcast([64, NB, H]),
                                  C["seq_row"][:64, :].unsqueeze(2).to_broadcast([64, NB, H]), ALU.mult).then_inc(g_ready, 1)
                dve.wait_ge(sums, 1)
                link(dve.tensor_copy(gate[:, GC], m.ps[:, 0, 0:36].rearrange("p (t h) -> p t h", t=NT)))
                link(dve.tensor_copy(gate[:, GL], m.ps[:, 0, 64:100].rearrange("p (t h) -> p t h", t=NT)))
                link(dve.tensor_scalar(gate[:, NGC], gate[:, GC], -1.0, None, ALU.mult))
                dve.tensor_tensor(gate[:, T0], gate[:, GL], gate[:, GC], ALU.subtract).then_inc(sums_out, 1)
                for pair in pairs():
                    for k in pair:
                        n, x = ROWS[k], k % 2
                        dve.wait_ge(raw, k + 1)
                        if k >= 2:
                            dve.wait_ge(vprod, k - 1)
                        dve.tensor_tensor(heads(vb[:n, x, :]), heads(m.ps[:n, 4 * x + 1, 0:256]),
                                          gate[:n, BETA, k, :].unsqueeze(2).to_broadcast([n, H, HD]),
                                          ALU.mult).then_inc(vb_out, 1)
                        dve.wait_ge(qk_out, 2 * k + 2)
                        link(dve.tensor_reduce(ssq[:n, x, :], sq[:n, :].rearrange("p (h d) -> p h d", h=8), AX.X, ALU.add))
                        link(dve.tensor_scalar(ssq[:n, x, :], ssq[:n, x, :], 1e-6, None, ALU.add))
                        dve.tensor_scalar(ssq[:n, x, 0:4], ssq[:n, x, 0:4], 64.0, None, ALU.mult).then_inc(ssq_ready, 1)
                        dve.wait_ge(rnorm_ready, k + 1)
                        v = qk[:n, x, :].rearrange("p (h d) -> p h d", h=8)
                        dve.tensor_tensor(v, v, rnorm[:n, x, :].unsqueeze(2).to_broadcast([n, 8, HD]),
                                          ALU.mult).then_inc(normed, 1)
                        dve.wait_ge(gram, k + 1)
                        dve.wait_ge(decay_ready, 4 * (k + 1))
                        for h in range(2):
                            bank = heads(m.ps[:n, 4 * x + (1, 2)[h], :])
                            dve.tensor_tensor(AT[:n, x, h::2, :n], bank[:, 0:2, :n], decay[:n, h::2, :n], ALU.mult).then_inc(a_ready, 1)
                            dve.tensor_tensor(aqkT[:n, x, h::2, :n], bank[:, 2:4, :n], decay[:n, h::2, :n], ALU.mult).then_inc(a_ready, 1)
                    for s in range(levels(pair[0])):
                        for k in pair:
                            n, x = ROWS[k], k % 2
                            if s == 0:
                                eye = m.ident[:n, :n].unsqueeze(1).to_broadcast([n, H, n])
                                dve.wait_ge(b_ready, order(k, 0))
                                link(dve.tensor_tensor(TT[:n, x, :, :n], eye, B[:n, x, :, :n], ALU.subtract))
                                dve.wait_ge(bt, order(k, 0))
                                dve.tensor_tensor(T[:n, x, :, :n], eye, heads(m.ps[:n, 4 * x, :])[:, :, :n],
                                                  ALU.subtract).then_inc(t_ready, 1)
                                continue
                            dve.wait_ge(tut, order1(k, s))
                            if s < levels(k) - 1:
                                link(dve.tensor_tensor(T[:n, x, :, :n], T[:n, x, :, :n],
                                                       heads(m.ps[:n, 4 * x + 1, :])[:, :, :n], ALU.subtract))
                            dve.tensor_tensor(TT[:n, x, :, :n], TT[:n, x, :, :n],
                                              heads(m.ps[:n, 4 * x + 3, :])[:, :, :n], ALU.subtract).then_inc(t_ready, 1)
                    for k in pair:
                        if k == TS:
                            continue
                        x = k % 2
                        dve.wait_ge(sprod, k + 1)
                        for h in range(H):
                            half = slice(64 * (h % 2), 64 * (h % 2) + 64)
                            blk = S[half, h // 2, half]
                            last = dve.scalar_tensor_tensor(blk, blk, gate[half, EGL, k, h:h + 1],
                                                            m.ps[half, 4 * x + 3, (h // 2) * P + 64 * (h % 2):(h // 2) * P + 64 * (h % 2) + 64],
                                                            ALU.mult, ALU.add)
                        last.then_inc(s_ready, 1)
                        dve.wait_ge(oprod, k + 1)
                        dve.tensor_copy(o_all[:, k, :], m.ps[:, 4 * x + 2, :256]).then_inc(o_out, 1)
                n = NB * NQ
                dve.wait_ge(w_ready, 2 * NT)
                col = C["seq_col"][:].rearrange("p (b n) -> p b n", b=NB)
                for c in range(2):
                    dve.tensor_tensor(wTm[:, c], wT[:, 0, c, :n].unsqueeze(1).to_broadcast([P, NB, n]), col, ALU.mult)
                    dve.tensor_tensor(qgm[:, c], featT[:, 0, 6 + c, :n].unsqueeze(1).to_broadcast([P, NB, n]), col, ALU.mult)
                for b in range(NB):
                    last = dve.tensor_scalar(kdecm(b), kdec[:n, 0, :], C["seq_row"][:n, b:b + 1], None, ALU.mult)
                last.then_inc(masked, 1)
                dve.wait_ge(sprod, NT)
                for h in range(H):
                    half = slice(64 * (h % 2), 64 * (h % 2) + 64)
                    blk = Ss[half, :, h // 2, half]
                    link(dve.tensor_tensor(blk, blk, egl_s[half, :, h:h + 1].to_broadcast([64, NB, 64]), ALU.mult))
                    upd = m.ps[half, 4:8, :].rearrange("p a n -> p (a n)").rearrange("p (b c n) -> p b c n", b=NB, c=2)
                    dve.tensor_tensor(blk, blk, upd[:, :, h // 2, half], ALU.add).then_inc(ss_ready, 1)
                dve.wait_ge(oprod, NT)
                dve.tensor_copy(o_all[:n, TS, :], m.ps[:n, 2, :256]).then_inc(o_out, 1)
                dve.wait_ge(o_out, NT)
                dve.wait_ge(vec_pool, 2)
                flat = o_all[:].rearrange("p t (h d) -> p (t h) d", h=H)
                squares = flat_hT[:, :NT * 256]
                link(dve.tensor_tensor(squares, o_all[:].rearrange("p t n -> p (t n)"), o_all[:].rearrange("p t n -> p (t n)"), ALU.mult))
                link(dve.tensor_reduce(gate[:, T0].rearrange("p t h -> p (t h)"), squares.rearrange("p (a d) -> p a d", d=HD), AX.X, ALU.add))
                dve.tensor_scalar(gate[:, T0], gate[:, T0], 1.0 / HD, EPS, ALU.mult, ALU.add).then_inc(osq, 1)
                link(dve.tensor_tensor(flat, flat, normw[:].unsqueeze(1).to_broadcast([P, NT * H, HD]), ALU.mult))
                dve.wait_ge(orn, 1)
                link(dve.tensor_tensor(flat, flat, gate[:, T1].rearrange("p t h -> p (t h)").unsqueeze(2).to_broadcast([P, NT * H, HD]), ALU.mult))
                dve.wait_ge(zsilu, 1)
                dve.tensor_tensor(o_all[:], o_all[:], m.small[:, :, 32:], ALU.mult).then_inc(fin, 1)

            @block.tensor
            def _(pe):
                pe.wait_ge(tables, 16 * len(names))
                pe.wait_ge(g_ready, 1)
                g = gate[:, GG, 0:TS, :].rearrange("p t h -> p (t h)")
                bank = m.ps[:, 0, :]
                pe.matmul(bank[:, 0:32], C["upto"][:], g, start=True, stop=True)
                pe.matmul(bank[:, 32:36], C["upto_s"][:64, :], gate[:64, GG, TS, :], start=True, stop=True)
                pe.matmul(bank[:, 64:96], C["ones"][:], g, start=True, stop=True)
                pe.matmul(bank[:, 96:100], C["ones_s"][:64, :], gate[:64, GG, TS, :], start=True, stop=True)
                pe.matmul(bank[:, 128:160], C["ones"][:64, :], gm[:].rearrange("p b h -> p (b h)"),
                          start=True, stop=True).then_inc(sums, 1)
                pe.wait_ge(gexp, 4)
                for pair in pairs():
                    for k in pair:
                        n, x = ROWS[k], k % 2
                        if k >= 2:
                            pe.wait_ge(v_ready, k - 1)
                            pe.wait_ge(o_out, k - 1)
                            pe.wait_ge(s_ready, k - 1)
                            pe.wait_ge(w_ready, 2 * (k - 1))
                        for f in range(6):
                            if k < TS:
                                src = conv[:, f, k * P:(k + 1) * P]
                            else:
                                src = convs[:, f, :]
                            last = pe.transpose(m.ps[:n, 4 * x + f // 4, (f % 4) * P:(f % 4) * P + P], src, m.ident[:])
                        last.then_inc(raw, 1)
                        pe.wait_ge(normed, k + 1)
                        pe.wait_ge(scaled, 4 * k + 2)
                        for c, src in enumerate((qk[:n, x, 0:128], qk[:n, x, 128:256], qk[:n, x, 256:384], qk[:n, x, 384:512],
                                                 kb[:n, 0:128], kb[:n, 128:256], qg[:n, 0:128], qg[:n, 128:256])):
                            last = pe.transpose(m.ps[:, 4 * x + 2 + c // 4, (c % 4) * P:(c % 4) * P + n], src, m.ident[:n, :n])
                        last.then_inc(turned, 1)
                        pe.wait_ge(qk_out, 2 * k + 2)
                        for h in range(H):
                            row = m.ps[:n, 4 * x, h * P:h * P + n]
                            pe.matmul(row, gate[:n, GG, k, h:h + 1].to_broadcast([n, n]),
                                      C["upto" if k < TS else "upto_s"][:n, :n], start=True, stop=False)
                            last = pe.matmul(row, m.ident[:n, :n], C["neg" if k < TS else "neg_s"][:n, :n], start=False, stop=True)
                        last.then_inc(drow, 1)
                        pe.wait_ge(feat_out, 2 * k + 2)
                        pe.wait_ge(vb_out, k + 1)
                        for h in (0, 2, 1, 3):
                            half = slice(64 * (h % 2), 64 * (h % 2) + 64)
                            bank = m.ps[:n, 4 * x + (1, 2)[h % 2], :]
                            kT = featT[half, x, 2 + h // 2, :n]
                            pe.matmul(bank[:, (h // 2) * P:(h // 2) * P + n], kT, featT[half, x, 4 + h // 2, :n], start=True, stop=True)
                            last = pe.matmul(bank[:, (2 + h // 2) * P:(2 + h // 2) * P + n], kT, featT[half, x, h // 2, :n], start=True, stop=True)
                        last.then_inc(gram, 1)
                    for s in range(levels(pair[0])):
                        for k in pair:
                            n, x = ROWS[k], k % 2
                            pe.wait_ge(b_ready, order(k, s))
                            if s:
                                pe.wait_ge(t_ready, order(k, s - 1))
                            else:
                                pe.wait_ge(a_ready, 4 * (k + 1))
                                pe.wait_ge(decay_ready, 4 * (k + 1))
                            for h in range(H):
                                last = pe.matmul(m.ps[:n, 4 * x, h * P:h * P + n], B[:n, x, h, :n],
                                                 T[:n, x, h, :n] if s else m.ident[:n, :n], start=True, stop=True)
                            last.then_inc(bt, 1)
                        if s == 0:
                            continue
                        for k in pair:
                            n, x = ROWS[k], k % 2
                            pe.wait_ge(u_ready, order1(k, s))
                            for h in range(H):
                                if s < levels(k) - 1:
                                    pe.matmul(m.ps[:n, 4 * x + 1, h * P:h * P + n], TT[:n, x, h, :n], U[:n, x, h, :n], start=True, stop=True)
                                last = pe.matmul(m.ps[:n, 4 * x + 3, h * P:h * P + n], U[:n, x, h, :n], TT[:n, x, h, :n], start=True, stop=True)
                            last.then_inc(tut, 1)
                    for k in pair:
                        n, x = ROWS[k], k % 2
                        pe.wait_ge(t_ready, order(k, levels(k) - 1))
                        pe.wait_ge(scaled, 4 * k + 4)
                        for h in range(H):
                            last = pe.matmul(m.ps[:, 4 * x, h * P:h * P + n], kbg[:n, x, (h // 2) * P:(h // 2) * P + P],
                                             TT[:n, x, h, :n], start=True, stop=True)
                        last.then_inc(wprod, 1)
                        if k == TS:
                            n = NB * NQ
                            vbank, obank = m.ps[:n, 1, :], m.ps[:n, 2, :]
                            pe.wait_ge(masked, 1)
                            pe.wait_ge(s_in, 16)
                            for h in range(H):
                                pe.matmul(vbank[:, h * HD:(h + 1) * HD], TT[:n, x, h, :n], vb[:n, x, h * HD:(h + 1) * HD],
                                          start=h == 0, stop=False, skip_group_check=True)
                            for b in range(NB):
                                for c in range(2):
                                    last = pe.matmul(vbank[:, c * P:(c + 1) * P], wTm[:, c, b, :], Ss[:, b, c, :],
                                                     start=False, stop=b == NB - 1, skip_group_check=True)
                            last.then_inc(vprod, 1)
                            for b in range(NB):
                                for c in range(2):
                                    pe.matmul(obank[:, c * P:(c + 1) * P], qgm[:, c, b, :], Ss[:, b, c, :],
                                              start=b + c == 0, stop=False, skip_group_check=True)
                            pe.wait_ge(v_ready, NT)
                            pe.wait_ge(v_ready, TS)
                            pe.wait_ge(o_out, TS)
                            pe.wait_ge(s_ready, TS)
                            for b in range(NB):
                                for c in range(2):
                                    last = pe.matmul(m.ps[:, 4 + b // 2, (b % 2) * 256 + c * P:(b % 2) * 256 + (c + 1) * P],
                                                     kdecm(b)[:, c * P:(c + 1) * P], vnew[:n, c * P:(c + 1) * P],
                                                     start=True, stop=True)
                            last.then_inc(sprod, 1)
                            for h in range(H):
                                last = pe.matmul(obank[:, h * HD:(h + 1) * HD], aqkT[:n, x, h, :n], vnew[:n, h * HD:(h + 1) * HD],
                                                 start=False, stop=h == 3, skip_group_check=True)
                            last.then_inc(oprod, 1)
                            continue
                        pe.wait_ge(w_ready, 2 * (k + 1))
                        if k:
                            pe.wait_ge(s_ready, k)
                        else:
                            pe.wait_ge(s_zero, 1)
                        vbank, obank, sbank = (m.ps[:, 4 * x + c, :] for c in (1, 2, 3))
                        for h in range(H):
                            pe.matmul(vbank[:, h * HD:(h + 1) * HD], TT[:, x, h, :], vb[:, x, h * HD:(h + 1) * HD],
                                      start=h == 0, stop=False, skip_group_check=True)
                        for c in range(2):
                            last = pe.matmul(vbank[:, c * P:(c + 1) * P], wT[:, x, c, :], S[:, c, :],
                                             start=False, stop=c == 1, skip_group_check=True)
                        last.then_inc(vprod, 1)
                        for c in range(2):
                            pe.matmul(obank[:, c * P:(c + 1) * P], featT[:, x, 6 + c, :], S[:, c, :],
                                      start=c == 0, stop=False, skip_group_check=True)
                        pe.wait_ge(v_ready, k + 1)
                        for c in range(2):
                            last = pe.matmul(sbank[:, c * P:(c + 1) * P], kdec[:, x, c * P:(c + 1) * P],
                                             vnew[:, c * P:(c + 1) * P], start=True, stop=True)
                        last.then_inc(sprod, 1)
                        for h in range(H):
                            last = pe.matmul(obank[:, h * HD:(h + 1) * HD], aqkT[:, x, h, :], vnew[:, h * HD:(h + 1) * HD],
                                             start=False, stop=h == 3, skip_group_check=True)
                        last.then_inc(oprod, 1)
                pe.wait_ge(fin, 1)
                for k in range(NT):
                    if k >= 2:
                        pe.wait_ge(fout, k - 1)
                    for c in range(2):
                        last = pe.transpose(m.ps[:, k % 2, c * P:c * P + ROWS[k]], o_all[:ROWS[k], k, c * P:(c + 1) * P],
                                            m.ident[:ROWS[k], :ROWS[k]])
                    last.then_inc(fturn, 1)



def key_prep(nc, m, held):
    hold = lambda n, s: held.enter_context(nc.sbuf_tensor(n, s, F32))
    m.kselT, m.kwinT = hold("kselT", [P, TOK]), hold("kwinT", [P, TOK])
    m.kcT, m.vc = hold("kcT", [P, 16]), hold("vc", [16, P])
    m.wck, m.wcv = hold("wck", [P, 4]), hold("wcv", [P, 2, 62])
    with ExitStack() as ctx:
        sb = lambda n, s: ctx.enter_context(nc.sbuf_tensor(f"prep_{n}", s, F32))
        sem = lambda n: m.sem(f"prep_{n}")
        loaded, turned, pooled, out, gates = sem("loaded"), sem("turned"), sem("pooled"), sem("out"), sem("gates")
        jobs = [(KSEL, m.kselT, (0, 1, 2, 3)), (KSEL, m.kselT, (4, 5, 6, 7)),
                (KWIN, m.kwinT, (0, 1, 2, 3)), (KWIN, m.kwinT, (4, 5, 6, 7))]
        with nc.Block() as block:
            @block.sync
            def _(sp):
                sp.dma_start(m.wck[:], m.a["wck"]).then_inc(loaded, 16)
                sp.dma_start(m.wcv[:], m.a["wcv"]).then_inc(loaded, 16)
                sp.dma_start(m.cw[:], m.cache_win.rearrange("b (a p) n -> p (b a) n", p=P)).then_inc(m.sem("caches_loaded"), 16)
                sp.wait_ge(loaded, 32)

            @block.tensor
            def _(pe):
                for j, (col, _, tiles) in enumerate(jobs):
                    for c, t in enumerate(tiles):
                        last = pe.transpose(m.ps[:, j, c * P:(c + 1) * P], m.kv[:, t, col:col + P], m.ident[:])
                    last.then_inc(turned, 1)
                for c, col in enumerate((KSEL, KWIN)):
                    last = pe.transpose(m.ps[:, 4, c * P:c * P + 64], m.kv[:64, TS, col:col + P], m.ident[:64, :64])
                last.then_inc(turned, 1)
                pe.wait_ge(loaded, 32)
                for t in range(TS):
                    pe.matmul(m.ps[:, 5, 4 * t:4 * t + 4], m.kv[:, t, KCMP:KCMP + P], m.wck[:], start=True, stop=True)
                for g in range(G):
                    for t in range(TS):
                        last = pe.matmul(m.ps[:16, 6, g * HD:(g + 1) * HD], m.wcv[:, g, 30 - 2 * t:46 - 2 * t],
                                         m.kv[:, t, VCMP + g * HD:VCMP + (g + 1) * HD], start=t == 0, stop=t == TS - 1)
                last.then_inc(pooled, 1)

            @block.scalar
            def _(act):
                act.activation(m.small[:, :, 0:24], m.small[:, :, 0:24], ACT.Sigmoid).then_inc(gates, 1)
                for j, (_, dst, tiles) in enumerate(jobs):
                    act.wait_ge(turned, j + 1)
                    act.activation(dst[:, tiles[0] * P:tiles[0] * P + 512], m.ps[:, j, :], ACT.Copy).then_inc(out, 1)

            @block.vector
            def _(dve):
                dve.wait_ge(turned, 5)
                for c, dst in enumerate((m.kselT, m.kwinT)):
                    dve.tensor_copy(dst[:, SEQ:TOK], m.ps[:, 4, c * P:c * P + 64]).then_inc(out, 1)
                dve.wait_ge(pooled, 1)
                for g in range(G):
                    half = slice(64 * g, 64 * g + 64)
                    src = m.ps[half, 5, 0:32].rearrange("p (t g b) -> p t g b", t=TS, g=G)[:, :, g, :]
                    dve.tensor_copy(m.kcT[half, :].rearrange("p (t b) -> p t b", t=TS), src).then_inc(out, 1)
                dve.tensor_copy(m.vc[:], m.ps[:16, 6, 0:P]).then_inc(out, 1)


def prompt_attention(nc, m):
    with ExitStack() as ctx:
        sb = lambda n, s: ctx.enter_context(nc.sbuf_tensor(f"pa_{n}", s, F32))
        sem = lambda n: m.sem(f"pa_{n}")
        SLOTS = 8
        WIN_AT, CMP_AT, WIDTH = SEQ, SEQ + 640, SEQ + 640 + 16
        probs = sb("probs", [P, SLOTS, WIDTH])
        dsel, dwin, dcmp = sb("dsel", [P, 1024]), sb("dwin", [P, 640]), sb("dcmp", [P, 128])
        mx, nm, rs, fac = (sb(n, [P, SLOTS, 3]) for n in ("mx", "nm", "rs", "fac"))
        PTN = 4
        PT = sb("PT", [P, PTN, 512])
        (loaded, score_ready, score_out, nm_ready, exp_done, scaled, turned, pt_ready, pv_step, o_out, vec) = (
            sem(n) for n in ("loaded", "score_ready", "score_out", "nm_ready", "exp_done", "scaled", "turned",
                             "pt_ready", "pv_step", "o_out", "vec"))
        units = [(i, g) for i in range(TS) for g in range(G)]
        RING = 4

        def window(i):
            f = max(0, i - WINDOW // P)
            return f, i - f + 1

        def pieces(i):
            out = [(o, min(512, (i + 1) * P - o), m.kselT, o, dsel[:, 1024 - (i + 1) * P + o:])
                   for o in range(0, (i + 1) * P, 512)]
            f, nw = window(i)
            out += [(WIN_AT + o, min(512, nw * P - o), m.kwinT, f * P + o, dwin[:, (f - i) * P + 512 + o:])
                    for o in range(0, nw * P, 512)]
            return out + [(CMP_AT, 16, m.kcT, 0, dcmp[:, 16 * i:])]

        def branches(i):
            return [(0, (i + 1) * P), (WIN_AT, window(i)[1] * P), (CMP_AT, 16)]

        def steps(n):
            i, g = units[n]
            f, nw = window(i)
            v = slice(g * HD, (g + 1) * HD)
            out = [(P * t, P, m.kv[:, t, VSEL:VSEL + P][:, v]) for t in range(i + 1)]
            out += [(WIN_AT + P * t, P, m.kv[:, f + t, VWIN:VWIN + P][:, v]) for t in range(nw)]
            return out + [(CMP_AT, 16, m.vc[:, v])]

        first_step = [0]
        for n in range(len(units)):
            first_step.append(first_step[-1] + len(steps(n)))

        def part(n, r):
            k = len(steps(n))
            return range(k * r // R, k * (r + 1) // R)

        with nc.Block() as block:
            @block.sync
            def _(sp):
                for name, dst in (("dist_sel", dsel), ("dist_win", dwin), ("dist_cmp", dcmp)):
                    at, w = CONST_AT[name]
                    sp.dma_start(dst[:], m.const[:, at:at + w]).then_inc(loaded, 16)
                sp.dma_start(m.out_raw[0][:], m.a["w_out"][0]).then_inc(m.out_raw[1], 16)

            @block.tensor
            def _(pe):
                count = [0]

                def scores(n, r):
                    i, g = units[n]
                    half = slice(64 * g, 64 * g + 64)
                    for _, w, keys, k0, _ in pieces(i):
                        c = count[0]
                        if c >= RING:
                            pe.wait_ge(score_out, c - RING + 1)
                        pe.matmul(m.ps[:, c % RING, :w], m.qT[half, r, i * P:(i + 1) * P], keys[half, k0:k0 + w],
                                  start=True, stop=True).then_inc(score_ready, 1)
                        count[0] += 1

                def multiply(n, s):
                    st = first_step[n] + s
                    _, k, values = steps(n)[s]
                    half = slice(64 * units[n][1], 64 * units[n][1] + 64)
                    if s == 0 and n >= 2:
                        pe.wait_ge(o_out, n - 1)
                    pe.wait_ge(pt_ready, st + 1)
                    pe.matmul(m.ps[half, 6 + n % 2, :], values, PT[:k, st % PTN, :], start=s == 0,
                              stop=s == len(steps(n)) - 1).then_inc(pv_step, 1)

                def turn(n, r):
                    if r == 0:
                        pe.wait_ge(scaled, R * (n + 1))
                    for s in part(n, r):
                        col, k, _ = steps(n)[s]
                        st = first_step[n] + s
                        if st >= 2:
                            pe.wait_ge(pt_ready, st - 1)
                        for h in range(R):
                            last = pe.transpose(m.ps[:k, 4 + st % 2, h * P:(h + 1) * P],
                                                probs[:, (R * n + h) % SLOTS, col:col + k], m.ident[:])
                        last.then_inc(turned, 1)
                        if s:
                            multiply(n, s - 1)
                    if r == R - 1:
                        multiply(n, len(steps(n)) - 1)

                pe.wait_ge(loaded, 48)
                for n in range(len(units) + 1):
                    for r in range(R):
                        if n < len(units):
                            scores(n, r)
                        if n:
                            turn(n - 1, r)

            @block.vector
            def _(dve):
                link = Link(dve, vec)
                count = [0]
                dve.wait_ge(loaded, 48)

                def rows(e):
                    n, r = e // R, e % R
                    i, g = units[n]
                    x = e % SLOTS
                    if n >= 2 and r == 0:
                        dve.wait_ge(turned, first_step[n - 1])
                    for col, w, _, _, table in pieces(i):
                        dve.wait_ge(score_ready, count[0] + 1)
                        last = dve.scalar_tensor_tensor(probs[:, x, col:col + w], table[:, :w], 2.0 ** -(4 * g + r + 1),
                                                        m.ps[:, count[0] % RING, :w], ALU.mult, ALU.add)
                        last.then_inc(score_out, 1)
                        count[0] += 1
                    dve.wait_ge(score_out, count[0])
                    for b, (o, w) in enumerate(branches(i)):
                        last = dve.tensor_reduce(mx[:, x, b:b + 1], probs[:, x, o:o + w], AX.X, ALU.max)
                    link(last)
                    dve.tensor_scalar(nm[:, x, :], mx[:, x, :], MFLOOR, -1.0, ALU.max, ALU.mult).then_inc(nm_ready, 1)

                def scale(e):
                    n, r = e // R, e % R
                    i, g = units[n]
                    x = e % SLOTS
                    dve.wait_ge(exp_done, e + 1)
                    link(dve.tensor_scalar(rs[:, x, :], rs[:, x, :], 1e-30, None, ALU.max))
                    link(dve.reciprocal(fac[:, x, :], rs[:, x, :]))
                    h = 4 * g + r
                    link(dve.tensor_tensor(fac[:, x, 0:2], fac[:, x, 0:2], m.small[:, i, 3 * h + 1:3 * h + 3], ALU.mult))
                    link(dve.tensor_tensor(fac[:, x, 2:3], fac[:, x, 2:3], m.small[:, i, 3 * h:3 * h + 1], ALU.mult))
                    for b, (o, w) in enumerate(branches(i)):
                        last = dve.tensor_scalar(probs[:, x, o:o + w], probs[:, x, o:o + w], fac[:, x, b:b + 1], None, ALU.mult)
                    last.then_inc(scaled, 1)

                E = R * len(units)
                for e in range(E + 1):
                    if e < E:
                        rows(e)
                    if e:
                        scale(e - 1)

            @block.scalar
            def _(act):
                def exps(e):
                    i, _ = units[e // R]
                    x = e % SLOTS
                    act.wait_ge(nm_ready, e + 1)
                    for b, (o, w) in enumerate(branches(i)):
                        last = act.activation(probs[:, x, o:o + w], probs[:, x, o:o + w], ACT.Exp, bias=nm[:, x, b:b + 1],
                                              accum_out=rs[:, x, b:b + 1])
                    last.then_inc(exp_done, 1)

                def copies(n, r):
                    for s in part(n, r):
                        st = first_step[n] + s
                        k = steps(n)[s][1]
                        act.wait_ge(turned, st + 1)
                        if st >= PTN:
                            act.wait_ge(pv_step, st - PTN + 1)
                        act.activation(PT[:k, st % PTN, :], m.ps[:k, 4 + st % 2, :], ACT.Copy).then_inc(pt_ready, 1)
                    if r == R - 1:
                        i, g = units[n]
                        half = slice(64 * g, 64 * g + 64)
                        act.wait_ge(pv_step, first_step[n + 1])
                        act.activation(m.mixT[half, 0:4, i * P:(i + 1) * P],
                                       m.ps[half, 6 + n % 2, :].rearrange("p (h n) -> p h n", h=R), ACT.Copy).then_inc(o_out, 1)

                for n in range(len(units) + 1):
                    for r in range(R):
                        if n:
                            copies(n - 1, r)
                        if n < len(units):
                            exps(R * n + r)


def sample_attention(nc, m):
    with ExitStack() as ctx:
        sb = lambda n, s: ctx.enter_context(nc.sbuf_tensor(f"sa_{n}", s, F32))
        sem = lambda n: m.sem(f"sa_{n}")
        ck, cw = m.ck, m.cw
        kT = sb("kT", [P, 2, NB * PAGES * P])
        dist, dcmp, slope = sb("dist", [P, 2, 320]), sb("dcmp", [P, 2, 32]), sb("slope", [P, 2])
        gsel = sb("gsel", [P, 2, R, P])
        qS = sb("qS", [P, NB, R, NQ])
        kcT, vc = sb("kcT", [P, 32]), sb("vc", [32, P])
        gates = sb("gates", [P, 2, 6])
        NEW = 64
        WIDTH = 2 * (PAST + NEW) + 32
        probs = sb("probs", [P, WIDTH])
        mx, nm, rs, fac = (sb(n, [P, 4, 3]) for n in ("mx", "nm", "rs", "fac"))
        PT = sb("PT", [P, 7, P])
        BR = [(0, PAST + NEW), (PAST + NEW, PAST + NEW), (2 * (PAST + NEW), 32)]
        items = [(g, h) for h in range(2) for g in range(G)]
        (consts, turned, t_out, pooled, pool_out, gate_prod, gate_out, sc, sc_out, nm_ready, exp_done,
         scaled, p_turned, p_out, pv, o_out, vec, q_out) = (sem(n) for n in (
             "consts", "turned", "t_out", "pooled", "pool_out", "gate_prod", "gate_out", "sc", "sc_out",
             "nm_ready", "exp_done", "scaled", "p_turned", "p_out", "pv", "o_out", "vec", "q_out"))
        jobs = [(which, j) for which in range(2) for j in range(4)]
        with nc.Block() as block:
            @block.sync
            def _(sp):
                for name, dst in (("sdist", dist[:].rearrange("p h n -> p (h n)")), ("sdist_cmp", dcmp[:].rearrange("p h n -> p (h n)")),
                                  ("sslope", slope[:]), ("gate_sel", gsel[:].rearrange("p h r n -> p (h r n)"))):
                    at, w = CONST_AT[name]
                    sp.dma_start(dst, m.const[:, at:at + w]).then_inc(consts, 16)

            @block.tensor
            def _(pe):
                pe.wait_ge(m.sem("caches_loaded"), 16 * (NB * PAGES + 1))
                pe.wait_ge(consts, 64)
                for j, (which, a) in enumerate(jobs):
                    if j >= 4:
                        pe.wait_ge(t_out, j - 3)
                    for c in range(4):
                        src = ck[:, 4 * a + c, 256:384] if which == 0 else cw[:, 4 * a + c, 0:128]
                        last = pe.transpose(m.ps[:, j % 4, c * P:(c + 1) * P], src, m.ident[:])
                    last.then_inc(turned, 1)
                for j in range(16):
                    pe.matmul(m.ps[:, 4, 4 * j:4 * j + 4], ck[:, j, 0:128], m.wck[:], start=True, stop=True)
                for g in range(G):
                    for j in range(16):
                        last = pe.matmul(m.ps[:32, 5, g * HD:(g + 1) * HD], m.wcv[:, g, 30 - 2 * j:62 - 2 * j],
                                         ck[:, j, 128 + g * HD:128 + (g + 1) * HD], start=j == 0, stop=j == 15)
                last.then_inc(pooled, 1)
                gt = m.small[:64, TS, 0:24].rearrange("p (g r c) -> p g r c", g=G, r=R)
                for h in range(2):
                    for r in range(R):
                        last = pe.matmul(m.ps[:, 6 + h, 0:6], gsel[:64, h, r, :], gt[:, :, r, :], start=r == 0, stop=r == R - 1)
                last.then_inc(gate_prod, 1)
                pe.wait_ge(t_out, 8)
                pe.wait_ge(q_out, R)
                pe.wait_ge(pool_out, 3)
                pe.wait_ge(gate_out, 1)
                for it, (g, h) in enumerate(items):
                    half = slice(64 * g, 64 * g + 64)
                    if it:
                        pe.wait_ge(sc_out, it)
                    for b in range(4):
                        rows = slice(32 * b, 32 * b + 32)
                        seq = 4 * h + b
                        q = qS[half, seq].rearrange("p r q -> p (r q)")
                        pe.matmul(m.ps[rows, 0, 0:PAST], q, kT[half, 0, seq * PAST:(seq + 1) * PAST], start=True, stop=True)
                        pe.matmul(m.ps[rows, 0, PAST:PAST + NEW], q, m.kselT[half, SEQ:TOK], start=True, stop=True)
                        pe.matmul(m.ps[rows, 1, 0:PAST], q, kT[half, 1, seq * PAST:(seq + 1) * PAST], start=True, stop=True)
                        pe.matmul(m.ps[rows, 1, PAST:PAST + NEW], q, m.kwinT[half, SEQ:TOK], start=True, stop=True)
                        last = pe.matmul(m.ps[rows, 2, 0:32], q, kcT[half, :], start=True, stop=True)
                    last.then_inc(sc, 1)
                    pe.wait_ge(scaled, it + 1)
                    if it:
                        pe.wait_ge(p_out, 3 * it)
                    for c, o in enumerate((0, P, 320, 320 + P)):
                        pe.transpose(m.ps[:, 6, c * P:(c + 1) * P], probs[:, o:o + P], m.ident[:])
                    for c, o in enumerate((PAST, 320 + PAST)):
                        pe.transpose(m.ps[:64, 7, c * P:(c + 1) * P], probs[:, o:o + NEW], m.ident[:])
                    pe.transpose(m.ps[:32, 7, 2 * P:3 * P], probs[:, 640:672], m.ident[:]).then_inc(p_turned, 1)
                    pe.wait_ge(p_out, 3 * (it + 1))
                    if it >= 2:
                        pe.wait_ge(o_out, it - 1)
                    acc = m.ps[half, 3 + it % 2, 0:P]
                    v = lambda t: t[:, g * HD:(g + 1) * HD]
                    args = dict(stop=False, skip_group_check=True)
                    pe.matmul(acc, v(m.kv[:64, TS, VSEL:VSEL + P]), PT[:64, 4, :], start=True, **args)
                    pe.matmul(acc, v(m.kv[:64, TS, VWIN:VWIN + P]), PT[:64, 5, :], start=False, **args)
                    pe.matmul(acc, v(vc[:, :]), PT[:32, 6, :], start=False, **args)
                    for b in range(4):
                        rows = slice(32 * b, 32 * b + 32)
                        for a in range(PAGES):
                            j = (4 * h + b) * PAGES + a
                            pe.matmul(acc[:, rows], v(ck[:, j, 384:512]), PT[:, a, rows], start=False, **args)
                            last = pe.matmul(acc[:, rows], v(cw[:, j, 128:256]), PT[:, 2 + a, rows], start=False,
                                             stop=b == 3 and a == 1, skip_group_check=True)
                    last.then_inc(pv, 1)

            @block.scalar
            def _(act):
                for r in range(R):
                    act.activation(qS[:, :, r, :], m.qT[:, r, SEQ:TOK].rearrange("p (b q) -> p b q", b=NB),
                                   ACT.Copy).then_inc(q_out, 1)
                for j, (which, a) in enumerate(jobs):
                    act.wait_ge(turned, j + 1)
                    act.activation(kT[:, which, 512 * a:512 * a + 512], m.ps[:, j % 4, :], ACT.Copy).then_inc(t_out, 1)
                for it, (g, h) in enumerate(items):
                    act.wait_ge(nm_ready, it + 1)
                    for b, (o, w) in enumerate(BR):
                        last = act.activation(probs[:, o:o + w], probs[:, o:o + w], ACT.Exp, bias=nm[:, it, b:b + 1],
                                              accum_out=rs[:, it, b:b + 1])
                    last.then_inc(exp_done, 1)
                    act.wait_ge(p_turned, it + 1)
                    if it:
                        act.wait_ge(pv, it)
                    act.activation(PT[:, 0:4, :], m.ps[:, 6, :].rearrange("p (c n) -> p c n", c=4), ACT.Copy).then_inc(p_out, 1)
                    act.activation(PT[:64, 4:6, :], m.ps[:64, 7, 0:256].rearrange("p (c n) -> p c n", c=2), ACT.Copy).then_inc(p_out, 1)
                    act.activation(PT[:32, 6, :], m.ps[:32, 7, 256:384], ACT.Copy).then_inc(p_out, 1)
                    act.wait_ge(pv, it + 1)
                    half = slice(64 * g, 64 * g + 64)
                    dst = m.mixT[half, 0:4, SEQ + 32 * h:SEQ + 32 * h + 32].rearrange("p r (b q) -> p r b q", b=4)
                    src = m.ps[half, 3 + it % 2, 0:P].rearrange("p (b r q) -> p r b q", b=4, r=R)
                    for r in range(R):
                        last = act.activation(dst[:, r], src[:, r], ACT.Copy)
                    last.then_inc(o_out, 1)

            @block.vector
            def _(dve):
                link = Link(dve, vec)
                dve.wait_ge(pooled, 1)
                for g in range(G):
                    half = slice(64 * g, 64 * g + 64)
                    src = m.ps[half, 4, 0:64].rearrange("p (j g b) -> p j g b", j=16, g=G)[:, :, g, :]
                    dve.tensor_copy(kcT[half, :].rearrange("p (j b) -> p j b", j=16), src).then_inc(pool_out, 1)
                dve.tensor_copy(vc[:], m.ps[:32, 5, 0:P]).then_inc(pool_out, 1)
                dve.wait_ge(gate_prod, 1)
                dve.tensor_copy(gates[:], m.ps[:, 6:8, 0:6]).then_inc(gate_out, 1)
                dve.wait_ge(gate_out, 1)
                dve.wait_ge(consts, 64)
                for it, (g, h) in enumerate(items):
                    dve.wait_ge(sc, it + 1)
                    if it:
                        dve.wait_ge(p_turned, it)
                    for b, (o, w) in enumerate(BR):
                        table = dist[:, h, :] if b < 2 else dcmp[:, h, :]
                        last = dve.scalar_tensor_tensor(probs[:, o:o + w], table, slope[:, g:g + 1], m.ps[:, b, 0:w],
                                                        ALU.mult, ALU.add)
                    last.then_inc(sc_out, 1)
                    dve.wait_ge(sc_out, it + 1)
                    for b, (o, w) in enumerate(BR):
                        last = dve.tensor_reduce(mx[:, it, b:b + 1], probs[:, o:o + w], AX.X, ALU.max)
                    link(last)
                    dve.tensor_scalar(nm[:, it, :], mx[:, it, :], MFLOOR, -1.0, ALU.max, ALU.mult).then_inc(nm_ready, 1)
                    dve.wait_ge(exp_done, it + 1)
                    link(dve.tensor_scalar(rs[:, it, :], rs[:, it, :], 1e-30, None, ALU.max))
                    link(dve.reciprocal(fac[:, it, :], rs[:, it, :]))
                    for b, c in enumerate((1, 2, 0)):
                        last = dve.tensor_tensor(fac[:, it, b:b + 1], fac[:, it, b:b + 1], gates[:, h, 3 * g + c:3 * g + c + 1], ALU.mult)
                    link(last)
                    for b, (o, w) in enumerate(BR):
                        last = dve.tensor_scalar(probs[:, o:o + w], probs[:, o:o + w], fac[:, it, b:b + 1], None, ALU.mult)
                    last.then_inc(scaled, 1)



def output_projection(nc, m):
    with ExitStack() as ctx:
        sb = lambda n, s, dt=F32: ctx.enter_context(nc.sbuf_tensor(f"out_{n}_sb", s, dt))
        sem = lambda n: m.sem(f"out_{n}")
        mix2 = [sb(n, [P, KT, PADT], F32R) for n in ("mix_hi", "mix_lo")]
        units = [(c, t) for c in range(OUT_CHUNKS) for t in range(TILES)]
        width = D // OUT_CHUNKS
        mix_hi, mix_lo, padded = sem("mix_hi"), sem("mix_lo"), sem("padded")
        x_loaded = [sem(f"x_loaded{t}") for t in range(TILES)]

        def load_x(sp, _):
            for t in range(TILES):
                src = m.x_prompt[t * P:(t + 1) * P, :] if t < TS else m.x_sample
                sp.dma_start(m.x2[:ROWS[t], t, :], src).then_inc(x_loaded[t], 16)

        def load_mlp(sp, evac):
            sp.wait_ge(evac[1], TILES * (OUT_CHUNKS - 1) + 1)
            sp.dma_start(m.out_raw[0][:], m.a["w_up"][0].rearrange("p a n -> p (a n)")).then_inc(m.sem("mlp_up_loaded"), 16)

        def pad(pool, _):
            for part in mix2:
                pool.memset(part[:, :, TOK:].bitcast(F32), 0.0).then_inc(padded, 1)

        def round_mix(act, _):
            for t in range(TILES):
                n = ROWS[t]
                act.activation(mix2[0][:, :, t * P:t * P + n], m.mixT[:, :, t * P:t * P + n], ACT.Copy).then_inc(mix_hi, 1)

        def rest_of_mix(dve, t):
            n = ROWS[t]
            dve.wait_ge(mix_hi, t + 1)
            dve.tensor_tensor(mix2[1][:, :, t * P:t * P + n], m.mixT[:, :, t * P:t * P + n],
                              mix2[0][:, :, t * P:t * P + n], ALU.subtract).then_inc(mix_lo, 1)

        def wait_for_mix(pe, t):
            pe.wait_ge(mix_lo, t + 1)
            if t == TS:
                pe.wait_ge(padded, 2)

        def first_rests(dve, _):
            for t in range(2):
                rest_of_mix(dve, t)

        def vector(dve, u):
            if u + 2 < TILES:
                rest_of_mix(dve, u + 2)

        def tensor(pe, u):
            if u + 1 < TILES:
                wait_for_mix(pe, u + 1)

        def evacuation(dve, _, u):
            c, t = units[u]
            n = ROWS[t]
            if c == 0:
                dve.wait_ge(x_loaded[t], 16)
            part = m.x2[:n, t, width * c:width * (c + 1)]
            return dve.tensor_tensor(part, part, m.ps[:n, u % 8, :width], ALU.add)

        m.hT2 = mix2
        project(nc, m, "op", [m.a["w_out"][c] for c in range(OUT_CHUNKS)], [width] * OUT_CHUNKS, units, evacuation, False,
                side={"sync_first": load_x, "sync": load_mlp, "gpsimd": pad, "scalar_first": round_mix, "vector_first": first_rests,
                      "vector": vector, "tensor_first": lambda pe, _: wait_for_mix(pe, 0), "tensor": tensor},
                preload=m.out_raw, out_by_dve=True)


def mlp_products(nc, m):
    with ExitStack() as ctx:
        sb = lambda n, s, dt=F32R: ctx.enter_context(nc.sbuf_tensor(f"mlp_{n}", s, dt))
        sem = lambda n: m.sem(f"mlp_{n}")
        NG, FT = FF // FG, FG // P
        KINDS = ("up", "down")
        WN = KT * FG
        assert WN == FT * D
        assert KT * D // OUT_CHUNKS == WN
        raw = {"up": m.out_raw[0], "down": sb("raw_down", [P, WN], F32)}
        hi = {k: sb("hi_" + k, [P, WN]) for k in KINDS}
        lo = {k: sb("lo_" + k, [P, WN]) for k in KINDS}
        RT = 2
        rect = sb("rect", [P, RT, 512], F32)
        hid = [sb(n, [P, 2, FT, PADT]) for n in ("hid_hi", "hid_lo")]
        loaded = {k: m.sem(f"mlp_{k}_loaded") for k in KINDS}
        hi_made = {k: sem(k + "_hi_made") for k in KINDS}
        lo_made = {k: sem(k + "_lo_made") for k in KINDS}
        (product, rectified, squared, hid_hi, hid_lo, added) = (
            sem(n) for n in ("product", "rectified", "squared", "hid_hi", "hid_lo", "added"))
        padded = sem("padded")
        gain = sb("gain", [P, D], F32)
        stat = sb("stat", [P, 4, TILES], F32)
        (gain_loaded, rowsq, var_ready, std_ready, vec, y_ready) = (
            sem(n) for n in ("gain_loaded", "rowsq", "var_ready", "std_ready", "vec", "y_ready"))
        stored = m.sem("fin_stored")
        UPS, DOWNS = 3 * FT, 2 * TILES
        phases = [("up", 0)]
        for g in range(NG):
            phases += [("up", g + 1)] * (g + 1 < NG) + [("down", g)]
        units = []
        for kind, g in phases:
            units += [(kind, g, a, b) for a in range(FT if kind == "up" else TILES) for b in range(3 if kind == "up" else 2)]
        rank, seen = [], {"up": 0, "down": 0}
        for kind, *_ in units:
            seen[kind] += 1
            rank.append(seen[kind])
        ends = {}
        for u, (kind, g, _, _) in enumerate(units):
            ends[kind, g] = u + 1
        w_of = {"up": lambda t: t[:].rearrange("p (k n) -> p k n", k=KT),
                "down": lambda t: t[:].rearrange("p (f n) -> p f n", f=FT)}
        with nc.Block() as block:
            @block.sync
            def _(sp):
                for kind, g in phases[1:]:
                    if g:
                        sp.wait_ge(lo_made[kind], g)
                    src = m.a["w_" + kind][g].rearrange("p a n -> p (a n)")
                    sp.dma_start(raw[kind][:], src).then_inc(loaded[kind], 16)
                sp.dma_start(gain[:], m.a["ln_f"]).then_inc(gain_loaded, 16)
                for t in range(TILES):
                    sp.wait_ge(y_ready, t + 1)
                    dst = m.o["y_p"][t * P:(t + 1) * P, :] if t < TS else m.o["y_s"]
                    sp.dma_start(dst, m.x2[:ROWS[t], t, :]).then_inc(stored, 16)
                sp.wait_ge(stored, 16 * TILES)

            @block.scalar
            def _(act):
                def round_weights(kind, g):
                    act.wait_ge(loaded[kind], 16 * (g + 1))
                    if g:
                        act.wait_ge(product, ends[kind, g - 1])
                    act.activation(hi[kind][:], raw[kind][:], ACT.Copy).then_inc(hi_made[kind], 1)

                def round_hidden(u):
                    _, g, a, b = units[u]
                    o, w = GROUPS_N[b]
                    act.wait_ge(squared, rank[u])
                    act.activation(hid[0][:, g % 2, a, o:o + w], rect[:, (rank[u] - 1) % RT, :w], ACT.Copy).then_inc(hid_hi, 1)

                round_weights("up", 0)
                waiting = None
                for u, (kind, g, a, b) in enumerate(units):
                    if kind == "down":
                        if waiting is not None:
                            round_hidden(waiting)
                            waiting = None
                        if (a, b) == (0, 0) and g + 2 < NG:
                            round_weights("up", g + 2)
                        if (a, b) == (0, 0) and g == NG - 1:
                            round_weights("down", g)
                        continue
                    o, w = GROUPS_N[b]
                    if (a, b) == (0, 0):
                        if g:
                            round_weights("down", g - 1)
                        if g >= 2:
                            act.wait_ge(product, ends["down", g - 2])
                    act.wait_ge(product, u + 1)
                    if rank[u] > RT:
                        act.wait_ge(hid_lo, rank[u] - RT)
                    act.activation(rect[:, (rank[u] - 1) % RT, :w], m.ps[:, u % 8, :w], ACT.Relu).then_inc(rectified, 1)
                    if waiting is not None:
                        round_hidden(waiting)
                    waiting = u
                    if g == 0 and (a, b) == (FT - 1, 2):
                        round_hidden(waiting)
                        waiting = None
                        round_weights("up", 1)
                junk = rect[:].rearrange("p a n -> p (a n)")
                for t in range(TILES):
                    n = ROWS[t]
                    act.wait_ge(added, DOWNS * (NG - 1) + 2 * t + 2)
                    if t:
                        act.wait_ge(rowsq, t)
                    else:
                        act.wait_ge(hid_lo, UPS * NG)
                    act.activation(junk[:n, :], m.x2[:n, t, :], ACT.Square, accum_out=stat[:n, 0, t:t + 1]).then_inc(rowsq, 1)
                    act.wait_ge(var_ready, t + 1)
                    act.activation(stat[:n, 2, t:t + 1], stat[:n, 1, t:t + 1], ACT.Sqrt).then_inc(std_ready, 1)

            @block.gpsimd
            def _(pool):
                for part in hid:
                    pool.memset(part[:, :, :, TOK:].bitcast(F32), 0.0).then_inc(padded, 1)
                for u, (kind, g, a, b) in enumerate(units):
                    if kind == "up":
                        w = GROUPS_N[b][1]
                        pool.wait_ge(rectified, rank[u])
                        part = rect[:, (rank[u] - 1) % RT, :w]
                        pool.tensor_tensor(part, part, part, ALU.mult).then_inc(squared, 1)

            @block.vector
            def _(dve):
                def rest_of_weights(kind, g):
                    dve.wait_ge(hi_made[kind], g + 1)
                    dve.tensor_tensor(lo[kind][:], raw[kind][:], hi[kind][:], ALU.subtract).then_inc(lo_made[kind], 1)

                link = Link(dve, vec)

                def variance(t):
                    n = ROWS[t]
                    dve.wait_ge(rowsq, t + 1)
                    dve.tensor_scalar(stat[:n, 1, t:t + 1], stat[:n, 0, t:t + 1], 1.0 / D, EPS, ALU.mult, ALU.add).then_inc(var_ready, 1)

                def normalise(t):
                    n = ROWS[t]
                    dve.wait_ge(std_ready, t + 1)
                    link(dve.reciprocal(stat[:n, 3, t:t + 1], stat[:n, 2, t:t + 1]))
                    dve.scalar_tensor_tensor(m.x2[:n, t, :], m.x2[:n, t, :], stat[:n, 3, t:t + 1], gain[:n, :],
                                             ALU.mult, ALU.mult).then_inc(y_ready, 1)

                rest_of_weights("up", 0)
                for u, (kind, g, a, b) in enumerate(units):
                    if kind == "up":
                        o, w = GROUPS_N[b]
                        if (a, b) == (0, 0) and g:
                            rest_of_weights("down", g - 1)
                        dve.wait_ge(hid_hi, rank[u])
                        dve.tensor_tensor(hid[1][:, g % 2, a, o:o + w], rect[:, (rank[u] - 1) % RT, :w],
                                          hid[0][:, g % 2, a, o:o + w], ALU.subtract).then_inc(hid_lo, 1)
                        if g == 0 and (a, b) == (FT - 1, 2):
                            rest_of_weights("up", 1)
                        continue
                    if (a, b) == (0, 0) and g + 2 < NG:
                        rest_of_weights("up", g + 2)
                    if (a, b) == (0, 0) and g == NG - 1:
                        rest_of_weights("down", g)
                    n = ROWS[a]
                    dve.wait_ge(product, u + 1)
                    if g:
                        dve.wait_ge(added, DOWNS * (g - 1) + 2 * a + b + 1)
                    part = m.x2[:n, a, 512 * b:512 * b + 512]
                    dve.tensor_tensor(part, part, m.ps[:n, u % 8, :], ALU.add).then_inc(added, 1)
                    if g == NG - 1 and a:
                        if b == 0:
                            variance(a - 1)
                        else:
                            if a == 1:
                                dve.wait_ge(gain_loaded, 16)
                            normalise(a - 1)
                variance(TS)
                normalise(TS)

            @block.tensor
            def _(pe):
                for u, (kind, g, a, b) in enumerate(units):
                    x = g % 2
                    if (a, b) == (0, 0):
                        pe.wait_ge(lo_made[kind], g + 1)
                        if kind == "down":
                            pe.wait_ge(hid_lo, UPS * (g + 1))
                            pe.wait_ge(padded, 2)
                    if u >= 8:
                        pe.wait_ge(rectified if units[u - 8][0] == "up" else added, rank[u - 8])
                    w2 = [w_of[kind](t[kind]) for t in (hi, lo)]
                    if kind == "up":
                        o, w = GROUPS_N[b]
                        for k in range(KT):
                            last = triple(pe, m.ps[:, u % 8, :w], [t[:, k, a * P:(a + 1) * P] for t in w2],
                                          [t[:, k, o:o + w] for t in m.h2], k == 0, k == KT - 1)
                    else:
                        for f in range(FT):
                            last = triple(pe, m.ps[:, u % 8, :], [t[:, x, f, a * P:(a + 1) * P] for t in hid],
                                          [t[:, f, 512 * b:512 * b + 512] for t in w2], f == 0, f == FT - 1)
                    last.then_inc(product, 1)


def mlp(nc, m):
    with ExitStack() as normed:
        m.h2 = [normed.enter_context(nc.sbuf_tensor(n, [P, KT, TOK], F32R)) for n in ("h2_hi", "h2_lo")]
        norm_transpose(nc, m, "ln2", m.a["ln2"], m.h2, m.x2, False)
        mlp_products(nc, m)



def hymba_layer(nc, a, o, stages):
    m = Memory()
    with ExitStack() as ctx:
        live = []
        stored = {n: nc.alloc_semaphore(n) for n in ("proj_stored", "dn_stored", "s5_stored", "fin_stored", "caches_loaded", "mlp_up_loaded")}

        def sem(name):
            if name in stored:
                return stored[name]
            live.append(nc.alloc_semaphore(name))
            return live[-1]

        def recycle_semaphores():
            nc.clear_and_free_semaphores(live)
            live.clear()
            nc.all_engine_barrier()

        m.sem = sem
        keep = lambda n, s: ctx.enter_context(nc.sbuf_tensor(n, s, F32))
        m.ps = ctx.enter_context(nc.psum_tensor("ps", [P, 8, 512], F32))
        m.const = a["const"]
        m.x_prompt, m.x_sample = a["x_prompt"], a["x_sample"]
        m.w_in = [a["w_feat"][c] for c in range(FEAT)] + [a["w_token"][c] for c in range(TOKEN_CHUNKS)]
        m.cache_win, m.state_conv, m.state_dn = a["cache_win"], a["state_conv"], a["state_dn"]
        m.conv_w, m.a_log, m.dt_bias, m.norm_w = a["conv_w"], a["a_log"], a["dt_bias"], a["norm_w"]
        m.kv_prompt, m.kv_sample, m.win_prompt, m.win_sample = o["kv_p"], o["kv_s"], o["win_p"], o["win_s"]
        m.conv_prompt, m.conv_sample = o["conv_p"], o["conv_s"]
        m.dn_prompt, m.dn_sample = o["dn_p"], o["dn_s"]
        m.a, m.o = a, o
        m.ident = keep("ident", [P, P])
        ident_loaded = m.sem("ident_loaded")
        with nc.Block() as block:
            @block.sync
            def _(sp):
                at, w = CONST_AT["ident"]
                sp.dma_start(m.ident[:], m.const[:, at:at + w]).then_inc(ident_loaded, 16)
                sp.wait_ge(ident_loaded, 16)
        right = lambda stack, n, s, dt=F32: stack.enter_context(nc.sbuf_tensor(n, s, dt, side="right"))
        with ExitStack() as mixed:
            m.mixT = mixed.enter_context(nc.sbuf_tensor("mixT", [P, KT, PADC], F32))
            mixers = mixed.enter_context(ExitStack())
            hold = lambda n, s: mixers.enter_context(nc.sbuf_tensor(n, s, F32))
            with ExitStack() as normed:
                m.hT2 = [right(normed, n, [P, KT, PADT], F32R) for n in ("h_hi", "h_lo")]
                norm_transpose(nc, m, "ln1", a["ln1"], m.hT2, None, True)
                m.uT = right(normed, "uT", [P, 2, TOK])
                with ExitStack() as features:
                    m.dnx = right(features, "dnx", [P, 6, PADC])
                    feature_and_s5(nc, m)
                    m.qT = hold("qT", [P, 4, TOK])
                    m.convs = hold("convs", [P, 6, NB * NQ])
                    token_raw = m.uT[:].rearrange("p c n -> p (c n)")[:, :KT * (KV + SMALL) // TOKEN_CHUNKS]
                    m.token_raw = token_raw, m.sem("token_raw_loaded")
                    query_projection(nc, m)
                tokens = hold("tokens", [P, TILES, KV + SMALL])
                m.kv, m.small = tokens[:, :, :KV], tokens[:, :, KV:]
                token_projection(nc, m, tokens)
            with ExitStack() as caches:
                m.ck = right(caches, "ck", [P, NB * PAGES, 512])
                delta_net(nc, m)
                recycle_semaphores()
                m.cw = right(caches, "cw", [P, NB * PAGES, 256])
                key_tables = mixers.enter_context(ExitStack())
                key_prep(nc, m, key_tables)
                sample_attention(nc, m)
            m.out_raw = right(ctx, "out_raw", [P, KT * D // OUT_CHUNKS]), m.sem("out_raw_loaded")
            prompt_attention(nc, m)
            mixers.close()
            m.x2 = right(ctx, "x2", [P, TILES, D])
            output_projection(nc, m)
            recycle_semaphores()
        if "mlp" in stages:
            mlp(nc, m)
        nc.clear_and_free_semaphores(live)



STAGES = ("dn","s5","attn","mlp")


def host_inputs(i):
    f = np.float32
    w = i["w_in"][0]
    kt = lambda x: np.ascontiguousarray(x.reshape(KT, P, -1).transpose(1, 0, 2).reshape(P, -1))
    feat = [np.concatenate([w[:, h * HD:(h + 1) * HD], w[:, (h + 4) * HD:(h + 5) * HD]], 1) for h in range(4)]
    feat += [w[:, 1304 + c * P:1304 + (c + 1) * P] for c in range(6)]
    feat += [w[:, 2336 + c * P:2336 + (c + 1) * P] for c in range(2)]
    a = {
        "const": constants_array(),
        "x_prompt": i["x_prompt"][0], "x_sample": i["x_sample"].reshape(NB * NQ, D),
        "ln1": i["ln1"][0].reshape(KT, P).T,
        "w_feat": np.stack([kt(x) for x in feat]),
        "w_token": np.stack([kt(x) for x in np.split(np.concatenate([w[:, 512:1304], w[:, 2072:2336]], 1), TOKEN_CHUNKS, 1)]),
        "cache_win": i["cache_win_kv"][0].reshape(NB, PAST, 256),
        "state_conv": i["state_dn_conv"][0].reshape(NB, 3, 6, P).transpose(3, 2, 0, 1),
        "conv_w": i["dn_conv_w"][0].reshape(6, P, 4).transpose(1, 0, 2),
        "a_log": np.broadcast_to(i["dn_a_log"][0], (P, 4)), "dt_bias": np.broadcast_to(i["dn_dt_bias"][0], (P, 4)),
        "norm_w": np.broadcast_to(i["dn_norm_w"][0], (P, HD)),
    }
    s = np.zeros((2, HD, NB, 2, 2, HD), f)
    dn = i["state_dn"][0].reshape(NB, 2, 2, HD, HD)
    for h in range(2):
        s[h, :, :, :, h] = dn[:, :, h].transpose(2, 0, 1, 3)
    state = lambda x: x.reshape(-1, 8, P).transpose(2, 0, 1)
    a["s5_par"] = state(np.stack([i["s5_lambda_re"][0], i["s5_lambda_im"][0],
                                  np.broadcast_to(i["s5_log_step"][0][:, None], (16, 64))]))
    a["s5_d"] = i["s5_d"][0].reshape(2, P).T
    a["w_glu"] = i["s5_w_glu"][0].reshape(2, P, 256).transpose(1, 0, 2)
    b, c = np.zeros((P, 2, 8, P), f), np.zeros((P, 2, 8, P), f)
    for g in range(16):
        rows, ch = slice((g % 2) * 64, (g % 2) * 64 + 64), slice((g % 8) * 16, (g % 8) * 16 + 16)
        for ri, part in enumerate(("re", "im")):
            b[rows, ri, g // 2, ch] = i["s5_b_" + part][0, g]
            c[rows, ri, g // 2, ch] = i["s5_c_" + part][0, g].T
    a["s5_b"], a["s5_c"] = b, c
    a["s5_h0"] = np.stack([i["state_s5_" + part][0].reshape(NB, 8, P).transpose(2, 1, 0) for part in ("re", "im")], 1)
    wck, wcv = np.zeros((P, 2, 2), f), np.zeros((P, 2, 62), f)
    for blk in range(2):
        wck[64 * blk:64 * blk + 64, :, blk] = i["nsa_wck"][0].T
        wcv[64 * blk:64 * blk + 64, :, 30 + blk] = i["nsa_wcv"][0].T
    a["wck"], a["wcv"] = wck.reshape(P, 4), wcv
    a["page_table"] = i["page_table"].reshape(1, NB * PAGES)
    a["cache_nsa"] = i["cache_nsa_kv"][0].reshape(-1, P, 512)
    a["ln2"] = i["ln2"][0].reshape(KT, P).T
    a["ln_f"] = np.broadcast_to(i["ln_f"], (P, D))
    wo = i["w_out"][0]
    heads = np.concatenate([np.concatenate([wo[h * HD:(h + 1) * HD], wo[(h + 4) * HD:(h + 5) * HD]], 0) for h in range(4)], 0)
    a["w_out"] = np.stack([kt(x) for x in np.split(np.concatenate([heads, wo[512:]], 0), OUT_CHUNKS, 1)])
    a["w_up"] = i["mlp_up"][0].reshape(KT, P, FF // FG, FG).transpose(2, 1, 0, 3)
    a["w_down"] = i["mlp_down"][0].reshape(FF // FG, FG // P, P, D).transpose(0, 2, 1, 3)
    a["state_dn"] = s.reshape(P, NB, 2, P)
    return a


OUTS = {"y_p": (SEQ, D), "y_s": (NB * NQ, D), "kv_p": (SEQ, 512), "kv_s": (NB * NQ, 512),
        "win_p": (512, 256), "win_s": (NB, PAST + NQ, 256), "conv_p": (P, 6, 3), "conv_s": (P, 6, NB, 3),
        "dn_p": (P, 2, HD), "dn_s": (P, NB, 2, HD), "s5_p": (P, 8, 2), "s5_s": (P, 8, 2, NB)}


def host_outputs(r):
    dn_s = r["dn_s"].reshape(2, HD, NB, 2, HD).transpose(2, 3, 0, 1, 4).reshape(1, NB, 4, HD, HD)
    dn_p = r["dn_p"].reshape(2, HD, 2, HD).transpose(2, 0, 1, 3).reshape(1, 1, 4, HD, HD)
    s5_p = r["s5_p"].transpose(2, 1, 0).reshape(2, 1, 1, 16, 64)
    s5_s = r["s5_s"].transpose(2, 3, 1, 0).reshape(2, 1, NB, 16, 64)
    return (r["y_p"].reshape(1, SEQ, D), r["y_s"].reshape(NB, NQ, D),
            r["kv_p"].reshape(1, 1, SEQ, 4, 2, HD), r["kv_s"].reshape(1, NB, NQ, 4, 2, HD),
            r["win_p"].reshape(1, 1, 512, 2, 2, HD), r["win_s"].reshape(1, NB, PAST + NQ, 2, 2, HD),
            r["conv_p"].transpose(2, 1, 0).reshape(1, 1, 3, KV), r["conv_s"].transpose(2, 3, 1, 0).reshape(1, NB, 3, KV),
            dn_p, dn_s, s5_p[0], s5_s[0], s5_p[1], s5_s[1])


def kernel(**inputs):
    import concourse.bacc as bacc
    from concourse.bass_utils import run_bass_kernel_spmd

    nc = bacc.Bacc("TRN2", target_bir_lowering=False, num_devices=1)
    arrays, a, o = {}, {}, {}
    for name, x in host_inputs({k: np.asarray(v) for k, v in inputs.items()}).items():
        x = np.ascontiguousarray(x)
        arrays["in_" + name] = x
        a[name] = nc.dram_tensor("in_" + name, x.shape, mybir.dt.from_np(x.dtype), kind="ExternalInput").ap()
    for name, shape in OUTS.items():
        o[name] = nc.dram_tensor("out_" + name, shape, F32, kind="ExternalOutput").ap()
    hymba_layer(nc, a, o, STAGES)
    r = run_bass_kernel_spmd(nc, [arrays], core_ids=[0])
    return tuple(np.ascontiguousarray(x) for x in host_outputs({n: np.asarray(r.results[0]["out_" + n]) for n in OUTS}))
```

```python
from contextlib import ExitStack

import numpy as np
import concourse.bass as bass
from concourse import mybir

P = 128
F32 = mybir.dt.float32
F32R = mybir.dt.float32r
I32 = mybir.dt.int32
ALU = mybir.AluOpType
ACT = mybir.ActivationFunctionType
AX = mybir.AxisListType

D = 1024
KT = D // P
SEQ = 1024
NB, NQ = 8, 8
TOK = SEQ + NB * NQ
TILES = SEQ // P + 1
ROWS = [P] * (TILES - 1) + [NB * NQ]
TS = TILES - 1
PADT = TILES * P
GROUPS_N = [(0, 364), (364, 364), (728, 360)]
HD = 64
G, R = 2, 4
PAST = 256
PAGES = 2
WINDOW = 512
KV = 768
KCMP, VCMP, KSEL, VSEL, KWIN, VWIN = (c * P for c in range(6))
SMALL = 24 + 8 + 256
TOKEN_CHUNKS = 4
FEAT = 12
PADC = 3 + SEQ + NB * (3 + NQ)
CONVN = PADC - 3
OUT_CHUNKS = 4
FF = 4096
FG = 256
EPS = 1e-6
NEG = -1e30
MFLOOR = -1e25
NCH = 8
LEVELS = 7
SLEVELS = 3



def constant_tables():
    p = np.arange(P)[:, None]
    f = np.float32
    t = {}
    t["ident"] = np.eye(P, dtype=f)
    t["ones"] = np.ones((P, P), f)
    j = np.arange(1024)[None, :] - 896
    t["dist_sel"] = np.where(j <= p, j - p, NEG).astype(f)
    jw = np.arange(640)[None, :] - 512
    t["dist_win"] = np.where((jw <= p) & (p - jw < WINDOW), jw - p, NEG).astype(f)
    blk = np.arange(16)[None, None, :]
    tok = np.arange(8)[None, :, None] * P + p[:, :, None]
    t["dist_cmp"] = np.where((blk + 1) * 64 - 1 <= tok, blk * 64 + 31.5 - tok, NEG).astype(f).reshape(P, -1)
    q, r, b4 = p % 8, (p // 8) % 4, p // 32
    past = np.arange(PAST)[None, :] - (PAST + q)
    new = np.arange(64)[None, :]
    dist, cmp_ = [], []
    for h in range(2):
        own = (new // 8 == b4 + 4 * h) & (new % 8 <= q)
        dist.append(np.concatenate([past, np.where(own, new % 8 - q, NEG)], 1))
        c = np.arange(32)[None, :]
        cmp_.append(np.where(c // 4 == b4 + 4 * h, (c % 4) * 64 + 31.5 - (PAST + q), NEG))
    t["sdist"] = np.concatenate(dist, 1).astype(f)
    t["sdist_cmp"] = np.concatenate(cmp_, 1).astype(f)
    t["sslope"] = np.concatenate([2.0 ** -(g * 4 + r + 1.0) for g in range(2)], 1).astype(f)
    sel = np.zeros((P, 2, 4, P), f)
    for h in range(2):
        for b in range(4):
            for rr in range(4):
                for qq in range(8):
                    sel[(4 * h + b) * 8 + qq, h, rr, b * 32 + rr * 8 + qq] = 1
    t["gate_sel"] = sel.reshape(P, -1)
    i = np.arange(P)[None, :]
    same = (p // 8 == i // 8) & (p < 64) & (i < 64)
    t["upto"] = (p <= i).astype(f)
    t["upto_s"] = ((p <= i) & same).astype(f)
    t["ones_s"] = same.astype(f)
    t["neg"] = np.where(p <= i, 0, NEG).astype(f)
    t["neg_s"] = np.where((p <= i) & (p // 8 == i // 8), 0, NEG).astype(f)
    t["level"] = np.concatenate([((i >> s) == (p >> s) + 1) & (i >> (s + 1) == p >> (s + 1))
                                 for s in range(LEVELS)], 1).astype(f)
    t["seq_col"] = np.concatenate([np.broadcast_to((np.arange(64)[None, :] // 8) == b, (P, 64))
                                   for b in range(8)], 1).astype(f)
    t["seq_row"] = np.concatenate([(p // 8) == b for b in range(8)], 1).astype(f)
    t["notfirst"] = np.broadcast_to((np.arange(64)[None, :] % 8) != 0, (P, 64)).astype(f)
    return t


CONST_AT = {}


def constants_array():
    t = constant_tables()
    at, cols = 0, []
    for k, v in t.items():
        CONST_AT[k] = (at, v.shape[1])
        at += v.shape[1]
        cols.append(v)
    return np.ascontiguousarray(np.concatenate(cols, 1))


class Link:

    def __init__(self, eng, sem):
        self.eng, self.sem, self.n = eng, sem, 0

    def __call__(self, ins):
        self.n += 1
        ins.then_inc(self.sem, 1)
        self.eng.wait_ge(self.sem, self.n)


class Memory:
    pass



def norm_transpose(nc, m, name, gain, outT, source, load):
    with ExitStack() as ctx:
        sb = lambda n, s: ctx.enter_context(nc.sbuf_tensor(f"{name}_{n}", s, F32))
        sem = m.sem
        if load:
            slots = sb("x", [P, 3, D])
        xn = sb("xn", [P, 2, D])
        whole = sb("whole", [P, 2, KT, P])
        junk = sb("junk", [P, D])
        stat = sb("stat", [P, 4, TILES])
        gainT = sb("gain", [P, KT])
        x_loaded = [sem(f"{name}_x_loaded{i}") for i in range(3)]
        gain_loaded = sem(f"{name}_gain_loaded")
        squared, var_ready, std_ready = sem(f"{name}_squared"), sem(f"{name}_var"), sem(f"{name}_std")
        normed, turned, evacuated = sem(f"{name}_normed"), sem(f"{name}_turned"), sem(f"{name}_evac")
        vec, hi_made, lo_made = sem(f"{name}_vec"), sem(f"{name}_hi_made"), sem(f"{name}_lo_made")
        hiT, loT = outT

        def x_at(t):
            return (slots[:ROWS[t], t % 3, :] if load else source[:ROWS[t], t, :])

        with nc.Block() as block:
            @block.sync
            def _(sp):
                sp.dma_start(gainT[:], gain).then_inc(gain_loaded, 16)
                if load:
                    for t in range(TILES):
                        if t >= 3:
                            sp.wait_ge(normed, t - 2)
                        src = m.x_prompt[t * P:(t + 1) * P, :] if t < TS else m.x_sample
                        sp.dma_start(x_at(t), src).then_inc(x_loaded[t % 3], 16)
                    sp.dma_start(m.feat_raw[0][:], m.w_in[10]).then_inc(m.feat_raw[1], 16)

            @block.gpsimd
            def _(pool):
                if hiT.shape[2] > TOK:
                    for part in outT:
                        pool.memset(part[:, :, TOK:].bitcast(F32), 0.0)

            @block.scalar
            def _(act):
                def square(t):
                    if load:
                        act.wait_ge(x_loaded[t % 3], 16 * (t // 3 + 1))
                    if t:
                        act.wait_ge(squared, t)
                    act.activation(junk[:ROWS[t], :], x_at(t), ACT.Square,
                                   accum_out=stat[:ROWS[t], 0, t:t + 1]).then_inc(squared, 1)

                def split(t):
                    n = ROWS[t]
                    act.wait_ge(evacuated, 2 * (t + 1))
                    act.activation(hiT[:, :, t * P:t * P + n], whole[:, t % 2, :, :n], ACT.Copy).then_inc(hi_made, 1)
                square(0)
                for t in range(TILES):
                    if t + 1 < TILES:
                        square(t + 1)
                    act.wait_ge(var_ready, t + 1)
                    act.activation(stat[:ROWS[t], 2, t:t + 1], stat[:ROWS[t], 1, t:t + 1],
                                   ACT.Sqrt).then_inc(std_ready, 1)
                    if t >= 2:
                        split(t - 2)
                split(TILES - 2)
                split(TILES - 1)

            @block.vector
            def _(dve):
                link = Link(dve, vec)

                def subtract(t):
                    n = ROWS[t]
                    dve.wait_ge(hi_made, t + 1)
                    dve.tensor_tensor(loT[:, :, t * P:t * P + n], whole[:, t % 2, :, :n], hiT[:, :, t * P:t * P + n],
                                      ALU.subtract).then_inc(lo_made, 1)

                def evacuate(t):
                    dve.wait_ge(turned, t + 1)
                    if t >= 2:
                        dve.wait_ge(lo_made, t - 1)
                    for h in range(2):
                        bank = m.ps[:, (t % 2) * 2 + h, :].rearrange("p (k n) -> p k n", k=4)[:, :, :ROWS[t]]
                        dve.tensor_tensor(whole[:, t % 2, 4 * h:4 * h + 4, :ROWS[t]], bank,
                                          gainT[:, 4 * h:4 * h + 4].unsqueeze(2).to_broadcast([P, 4, ROWS[t]]),
                                          ALU.mult).then_inc(evacuated, 1)
                dve.wait_ge(gain_loaded, 16)
                for t in range(TILES):
                    n = ROWS[t]
                    dve.wait_ge(squared, t + 1)
                    dve.tensor_scalar(stat[:n, 1, t:t + 1], stat[:n, 0, t:t + 1], 1.0 / D, EPS,
                                      ALU.mult, ALU.add).then_inc(var_ready, 1)
                    dve.wait_ge(std_ready, t + 1)
                    link(dve.reciprocal(stat[:n, 3, t:t + 1], stat[:n, 2, t:t + 1]))
                    if t >= 2:
                        dve.wait_ge(turned, t - 1)
                    dve.tensor_scalar(xn[:n, t % 2, :], x_at(t), stat[:n, 3, t:t + 1], None,
                                      ALU.mult).then_inc(normed, 1)
                    if t >= 3:
                        subtract(t - 3)
                    if t:
                        evacuate(t - 1)
                subtract(TILES - 3)
                evacuate(TILES - 1)
                subtract(TILES - 2)
                subtract(TILES - 1)

            @block.tensor
            def _(pe):
                for t in range(TILES):
                    pe.wait_ge(normed, t + 1)
                    if t >= 2:
                        pe.wait_ge(evacuated, 2 * (t - 1))
                    for k in range(KT):
                        last = pe.transpose(m.ps[:, (t % 2) * 2 + k // 4, (k % 4) * P:(k % 4) * P + ROWS[t]],
                                            xn[:ROWS[t], t % 2, k * P:(k + 1) * P],
                                            m.ident[:ROWS[t], :ROWS[t]])
                    last.then_inc(turned, 1)


def triple(pe, out, lhs, rhs, first, last):
    pe.matmul(out, lhs[0], rhs[0], start=first, stop=False)
    pe.matmul(out, lhs[0], rhs[1], start=False, stop=False)
    return pe.matmul(out, lhs[1], rhs[0], start=False, stop=last)



def no_steps(*_):
    pass


def project(nc, m, name, chunks, widths, units, evacuation, feature, banks=range(8), side=None, evac=None,
            preload=None, out_by_dve=False):
    side = side or {}
    with ExitStack() as ctx:
        sem = lambda n: m.sem(f"{name}_{n}")
        NC, W, BANKS = len(chunks), KT * max(widths), len(banks)
        if preload is None:
            preload = ctx.enter_context(nc.sbuf_tensor(f"{name}_raw", [P, W], F32)), sem("w_loaded")
            loads = range(NC)
        else:
            loads = range(1, NC)
        raw, w_loaded = preload
        hi, lo = (ctx.enter_context(nc.sbuf_tensor(f"{name}_{n}", [P, 2, W], F32R)) for n in ("whi", "wlo"))
        hi_made, lo_made, product = (sem(n) for n in ("hi_made", "lo_made", "product"))
        evac = evac or [sem("evac_act"), sem("evac_dve")]
        ends = [max(u for u, unit in enumerate(units) if unit[0] == c) + 1 for c in range(NC)]
        begins = [0] + ends[:-1]

        def out_by(u):
            return (1, u + 1) if out_by_dve else (u % 2, u // 2 + 1)

        def slot(t, c):
            return t[:, c % 2, :KT * widths[c]].rearrange("p (k n) -> p k n", k=KT)

        with nc.Block() as block:
            @block.sync
            def _(sp):
                side.get("sync_first", no_steps)(sp, evac)
                for c in loads:
                    if c:
                        sp.wait_ge(lo_made, c)
                    sp.dma_start(raw[:, :KT * widths[c]], chunks[c]).then_inc(w_loaded, 16)
                side.get("sync", no_steps)(sp, evac)

            @block.gpsimd
            def _(pool):
                side.get("gpsimd", no_steps)(pool, evac)

            @block.scalar
            def _(act):
                def round_weights(c):
                    act.wait_ge(w_loaded, 16 * (c + 1))
                    if c >= 2:
                        act.wait_ge(product, ends[c - 2])
                    n = KT * widths[c]
                    act.activation(hi[:, c % 2, :n], raw[:, :n], ACT.Copy).then_inc(hi_made, 1)
                round_weights(0)
                side.get("scalar_first", no_steps)(act, evac)
                for u in range(len(units)):
                    if u in begins and begins.index(u) + 1 < NC:
                        round_weights(begins.index(u) + 1)
                    if out_by(u)[0] == 0:
                        act.wait_ge(product, u + 1)
                        evacuation(act, True, u).then_inc(evac[0], 1)
                    side.get("scalar", no_steps)(act, u)
                side.get("stores", no_steps)(act, evac)

            @block.vector
            def _(dve):
                def rest_of_weights(c):
                    dve.wait_ge(hi_made, c + 1)
                    n = KT * widths[c]
                    dve.tensor_tensor(lo[:, c % 2, :n], raw[:, :n], hi[:, c % 2, :n], ALU.subtract).then_inc(lo_made, 1)
                rest_of_weights(0)
                side.get("vector_first", no_steps)(dve, evac)
                for u in range(len(units)):
                    if u in begins and begins.index(u) + 1 < NC:
                        rest_of_weights(begins.index(u) + 1)
                    if out_by(u)[0]:
                        dve.wait_ge(product, u + 1)
                        evacuation(dve, False, u).then_inc(evac[1], 1)
                    side.get("vector", no_steps)(dve, u)

            @block.tensor
            def _(pe):
                side.get("tensor_first", no_steps)(pe, evac)
                for u, (c, n) in enumerate(units):
                    if u in begins:
                        pe.wait_ge(lo_made, c + 1)
                    if u >= BANKS:
                        pe.wait_ge(evac[out_by(u - BANKS)[0]], out_by(u - BANKS)[1])
                    w = (slot(hi, c), slot(lo, c))
                    bank = m.ps[:, banks[u % BANKS], :]
                    for k in range(KT):
                        wk = [x[:, k, :] for x in w]
                        if feature:
                            o, width = GROUPS_N[n]
                            last = triple(pe, bank[:, :width], wk, [x[:, k, o:o + width] for x in m.hT2],
                                          k == 0, k == KT - 1)
                        else:
                            last = triple(pe, bank[:, :widths[c]],
                                          [x[:, k, n * P:(n + 1) * P] for x in m.hT2], wk, k == 0, k == KT - 1)
                    last.then_inc(product, 1)
                    side.get("tensor", no_steps)(pe, u)


def token_projection(nc, m, tokens):
    stored, zeroed = m.sem("proj_stored"), m.sem("kv_zeroed")
    units = [(c, t) for c in range(TOKEN_CHUNKS) for t in range(TILES)]
    width = (KV + SMALL) // TOKEN_CHUNKS

    def evacuation(eng, scalar, u):
        c, t = units[u]
        rows = ROWS[t]
        src, dst = m.ps[:rows, u % 8, :width], tokens[:rows, t, width * c:width * (c + 1)]
        return eng.activation(dst, src, ACT.Copy) if scalar else eng.tensor_copy(dst, src)

    def stores(sp, evac):
        sp.wait_ge(evac[0], (len(units) + 1) // 2)
        sp.wait_ge(evac[1], len(units) // 2)
        for t in range(TS):
            sp.dma_start(m.kv_prompt[t * P:(t + 1) * P, :], m.kv[:, t, 0:512]).then_inc(stored, 16)
            if t >= TS // 2:
                sp.dma_start(m.win_prompt[(t - 4) * P:(t - 3) * P, :], m.kv[:, t, 512:768]).then_inc(stored, 16)
        sp.dma_start(m.kv_sample, m.kv[:NB * NQ, TS, 0:512]).then_inc(stored, 16)
        for b in range(NB):
            sp.dma_start(m.win_sample[b, PAST:PAST + NQ, :],
                         m.kv[b * NQ:(b + 1) * NQ, TS, 512:768]).then_inc(stored, 16)
        sp.dma_start(m.win_sample[:, 0:PAST, :], m.cache_win).then_inc(stored, 16)

    def gpsimd(pool, _):
        pool.memset(m.small[64:128, TS, :], 0.0).then_inc(zeroed, 1)

    project(nc, m, "kvp", m.w_in[FEAT:], [width] * TOKEN_CHUNKS, units, evacuation, False, side={"stores": stores, "gpsimd": gpsimd},
            preload=m.token_raw)


def query_projection(nc, m):
    with ExitStack() as ctx:
        units = [(c, n) for c in range(4) for n in range(3)]
        convw = ctx.enter_context(nc.sbuf_tensor("convw", [P, 6, 4], F32))
        conv = m.mixT[:, 0:6, :]
        loaded, tap, conv_made, silu_made = (m.sem(f"conv_{n}") for n in ("loaded", "tap", "made", "silu"))

        def evacuation(eng, scalar, u):
            c, n = units[u]
            o, w = GROUPS_N[n]
            src, dst = m.ps[:, u % 8, :w], m.qT[:, c, o:o + w]
            if scalar:
                return eng.activation(dst, src, ACT.Copy, scale=0.125)
            return eng.tensor_scalar(dst, src, 0.125, None, ALU.mult)

        def load(pool, _):
            pool.dma_start(convw[:], m.conv_w).then_inc(loaded, 16)

        def load_next(sp, _):
            sp.dma_start(m.token_raw[0], m.w_in[FEAT]).then_inc(m.token_raw[1], 16)

        def vector(dve, u):
            if u % 3 == 2 or u // 3 * 2 >= 6:
                return
            f = u // 3 * 2 + u % 3
            if f == 0:
                dve.wait_ge(loaded, 16)
            for j in range(4):
                src, w = m.dnx[:, f, j:j + CONVN], convw[:, f, j:j + 1]
                if j == 0:
                    dve.tensor_scalar(conv[:, f, :CONVN], src, w, None, ALU.mult).then_inc(tap, 1)
                else:
                    last = dve.scalar_tensor_tensor(conv[:, f, :CONVN], src, w, conv[:, f, :CONVN], ALU.mult, ALU.add)
                    last.then_inc(conv_made if j == 3 else tap, 1)
                if j < 3:
                    dve.wait_ge(tap, 3 * f + j + 1)

        def silu(act, f):
            act.wait_ge(conv_made, f + 1)
            act.activation(conv[:, f, :SEQ], conv[:, f, :SEQ], ACT.Silu).then_inc(silu_made, 1)
            act.activation(m.convs[:, f].rearrange("p (b q) -> p b q", b=NB),
                           conv[:, f, 3 + SEQ:].rearrange("p (b s) -> p b s", b=NB)[:, :, :NQ],
                           ACT.Silu).then_inc(silu_made, 1)

        def scalar(act, u):
            if u % 3 == 2 and u // 3 * 2 < 6:
                silu(act, u // 3 * 2)
                silu(act, u // 3 * 2 + 1)

        project(nc, m, "qp", m.w_in[:4], [P] * 4, units, evacuation, True,
                side={"gpsimd": load, "sync": load_next, "vector": vector, "scalar": scalar}, preload=m.query_raw)


def feature_and_s5(nc, m):
    with ExitStack() as ctx:
        convbuf = ctx.enter_context(nc.sbuf_tensor("convbuf", [P, 6, NB, 3], F32))
        stored, conv_in, conv_put = m.sem("proj_stored"), m.sem("conv_in"), m.sem("conv_put")
        units = [(c, n) for c in range(8) for n in range(3)]
        banks = [5, 6, 7]
        evac = [m.sem("fp_evac_act"), m.sem("fp_evac_dve")]
        s5 = S5(nc, m, ctx, evac)

        def evacuation(eng, scalar, u):
            c, n = units[u]
            o, w = GROUPS_N[n]
            src = m.ps[:, banks[u % 3], :w]
            if c < 2:
                dst = m.uT[:, c, o:o + w]
            elif n < 2:
                dst = m.dnx[:, c - 2, 3 + o:3 + o + w]
            else:
                dst, part = m.dnx[:, c - 2, 3 + o:3 + SEQ], src[:, :SEQ - o]
                if scalar:
                    eng.activation(dst, part, ACT.Copy)
                else:
                    eng.tensor_copy(dst, part)
                dst = m.dnx[:, c - 2, 3 + SEQ:].rearrange("p (b s) -> p b s", b=NB)[:, :, 3:]
                src = src[:, SEQ - o:].rearrange("p (b s) -> p b s", b=NB)
            return eng.activation(dst, src, ACT.Copy) if scalar else eng.tensor_copy(dst, src)

        def stores(sp, evac):
            sp.wait_ge(evac[1], (len(units) - 3) // 2 + 1)
            sp.dma_start(m.query_raw[0][:], m.w_in[0]).then_inc(m.query_raw[1], 16)
            sp.wait_ge(evac[0], (len(units) + 1) // 2)
            sp.wait_ge(evac[1], len(units) // 2)
            sp.wait_ge(conv_put, 7)
            sp.dma_start(m.conv_prompt, m.dnx[:, :, SEQ:SEQ + 3]).then_inc(stored, 16)
            for f in range(6):
                sp.dma_start(m.conv_sample[:, f],
                             m.dnx[:, f, 3 + SEQ:].rearrange("p (b s) -> p b s", b=NB)[:, :, NQ:NQ + 3]
                             ).then_inc(stored, 16)
            s5.store(sp)
            sp.wait_ge(stored, 16 * 7)

        def gpsimd(pool, _):
            pool.dma_start(convbuf[:], m.state_conv).then_inc(conv_in, 16)
            s5.load(pool)
            pool.memset(m.dnx[:, :, 0:3], 0.0).then_inc(conv_put, 1)
            pool.wait_ge(conv_in, 16)
            pool.wait_ge(conv_put, 1)
            for f in range(6):
                pool.tensor_copy(m.dnx[:, f, 3 + SEQ:].rearrange("p (b s) -> p b s", b=NB)[:, :, 0:3],
                                 convbuf[:, f]).then_inc(conv_put, 1)
            s5.pool(pool)

        project(nc, m, "fp", m.w_in[10:FEAT] + m.w_in[4:10], [P] * 8, units, evacuation, True, banks,
                {"sync": stores, "gpsimd": gpsimd, "scalar": s5.scalar, "vector": s5.vector, "tensor": s5.tensor}, evac, m.feat_raw)


STORES_OF_INPUT = TS + TS // 2 + 1 + NB + 1 + 1 + 6



class S5:
    M = 8
    CH = NCH + 1
    W = [P] * NCH + [NB * NQ]
    LR, LI, LS = range(3)
    (DT, MAG, TH, K, RS, RC, COS, SIN, AR, AI, DEN, FR, FI, T0, T1, T2) = range(16)

    def __init__(self, nc, m, stack, u_out):
        self.m, self.u_out = m, u_out
        M = self.M
        sb = lambda n, s: stack.enter_context(nc.sbuf_tensor(f"s5_{n}", s, F32))
        flat = m.mixT[:].rearrange("p k n -> p (k n)")
        parts = lambda i: flat[:, i * 2 * M * P:(i + 1) * 2 * M * P].rearrange("p (r m n) -> p r m n", r=2, m=M)
        self.bu, self.rot, self.rot_p = parts(0), parts(1), parts(2)
        self.bpad = self.bu
        self.mags = flat[:, 6 * M * P:6 * M * P + 64 * M].rearrange("p (m n) -> p m n", m=M)
        self.gelu, self.sigm = m.mixT[:, 0:2, :], m.mixT[:, 2:4, :]
        self.par = sb("par", [P, 3, M])
        self.dvec, self.wglu = sb("d", [P, 2]), sb("wglu", [P, 2, 256])
        self.cpad = sb("cpad", [P, 2, M, P])
        self.h0 = sb("h0", [P, 2, M, NB])
        self.notfirst = sb("notfirst", [P, 64])
        self.v = sb("v", [P, 16, M])
        self.bbT = sb("bbT", [P, 2, M, P])
        self.cs = sb("cs", [P, 2, M, P])
        self.magp = sb("magp", [P, M, P])
        self.h = sb("h", [P, 2, M, P])
        self.fin_p, self.fin_s = sb("fin_p", [P, M, 2]), sb("fin_s", [P, M, 2, NB])
        sem = lambda n: m.sem(f"s5_{n}")
        self.loaded, self.vec, self.e1, self.e2 = (sem(n) for n in ("loaded", "vec", "e1", "e2"))
        self.trig_in, self.trig, self.bb_made, self.bbT_turned = (sem(n) for n in ("trig_in", "trig", "bb_made", "bbT_turned"))
        self.bbT_out, self.neg_made, self.bu_prod, self.bu_out = (sem(n) for n in ("bbT_out", "neg_made", "bu_prod", "bu_out"))
        self.pin, self.vin, self.scanned, self.pout = (sem(n) for n in ("pin", "vin", "scanned", "pout"))
        self.h_ready, self.yprod, self.y_out, self.fin_ready = (sem(n) for n in ("h_ready", "yprod", "y_out", "fin_ready"))
        self.stored, self.gelu_made, self.glu, self.sig_made = (sem(n) for n in ("stored", "gelu_made", "glu", "sig_made"))
        self.mix_made = sem("mix_made")

    def shape(self, x, c):
        if c < NCH:
            return x
        return x[:, :, :NB * NQ].rearrange("p m (b q) -> p m b q", b=NB)

    def phase(self, ri, c):
        if c < NCH:
            return self.cs[:, ri]
        return self.cs[:, ri, :, :NQ].unsqueeze(2).to_broadcast([P, self.M, NB, NQ])

    def load(self, pool):
        m = self.m
        at, w = CONST_AT["notfirst"]
        for dst, src in ((self.par[:], m.a["s5_par"]), (self.bpad, m.a["s5_b"]), (self.cpad[:], m.a["s5_c"]),
                         (self.dvec[:], m.a["s5_d"]), (self.h0[:], m.a["s5_h0"]), (self.wglu[:], m.a["w_glu"]),
                         (self.notfirst[:], m.const[:, at:at + w])):
            pool.dma_start(dst, src).then_inc(self.loaded, 16)

    def store(self, sp):
        sp.wait_ge(self.fin_ready, 2)
        sp.dma_start(self.m.o["s5_p"], self.fin_p[:]).then_inc(self.stored, 16)
        sp.dma_start(self.m.o["s5_s"], self.fin_s[:]).then_inc(self.stored, 16)
        sp.wait_ge(self.stored, 32)


    def pool(self, pool):
        bu, rot, rot_p, at = self.bu, self.rot, self.rot_p, self.shape
        pool.wait_ge(self.trig, 3)
        for c in range(self.CH):
            pool.wait_ge(self.bu_out, 2 * (c + 1))
            if c:
                pool.wait_ge(self.h_ready, c)
            for ri in range(2):
                pool.tensor_tensor(at(rot_p[:, ri], c), at(bu[:, ri], c), self.phase(1 - ri, c), ALU.mult).then_inc(self.pin, 1)
            pool.wait_ge(self.scanned, c + 1)
            for ri in range(2):
                pool.tensor_tensor(at(rot_p[:, ri], c), at(rot[:, ri], c), self.phase(1 - ri, c), ALU.mult).then_inc(self.pout, 1)


    def scalar(self, act, u):
        v, m = self.v, self.m
        if u == 0:
            act.wait_ge(self.loaded, 16 * 7)
            act.activation(v[:, self.DT], self.par[:, self.LS], ACT.Exp).then_inc(self.e1, 1)
            act.activation(self.cpad[:, 1], self.cpad[:, 1], ACT.Copy, scale=-1.0).then_inc(self.neg_made, 1)
        if u == 1:
            act.wait_ge(self.e2, 1)
            act.activation(v[:, self.MAG], v[:, self.T0], ACT.Exp).then_inc(self.e1, 1)
        if u == 2:
            act.wait_ge(self.trig_in, 1)
            act.activation(v[:, self.COS], v[:, self.RC], ACT.Sin).then_inc(self.trig, 1)
            act.activation(v[:, self.SIN], v[:, self.RS], ACT.Sin).then_inc(self.trig, 1)
        if u == 5:
            for ri in range(2):
                act.wait_ge(self.bbT_turned, ri + 1)
                act.activation(self.bbT[:, ri].rearrange("p m n -> p (m n)"),
                               m.ps[:, 2 * ri:2 * ri + 2, :].rearrange("p a n -> p (a n)"), ACT.Copy).then_inc(self.bbT_out, 1)
        c = (u - 5) // 2
        if u >= 5 and u % 2 and c < self.CH:
            n = self.W[c]
            act.wait_ge(self.bu_prod, c + 1)
            if c == 0:
                act.wait_ge(self.trig, 3)
            else:
                act.wait_ge(self.pin, 2 * c)
                act.wait_ge(self.vin, c)
            for ri in range(2):
                act.activation(self.bu[:, ri, :, :n],
                               m.ps[:, 2 * ri:2 * ri + 2, :].rearrange("p a (q n) -> p (a q) n", n=P)[:, :, :n],
                               ACT.Copy).then_inc(self.bu_out, 1)
        if u == 20:
            act.wait_ge(self.h_ready, NCH)
            act.activation(self.fin_p[:], self.h[:, :, :, P - 1].rearrange("p r m -> p m r"), ACT.Copy).then_inc(self.fin_ready, 1)
        if u == 22:
            act.wait_ge(self.h_ready, self.CH)
            for ri in range(2):
                last = act.activation(self.fin_s[:, :, ri], self.h[:, ri, :, NQ - 1:NB * NQ:NQ], ACT.Copy)
            last.then_inc(self.fin_ready, 1)
        if u == 23:
            act.wait_ge(self.y_out, 2 * self.CH)
            act.wait_ge(self.vin, self.CH)
            for o, w in GROUPS_N:
                act.activation(self.gelu[:, :, o:o + w], m.mixT[:, 6:8, o:o + w], ACT.Gelu_apprx_tanh).then_inc(self.gelu_made, 1)
            for g, (o, w) in enumerate(GROUPS_N):
                act.wait_ge(self.glu, g + 1)
                act.activation(self.sigm[:, :, o:o + w], m.ps[:, 2 * (g % 2):2 * (g % 2) + 2, :w], ACT.Sigmoid).then_inc(self.sig_made, 1)


    def vector(self, dve, u):
        if u == 0:
            self.link = Link(dve, self.vec)
        if u == 1:
            self.angles(dve)
        if u == 3:
            self.input_matrix(dve)
            self.tables(dve)
        if u == 5:
            dve.wait_ge(self.bbT_out, 2)
        c = (u - 5) // 2
        if u >= 5 and u % 2 and c < self.CH:
            self.chunk(dve, c)
        if u == 23:
            self.y_out_of(dve, self.CH - 1)
            for g, (o, w) in enumerate(GROUPS_N):
                dve.wait_ge(self.sig_made, g + 1)
                dve.tensor_tensor(self.m.mixT[:, 6:8, o:o + w], self.gelu[:, :, o:o + w], self.sigm[:, :, o:o + w],
                                  ALU.mult).then_inc(self.mix_made, 1)

    def angles(self, dve):
        v, par, tt, link = self.v, self.par, dve.tensor_tensor, self.link
        DT, TH, K, RS, RC, T0, T1, T2 = (self.DT, self.TH, self.K, self.RS, self.RC, self.T0, self.T1, self.T2)
        dve.wait_ge(self.e1, 1)
        tt(v[:, T0], par[:, self.LR], v[:, DT], ALU.mult).then_inc(self.e2, 1)
        link(tt(v[:, TH], par[:, self.LI], v[:, DT], ALU.mult))
        link(dve.tensor_scalar(v[:, K], v[:, TH], 1.0 / (2 * np.pi), 12582912.0, ALU.mult, ALU.add))
        link(dve.tensor_scalar(v[:, K], v[:, K], 12582912.0, None, ALU.subtract))
        c1 = 6.28125
        c2 = float(np.float32(2 * np.pi - c1))
        c3 = 2 * np.pi - c1 - c2
        link(dve.scalar_tensor_tensor(v[:, T1], v[:, K], -c1, v[:, TH], ALU.mult, ALU.add))
        link(dve.scalar_tensor_tensor(v[:, T1], v[:, K], -c2, v[:, T1], ALU.mult, ALU.add))
        link(dve.scalar_tensor_tensor(v[:, T1], v[:, K], -c3, v[:, T1], ALU.mult, ALU.add))
        pi = 3.1415925
        link(dve.tensor_scalar(v[:, RS], v[:, T1], pi, -pi, ALU.min, ALU.max))
        link(dve.tensor_scalar(v[:, T1], v[:, T1], np.pi / 2, None, ALU.add))
        link(dve.tensor_scalar(v[:, T2], v[:, T1], np.pi, -2 * np.pi, ALU.is_gt, ALU.mult))
        link(tt(v[:, T1], v[:, T1], v[:, T2], ALU.add))
        dve.tensor_scalar(v[:, RC], v[:, T1], pi, -pi, ALU.min, ALU.max).then_inc(self.trig_in, 1)

    def over(self, c, n):
        return self.v[:, c].unsqueeze(2).to_broadcast([P, self.M, n])

    def input_matrix(self, dve):
        v, par, tt, link, h, rot = self.v, self.par, dve.tensor_tensor, self.link, self.h, self.rot
        LR, LI, AR, AI, DEN, FR, FI, T0, T1 = (self.LR, self.LI, self.AR, self.AI, self.DEN, self.FR, self.FI, self.T0, self.T1)
        dve.wait_ge(self.trig, 2)
        dve.wait_ge(self.e1, 2)
        link(tt(v[:, AR], v[:, self.MAG], v[:, self.COS], ALU.mult))
        link(tt(v[:, AI], v[:, self.MAG], v[:, self.SIN], ALU.mult))
        link(dve.tensor_scalar(v[:, AR], v[:, AR], 1.0, None, ALU.subtract))
        link(tt(v[:, T0], par[:, LR], par[:, LR], ALU.mult))
        link(tt(v[:, T1], par[:, LI], par[:, LI], ALU.mult))
        link(tt(v[:, T0], v[:, T0], v[:, T1], ALU.add))
        link(dve.reciprocal(v[:, DEN], v[:, T0]))
        link(tt(v[:, T0], v[:, AR], par[:, LR], ALU.mult))
        link(tt(v[:, T1], v[:, AI], par[:, LI], ALU.mult))
        link(tt(v[:, T0], v[:, T0], v[:, T1], ALU.add))
        link(tt(v[:, FR], v[:, T0], v[:, DEN], ALU.mult))
        link(tt(v[:, T0], v[:, AI], par[:, LR], ALU.mult))
        link(tt(v[:, T1], v[:, AR], par[:, LI], ALU.mult))
        link(tt(v[:, T0], v[:, T0], v[:, T1], ALU.subtract))
        link(tt(v[:, FI], v[:, T0], v[:, DEN], ALU.mult))
        dve.wait_ge(self.loaded, 16 * 7)
        for ri, (x, y, op) in enumerate(((0, 1, ALU.subtract), (1, 0, ALU.add))):
            link(tt(rot[:, ri], self.bpad[:, x], self.over(FR, P), ALU.mult))
            link(tt(h[:, ri], self.bpad[:, y], self.over(FI, P), ALU.mult))
            tt(rot[:, ri], rot[:, ri], h[:, ri], op).then_inc(self.bb_made, 1)

    def tables(self, dve):
        v, tt, link, h, cs, bu, magp = self.v, dve.tensor_tensor, self.link, self.h, self.cs, self.bu, self.magp
        M, MAG = self.M, self.MAG
        dve.wait_ge(self.bb_made, 2)
        link(dve.tensor_copy(cs[:, 0, :, 0:1], v[:, self.COS].unsqueeze(2)))
        link(dve.tensor_copy(cs[:, 1, :, 0:1], v[:, self.SIN].unsqueeze(2)))
        n = 1
        while n < P:
            cn = cs[:, 0, :, n - 1:n].to_broadcast([P, M, n])
            sn = cs[:, 1, :, n - 1:n].to_broadcast([P, M, n])
            tt(h[:, 0, :, :n], cs[:, 0, :, :n], cn, ALU.mult)
            tt(h[:, 1, :, :n], cs[:, 1, :, :n], cn, ALU.mult)
            tt(magp[:, :, :n], cs[:, 1, :, :n], sn, ALU.mult)
            link(tt(bu[:, 0, :, :n], cs[:, 0, :, :n], sn, ALU.mult))
            tt(cs[:, 0, :, n:2 * n], h[:, 0, :, :n], magp[:, :, :n], ALU.subtract)
            link(tt(cs[:, 1, :, n:2 * n], h[:, 1, :, :n], bu[:, 0, :, :n], ALU.add))
            n *= 2
        dve.tensor_copy(magp[:], self.over(MAG, P))
        tt(self.mags, self.over(MAG, 64), self.notfirst[:].unsqueeze(1).to_broadcast([P, M, 64]), ALU.mult)
        for ri in range(2):
            last = tt(self.h0[:, ri], self.h0[:, ri], self.over(MAG, NB), ALU.mult)
        last.then_inc(self.trig, 1)
        dve.wait_ge(self.trig, 3)

    def y_out_of(self, dve, c):
        m, n = self.m, self.W[c]
        dve.wait_ge(self.yprod, c + 1)
        for ct in range(2):
            dve.scalar_tensor_tensor(m.mixT[:, 6 + ct, c * P:c * P + n], m.uT[:, ct, c * P:c * P + n], self.dvec[:, ct:ct + 1],
                                     m.ps[:, 4, ct * P:ct * P + n], ALU.mult, ALU.add).then_inc(self.y_out, 1)

    def chunk(self, dve, c):
        tt, link, n = dve.tensor_tensor, self.link, self.W[c]
        bu, rot, rot_p, h, at = self.bu, self.rot, self.rot_p, self.h, self.shape
        dve.wait_ge(self.bu_out, 2 * (c + 1))
        tt(at(rot[:, 0], c), at(bu[:, 0], c), self.phase(0, c), ALU.mult)
        link(tt(at(rot[:, 1], c), at(bu[:, 1], c), self.phase(1, c), ALU.mult))
        link(tt(rot[:, 0, :, :n], rot[:, 0, :, :n], rot[:, 1, :, :n], ALU.add))
        dve.wait_ge(self.pin, 2 * (c + 1))
        tt(rot[:, 1, :, :n], rot_p[:, 1, :, :n], rot_p[:, 0, :, :n], ALU.subtract).then_inc(self.vin, 1)
        dve.wait_ge(self.vin, c + 1)
        if c == NCH:
            first = rot[:, :, :, 0:64:NQ]
            for ri in range(2):
                last = tt(first[:, ri], first[:, ri], self.h0[:, ri], ALU.add)
            link(last)
        for ri in range(2):
            for mm in range(self.M):
                data0 = self.magp[:, mm, :] if c < NCH else self.mags[:, mm, :]
                init = h[:, ri, mm, P - 1:P] if 0 < c < NCH else 0.0
                last = dve.tensor_tensor_scan(rot[:, ri, mm, :n], data0[:, :n], rot[:, ri, mm, :n], init,
                                              ALU.mult, ALU.add)
        last.then_inc(self.scanned, 1)
        dve.wait_ge(self.scanned, c + 1)
        if c:
            dve.wait_ge(self.yprod, c)
        if c == NCH:
            dve.wait_ge(self.fin_ready, 1)
        tt(at(h[:, 0], c), at(rot[:, 0], c), self.phase(0, c), ALU.mult)
        link(tt(at(h[:, 1], c), at(rot[:, 1], c), self.phase(1, c), ALU.mult))
        link(tt(h[:, 0, :, :n], h[:, 0, :, :n], h[:, 1, :, :n], ALU.subtract))
        dve.wait_ge(self.pout, 2 * (c + 1))
        tt(h[:, 1, :, :n], rot_p[:, 0, :, :n], rot_p[:, 1, :, :n], ALU.add).then_inc(self.h_ready, 1)
        dve.wait_ge(self.h_ready, c + 1)
        if c:
            self.y_out_of(dve, c - 1)


    def tensor(self, pe, u):
        m, M, rot = self.m, self.M, self.rot
        if u == 5:
            for ri in range(2):
                pe.wait_ge(self.bb_made, ri + 1)
                for mm in range(M):
                    last = pe.transpose(m.ps[:, 2 * ri + mm // 4, (mm % 4) * P:(mm % 4) * P + P], rot[:, ri, mm, :], m.ident[:])
                last.then_inc(self.bbT_turned, 1)
            pe.wait_ge(self.bbT_out, 2)
            pe.wait_ge(self.neg_made, 1)
            pe.wait_ge(self.u_out[0], 3)
            pe.wait_ge(self.u_out[1], 3)
            self.bu_products(pe, 0)
        c = (u - 6) // 2
        if u >= 6 and u % 2 == 0 and c + 1 < self.CH:
            self.bu_products(pe, c + 1)
        if u >= 7 and u % 2:
            self.y_products(pe, c)
        if u == 23:
            for g, (o, w) in enumerate(GROUPS_N):
                pe.wait_ge(self.gelu_made, g + 1)
                if g >= 2:
                    pe.wait_ge(self.sig_made, g - 1)
                for co in range(2):
                    for kt in range(2):
                        last = pe.matmul(m.ps[:, 2 * (g % 2) + co, :w], self.wglu[:, kt, co * P:co * P + P],
                                         self.gelu[:, kt, o:o + w], start=kt == 0, stop=kt == 1)
                last.then_inc(self.glu, 1)

    def bu_products(self, pe, c):
        n = self.W[c]
        if c:
            pe.wait_ge(self.bu_out, 2 * c)
        for ri in range(2):
            for mm in range(self.M):
                last = pe.matmul(self.m.ps[:, 2 * ri + mm // 4, (mm % 4) * P:(mm % 4) * P + n], self.bbT[:, ri, mm, :],
                                 self.m.uT[:, mm // 4, c * P:c * P + n], start=True, stop=True)
        last.then_inc(self.bu_prod, 1)

    def y_products(self, pe, c):
        n = self.W[c]
        pe.wait_ge(self.h_ready, c + 1)
        if c:
            pe.wait_ge(self.y_out, 2 * c)
        for ct in range(2):
            for i in range(8):
                mm, ri = 4 * ct + i // 2, i % 2
                last = pe.matmul(self.m.ps[:, 4, ct * P:ct * P + n], self.cpad[:, ri, mm, :], self.h[:, ri, mm, :n],
                                 start=i == 0, stop=i == 7)
        last.then_inc(self.yprod, 1)



def delta_net(nc, m):
    with ExitStack() as ctx:
        sb = lambda n, s: ctx.enter_context(nc.sbuf_tensor(f"dn_{n}", s, F32))
        sem = lambda n: m.sem(f"dn_{n}")
        H = 4
        NT = TILES
        flat_hT = m.mixT[:].rearrange("p k n -> p (k n)")
        conv, convs = m.mixT[:, 0:6, :], m.convs
        names = ["ones", "ones_s", "upto", "upto_s", "neg", "neg_s", "level", "seq_row"]
        C = {n: sb(n, [P, CONST_AT[n][1]]) for n in names}
        alog, dtb, normw = sb("alog", [P, H]), sb("dtb", [P, H]), sb("normw", [P, HD])
        minus_half = sb("minus_half", [P, NT * H])
        gate = sb("gate", [P, 12, NT, H])
        X, GG, BETA, GC, GL, NGC, EGC, EGL, EDEC, T0, T1, T2 = range(12)
        gm = sb("gm", [64, NB, H])
        egl_s = sb("egl_s", [P, NB, H])
        o_all = sb("o", [P, NT, 256])
        qk = sb("qk", [P, 2, 512])
        sq = sb("sq", [P, 512])
        ssq = sb("ssq", [P, 2, 8])
        rnorm = sb("rnorm", [P, 2, 8])
        kb, kbg, qg = sb("kb", [P, 256]), sb("kbg", [P, 4, 256]), sb("qg", [P, 256])
        kdec, vb = sb("kdec", [P, 4, 256]), sb("vb", [P, 4, 256])
        featT = sb("featT", [P, 6, P])
        qgT = sb("qgT", [P, 4, 2, P])
        decay = sb("decay", [P, H, P])
        AT, aqkT = sb("AT", [P, 4, H, P]), sb("aqkT", [P, 4, H, P])
        B, U, T, TT = (sb(n, [P, 2, H, P]) for n in ("B", "U", "T", "TT"))
        wT = sb("wT", [P, 2, 2, P])
        S = sb("S", [P, 2, P])
        vnew = sb("vnew", [P, 256])

        pages = ctx.enter_context(nc.sbuf_tensor("pages", [1, NB * PAGES], I32))
        tables, params, pages_loaded = sem("tables"), sem("params"), sem("pages_loaded")
        vec, vec_pool, vec_act = sem("vec"), sem("vec_pool"), sem("vec_act")
        x_ready, ex_ready, lnin, ln_ready, g_ready = (sem(n) for n in ("x_ready", "ex_ready", "lnin", "ln_ready", "g_ready"))
        sums, sums_out, gexp = sem("sums"), sem("sums_out"), sem("gexp")
        raw, qk_out, vb_out = sem("raw"), sem("qk_out"), sem("vb_out")
        ssq_ready, rnorm_ready, normed = sem("ssq_ready"), sem("rnorm_ready"), sem("normed")
        scaled, turned, feat_out = sem("scaled"), sem("turned"), sem("feat_out")
        drow, decay_ready = sem("drow"), sem("decay_ready")
        gram, a_ready = sem("gram"), sem("a_ready")
        b_ready, bt, u_ready, tut, t_ready = sem("b_ready"), sem("bt"), sem("u_ready"), sem("tut"), sem("t_ready")
        wprod, w_ready = sem("wprod"), sem("w_ready")
        vprod, v_ready, oprod, o_out, sprod, s_ready = (sem(n) for n in ("vprod", "v_ready", "oprod", "o_out", "sprod", "s_ready"))
        s_zero, stored, s_in = sem("s_zero"), sem("stored"), sem("s_in")
        osq, orn, fin, fturn, fout, zsilu = (sem(n) for n in ("osq", "orn", "fin", "fturn", "fout", "zsilu"))
        masked, ss_ready = sem("masked"), sem("ss_ready")
        Ss = flat_hT[:, :NB * 2 * P].rearrange("p (b c n) -> p b c n", b=NB, c=2)
        seq_col = flat_hT[:, NB * 2 * P:NB * 2 * P + CONST_AT["seq_col"][1]]
        wTm = B[:].rearrange("p a h n -> p (a h n)").rearrange("p (c b n) -> p c b n", c=2, b=NB)
        qgm = U[:].rearrange("p a h n -> p (a h n)").rearrange("p (c b n) -> p c b n", c=2, b=NB)

        def kdecm(b):
            t = (AT if b < 4 else T)[:].rearrange("p a h n -> p (a h n)")
            return t[:64, (b % 4) * 256:(b % 4) * 256 + 256]

        def order(k, s):
            if k == TS:
                return TS * LEVELS + s + 1
            return (k // 2) * 2 * LEVELS + 2 * s + k % 2 + 1

        def order1(k, s):
            if k == TS:
                return TS * (LEVELS - 1) + s
            return (k // 2) * 2 * (LEVELS - 1) + 2 * (s - 1) + k % 2 + 1

        def pairs():
            return [(0, 1), (2, 3), (4, 5), (6, 7), (TS,)]

        def after_level(p, s, stages):
            if p + 1 < len(pairs()):
                a, b = (pairs()[p + 1] + (None,))[:2]
                if s in stages:
                    stages[s](a)
                if s - 4 in stages and b is not None:
                    stages[s - 4](b)

        def second_of(p):
            return pairs()[p + 1][1] if p + 1 < len(pairs()) and len(pairs()[p + 1]) > 1 else None

        def levels(k):
            return SLEVELS if k == TS else LEVELS

        def heads(t):
            return t.rearrange("p (h n) -> p h n", h=H)

        with nc.Block() as block:
            @block.sync
            def _(sp):
                sp.dma_start(alog[:], m.a_log).then_inc(params, 16)
                sp.dma_start(dtb[:], m.dt_bias).then_inc(params, 16)
                sp.dma_start(normw[:], m.norm_w).then_inc(params, 16)
                for n in names:
                    at, w = CONST_AT[n]
                    sp.dma_start(C[n][:], m.const[:, at:at + w]).then_inc(tables, 16)
                caches_loaded = m.sem("caches_loaded")
                sp.dma_start(pages[:], m.a["page_table"]).then_inc(pages_loaded, 16)
                sp.wait_ge(pages_loaded, 16)
                for j in range(NB * PAGES):
                    page = sp.value_load(pages[0:1, j:j + 1], min_val=0, max_val=m.a["cache_nsa"].shape[0] - 1)
                    sp.dma_start(m.ck[:, j, :], m.a["cache_nsa"][bass.DynSlice(page, 1)].rearrange("a p n -> p (a n)")
                                 ).then_inc(caches_loaded, 16)
                sp.wait_ge(raw, NT)
                sp.dma_start(Ss, m.state_dn).then_inc(s_in, 16)
                at, w = CONST_AT["seq_col"]
                sp.dma_start(seq_col, m.const[:, at:at + w]).then_inc(s_in, 16)
                sp.wait_ge(s_ready, TS)
                for h in range(2):
                    half = slice(64 * h, 64 * h + 64)
                    sp.dma_start(m.dn_prompt[half], S[half, :, half]).then_inc(stored, 16)
                sp.wait_ge(ss_ready, H)
                for h in range(2):
                    half = slice(64 * h, 64 * h + 64)
                    for c in range(2):
                        sp.dma_start(m.dn_sample[half, :, c], Ss[half, :, c, half]).then_inc(stored, 16)
                sp.wait_ge(stored, 16 * 6)
                sp.wait_ge(m.sem("proj_stored"), 16 * STORES_OF_INPUT)

            @block.gpsimd
            def _(pool):
                link = Link(pool, vec_pool)
                link(pool.memset(o_all[64:128, TS, :], 0.0))
                link(pool.memset(minus_half[:], -0.5))
                pool.memset(S[:], 0.0).then_inc(s_zero, 1)

                def scale(k):
                    n, x, y = ROWS[k], k % 2, k % 4
                    bc = lambda c: gate[:n, c, k, :].unsqueeze(2).to_broadcast([n, H, HD])
                    pool.wait_ge(ssq_ready, k + 1)
                    pool.tensor_tensor(rnorm[:n, x, :], ssq[:n, x, :], minus_half[:n, :8], ALU.pow).then_inc(rnorm_ready, 1)
                    pool.wait_ge(normed, k + 1)
                    pool.wait_ge(gexp, 3)
                    if k:
                        pool.wait_ge(turned, k)
                    kn = heads(qk[:n, x, 256:512])
                    pool.tensor_tensor(heads(kb[:n, :]), kn, bc(BETA), ALU.mult).then_inc(scaled, 1)
                    pool.tensor_tensor(heads(qg[:n, :]), heads(qk[:n, x, 0:256]), bc(EGC), ALU.mult).then_inc(scaled, 1)
                    if k >= 4:
                        pool.wait_ge(wprod, k - 3)
                        pool.wait_ge(sprod, k - 3)
                    pool.tensor_tensor(heads(kdec[:n, y, :]), kn, bc(EDEC), ALU.mult).then_inc(scaled, 1)
                    pool.wait_ge(scaled, 4 * k + 1)
                    pool.tensor_tensor(heads(kbg[:n, y, :]), heads(kb[:n, :]), bc(EGC), ALU.mult).then_inc(scaled, 1)

                scale(0)
                scale(1)
                for p, pair in enumerate(pairs()):
                    for s in range(levels(pair[0])):
                        for k in pair:
                            n, x = ROWS[k], k % 2
                            pool.wait_ge(a_ready, 4 * (k + 1))
                            if s:
                                pool.wait_ge(bt, order(k, s - 1))
                            elif k >= 2:
                                pool.wait_ge(bt, order(k - 2, LEVELS - 1))
                            if s == 1:
                                pool.wait_ge(t_ready, order(k, 0))
                            mask = C["level"][:n, s * P:s * P + n].unsqueeze(1).to_broadcast([n, H, n])
                            pool.tensor_tensor(B[:n, x, :, :n], AT[:n, k % 4, :, :n], mask, ALU.mult).then_inc(b_ready, 1)
                        after_level(p, s, {1: scale})
                for i, (t0, t1) in enumerate(((0, TS), (TS, NT))):
                    part = lambda c: gate[:, c, t0:t1].rearrange("p t h -> p (t h)")
                    pool.wait_ge(osq, i + 1)
                    pool.tensor_tensor(part(T1), part(T0), minus_half[:, :H * (t1 - t0)], ALU.pow).then_inc(orn, 1)

            @block.scalar
            def _(act):
                act.activation(m.small[:, :, 32:], m.small[:, :, 32:], ACT.Silu).then_inc(zsilu, 1)
                act.wait_ge(x_ready, 1)
                act.activation(gate[:, T1], gate[:, T0], ACT.Exp).then_inc(ex_ready, 1)
                act.activation(gate[:, T2], m.small[:, :, 28:32], ACT.Exp, scale=-1.0).then_inc(ex_ready, 1)
                act.activation(alog[:], alog[:], ACT.Exp).then_inc(ex_ready, 1)
                act.wait_ge(lnin, 1)
                act.activation(gate[:, T1], gate[:, T1], ACT.Ln, bias=1.0).then_inc(ln_ready, 1)
                act.wait_ge(sums_out, 1)
                act.activation(gate[:, EGC], gate[:, GC], ACT.Exp).then_inc(gexp, 1)
                act.activation(gate[:, EGL], gate[:, GL], ACT.Exp).then_inc(gexp, 1)
                act.activation(gate[:, EDEC], gate[:, T0], ACT.Exp).then_inc(gexp, 1)
                act.activation(egl_s[:], m.ps[:, 0, 128:160].rearrange("p (b h) -> p b h", b=NB), ACT.Exp).then_inc(gexp, 1)

                def squares_of(k):
                    n, x = ROWS[k], k % 2
                    act.wait_ge(raw, k + 1)
                    if k:
                        act.wait_ge(ssq_ready, k)
                    if k >= 2:
                        act.wait_ge(scaled, 4 * (k - 1))
                        act.wait_ge(turned, k - 1)
                    act.activation(sq[:n, :], m.ps[:n, 6, :], ACT.Square).then_inc(qk_out, 1)
                    act.activation(qk[:n, x, :], m.ps[:n, 6, :], ACT.Copy).then_inc(qk_out, 1)

                def features_of(k):
                    n, y = ROWS[k], k % 4
                    act.wait_ge(turned, k + 1)
                    if k:
                        act.wait_ge(gram, 2 * k)
                    if k >= 4:
                        act.wait_ge(oprod, k - 3)
                    act.activation(featT[:, 0:4, :n], heads(m.ps[:, 7, :])[:, :, :n], ACT.Copy).then_inc(feat_out, 1)
                    act.activation(featT[:, 4:6, :n], heads(m.ps[:, 6, :])[:, 0:2, :n], ACT.Copy).then_inc(feat_out, 1)
                    act.activation(qgT[:, y, :, :n], heads(m.ps[:, 6, :])[:, 2:4, :n], ACT.Copy).then_inc(feat_out, 1)

                def decay_of(k):
                    n = ROWS[k]
                    act.wait_ge(drow, k + 1)
                    if k:
                        act.wait_ge(a_ready, 4 * k)
                    for h in range(H):
                        act.activation(decay[:n, h, :n], m.ps[:n, 6, h * P:h * P + n], ACT.Exp,
                                       bias=gate[:n, NGC, k, h:h + 1]).then_inc(decay_ready, 1)

                for k in pairs()[0]:
                    squares_of(k)
                    features_of(k)
                    decay_of(k)
                for p, pair in enumerate(pairs()):
                    for s in range(levels(pair[0])):
                        for k in pair:
                            if s == 0:
                                continue
                            n, x = ROWS[k], k % 2
                            act.wait_ge(bt, order(k, s))
                            if s > 1:
                                act.wait_ge(tut, order1(k, s - 1))
                            elif k >= 2:
                                act.wait_ge(tut, order1(k - 2, LEVELS - 1))
                            act.activation(U[:n, x, :, :n], heads(m.ps[:n, 3 * x, :])[:, :, :n], ACT.Copy).then_inc(u_ready, 1)
                        after_level(p, s, {0: squares_of, 1: features_of, 2: decay_of})
                    for k in pair:
                        n, x = ROWS[k], k % 2
                        act.wait_ge(wprod, k + 1)
                        for h in range(2):
                            act.activation(wT[64 * h:64 * h + 64, x, :, :n],
                                           heads(m.ps[64 * h:64 * h + 64, 3 * x, :])[:, h::2, :n],
                                           ACT.Copy, scale=-1.0).then_inc(w_ready, 1)
                        act.wait_ge(vprod, k + 1)
                        if k:
                            act.wait_ge(oprod, k)
                        act.activation(vnew[:n, :], m.ps[:n, 3 * x + 1, :256], ACT.Copy).then_inc(v_ready, 1)
                for k in range(NT):
                    act.wait_ge(fturn, k + 1)
                    act.activation(m.mixT[:, 4:6, k * P:k * P + ROWS[k]],
                                   heads(m.ps[:, k % 2, :])[:, 0:2, :ROWS[k]], ACT.Copy).then_inc(fout, 1)

            @block.vector
            def _(dve):
                link = Link(dve, vec)
                dve.wait_ge(params, 48)
                bcH = lambda t: t[:].unsqueeze(1).to_broadcast([P, NT, H])
                link(dve.tensor_tensor(gate[:, X], m.small[:, :, 24:28], bcH(dtb), ALU.add))
                link(dve.tensor_scalar(gate[:, T1], gate[:, X], -1.0, None, ALU.mult))
                dve.tensor_tensor(gate[:, T0], gate[:, X], gate[:, T1], ALU.min).then_inc(x_ready, 1)
                dve.wait_ge(ex_ready, 3)
                link(dve.tensor_scalar(gate[:, T2], gate[:, T2], 1.0, None, ALU.add))
                dve.reciprocal(gate[:, BETA], gate[:, T2]).then_inc(lnin, 1)
                dve.wait_ge(ln_ready, 1)
                link(dve.tensor_scalar(gate[:, X], gate[:, X], 0.0, None, ALU.max))
                link(dve.tensor_tensor(gate[:, X], gate[:, X], gate[:, T1], ALU.add))
                link(dve.tensor_tensor(gate[:, X], gate[:, X], bcH(alog), ALU.mult))
                link(dve.tensor_scalar(gate[:, GG], gate[:, X], -1.0, None, ALU.mult))
                dve.wait_ge(tables, 16 * len(names))
                dve.tensor_tensor(gm[:], gate[:64, GG, TS, :].unsqueeze(1).to_broadcast([64, NB, H]),
                                  C["seq_row"][:64, :].unsqueeze(2).to_broadcast([64, NB, H]), ALU.mult).then_inc(g_ready, 1)
                dve.wait_ge(sums, 1)
                link(dve.tensor_copy(gate[:, GC], m.ps[:, 0, 0:36].rearrange("p (t h) -> p t h", t=NT)))
                link(dve.tensor_copy(gate[:, GL], m.ps[:, 0, 64:100].rearrange("p (t h) -> p t h", t=NT)))
                link(dve.tensor_scalar(gate[:, NGC], gate[:, GC], -1.0, None, ALU.mult))
                dve.tensor_tensor(gate[:, T0], gate[:, GL], gate[:, GC], ALU.subtract).then_inc(sums_out, 1)

                def normalise(k):
                    n, x, y = ROWS[k], k % 2, k % 4
                    dve.wait_ge(raw, k + 1)
                    if k >= 4:
                        dve.wait_ge(vprod, k - 3)
                    dve.tensor_tensor(heads(vb[:n, y, :]), heads(m.ps[:n, 7, 0:256]),
                                      gate[:n, BETA, k, :].unsqueeze(2).to_broadcast([n, H, HD]),
                                      ALU.mult).then_inc(vb_out, 1)
                    dve.wait_ge(qk_out, 2 * k + 2)
                    link(dve.tensor_reduce(ssq[:n, x, :], sq[:n, :].rearrange("p (h d) -> p h d", h=8), AX.X, ALU.add))
                    link(dve.tensor_scalar(ssq[:n, x, :], ssq[:n, x, :], 1e-6, None, ALU.add))
                    dve.tensor_scalar(ssq[:n, x, 0:4], ssq[:n, x, 0:4], 64.0, None, ALU.mult).then_inc(ssq_ready, 1)
                    dve.wait_ge(rnorm_ready, k + 1)
                    v = qk[:n, x, :].rearrange("p (h d) -> p h d", h=8)
                    dve.tensor_tensor(v, v, rnorm[:n, x, :].unsqueeze(2).to_broadcast([n, 8, HD]),
                                      ALU.mult).then_inc(normed, 1)

                def decayed(k, h):
                    n, y = ROWS[k], k % 4
                    dve.wait_ge(gram, 2 * k + 1 + h)
                    dve.wait_ge(decay_ready, 4 * (k + 1))
                    bank = heads(m.ps[:n, (7, 6)[h], :])
                    dve.tensor_tensor(AT[:n, y, h::2, :n], bank[:, 0:2, :n], decay[:n, h::2, :n], ALU.mult).then_inc(a_ready, 1)
                    dve.tensor_tensor(aqkT[:n, y, h::2, :n], bank[:, 2:4, :n], decay[:n, h::2, :n], ALU.mult).then_inc(a_ready, 1)

                for k in pairs()[0]:
                    normalise(k)
                    decayed(k, 0)
                    decayed(k, 1)
                for p, pair in enumerate(pairs()):
                    for s in range(levels(pair[0])):
                        for k in pair:
                            n, x = ROWS[k], k % 2
                            if s == 0:
                                eye = m.ident[:n, :n].unsqueeze(1).to_broadcast([n, H, n])
                                dve.wait_ge(b_ready, order(k, 0))
                                link(dve.tensor_tensor(TT[:n, x, :, :n], eye, B[:n, x, :, :n], ALU.subtract))
                                dve.wait_ge(bt, order(k, 0))
                                dve.tensor_tensor(T[:n, x, :, :n], eye, heads(m.ps[:n, 3 * x, :])[:, :, :n],
                                                  ALU.subtract).then_inc(t_ready, 1)
                                continue
                            dve.wait_ge(tut, order1(k, s))
                            if s < levels(k) - 1:
                                link(dve.tensor_tensor(T[:n, x, :, :n], T[:n, x, :, :n],
                                                       heads(m.ps[:n, 3 * x + 1, :])[:, :, :n], ALU.subtract))
                            dve.tensor_tensor(TT[:n, x, :, :n], TT[:n, x, :, :n],
                                              heads(m.ps[:n, 3 * x + 2, :])[:, :, :n], ALU.subtract).then_inc(t_ready, 1)
                        after_level(p, s, {0: normalise, 2: lambda k: decayed(k, 0), 3: lambda k: decayed(k, 1)})
                    for k in pair:
                        if k == TS:
                            continue
                        x = k % 2
                        dve.wait_ge(sprod, k + 1)
                        for h in range(H):
                            half = slice(64 * (h % 2), 64 * (h % 2) + 64)
                            blk = S[half, h // 2, half]
                            last = dve.scalar_tensor_tensor(blk, blk, gate[half, EGL, k, h:h + 1],
                                                            m.ps[half, 3 * x, (h // 2) * P + 64 * (h % 2):(h // 2) * P + 64 * (h % 2) + 64],
                                                            ALU.mult, ALU.add)
                        last.then_inc(s_ready, 1)
                        dve.wait_ge(oprod, k + 1)
                        dve.tensor_copy(o_all[:, k, :], m.ps[:, 3 * x + 2, :256]).then_inc(o_out, 1)
                        if k % 2 == 0 and second_of(p) is not None:
                            decayed(second_of(p), 1)

                def finish(i, t0, t1):
                    dve.wait_ge(o_out, t1)
                    dve.wait_ge(vec_pool, 2)
                    part = o_all[:, t0:t1, :].rearrange("p t n -> p (t n)")
                    by_head = part.rearrange("p (a d) -> p a d", d=HD)
                    at = NB * 2 * P + CONST_AT["seq_col"][1]
                    squares = flat_hT[:, at:at + (t1 - t0) * 256]
                    a = H * (t1 - t0)
                    ms, rn = (gate[:, c, t0:t1].rearrange("p t h -> p (t h)") for c in (T0, T1))
                    link(dve.tensor_tensor(squares, part, part, ALU.mult))
                    link(dve.tensor_reduce(ms, squares.rearrange("p (a d) -> p a d", d=HD), AX.X, ALU.add))
                    dve.tensor_scalar(ms, ms, 1.0 / HD, EPS, ALU.mult, ALU.add).then_inc(osq, 1)
                    link(dve.tensor_tensor(by_head, by_head, normw[:].unsqueeze(1).to_broadcast([P, a, HD]), ALU.mult))
                    dve.wait_ge(orn, i + 1)
                    link(dve.tensor_tensor(by_head, by_head, rn.unsqueeze(2).to_broadcast([P, a, HD]), ALU.mult))
                    dve.wait_ge(zsilu, 1)
                    dve.tensor_tensor(o_all[:, t0:t1, :], o_all[:, t0:t1, :], m.small[:, t0:t1, 32:], ALU.mult).then_inc(fin, 1)

                n = NB * NQ
                dve.wait_ge(w_ready, 2 * NT)
                dve.wait_ge(s_in, 32)
                col = seq_col.rearrange("p (b n) -> p b n", b=NB)
                for c in range(2):
                    dve.tensor_tensor(wTm[:, c], wT[:, 0, c, :n].unsqueeze(1).to_broadcast([P, NB, n]), col, ALU.mult)
                    dve.tensor_tensor(qgm[:, c], qgT[:, TS % 4, c, :n].unsqueeze(1).to_broadcast([P, NB, n]), col, ALU.mult)
                for b in range(NB):
                    last = dve.tensor_scalar(kdecm(b), kdec[:n, TS % 4, :], C["seq_row"][:n, b:b + 1], None, ALU.mult)
                last.then_inc(masked, 1)
                finish(0, 0, TS)
                dve.wait_ge(sprod, NT)
                for h in range(H):
                    half = slice(64 * (h % 2), 64 * (h % 2) + 64)
                    blk = Ss[half, :, h // 2, half]
                    link(dve.tensor_tensor(blk, blk, egl_s[half, :, h:h + 1].to_broadcast([64, NB, 64]), ALU.mult))
                    upd = m.ps[half, 4:8, :].rearrange("p a n -> p (a n)").rearrange("p (b c n) -> p b c n", b=NB, c=2)
                    dve.tensor_tensor(blk, blk, upd[:, :, h // 2, half], ALU.add).then_inc(ss_ready, 1)
                dve.wait_ge(oprod, NT)
                dve.tensor_copy(o_all[:n, TS, :], m.ps[:n, 2, :256]).then_inc(o_out, 1)
                finish(1, TS, NT)

            @block.tensor
            def _(pe):
                pe.wait_ge(tables, 16 * len(names))
                pe.wait_ge(g_ready, 1)
                g = gate[:, GG, 0:TS, :].rearrange("p t h -> p (t h)")
                bank = m.ps[:, 0, :]
                pe.matmul(bank[:, 0:32], C["upto"][:], g, start=True, stop=True)
                pe.matmul(bank[:, 32:36], C["upto_s"][:64, :], gate[:64, GG, TS, :], start=True, stop=True)
                pe.matmul(bank[:, 64:96], C["ones"][:], g, start=True, stop=True)
                pe.matmul(bank[:, 96:100], C["ones_s"][:64, :], gate[:64, GG, TS, :], start=True, stop=True)
                pe.matmul(bank[:, 128:160], C["ones"][:64, :], gm[:].rearrange("p b h -> p (b h)"),
                          start=True, stop=True).then_inc(sums, 1)
                pe.wait_ge(gexp, 4)

                def rows_of(k):
                    n = ROWS[k]
                    if k:
                        pe.wait_ge(a_ready, 4 * k)
                    for f in range(6):
                        src = conv[:, f, k * P:(k + 1) * P] if k < TS else convs[:, f, :]
                        last = pe.transpose(m.ps[:n, 6 + f // 4, (f % 4) * P:(f % 4) * P + P], src, m.ident[:])
                    last.then_inc(raw, 1)

                def turn(k):
                    n, x = ROWS[k], k % 2
                    pe.wait_ge(normed, k + 1)
                    pe.wait_ge(scaled, 4 * k + 2)
                    pe.wait_ge(qk_out, 2 * k + 2)
                    pe.wait_ge(vb_out, k + 1)
                    for c, src in enumerate((qk[:n, x, 0:128], qk[:n, x, 128:256], qk[:n, x, 256:384], qk[:n, x, 384:512],
                                             kb[:n, 0:128], kb[:n, 128:256], qg[:n, 0:128], qg[:n, 128:256])):
                        last = pe.transpose(m.ps[:, 7 - c // 4, (c % 4) * P:(c % 4) * P + n], src, m.ident[:n, :n])
                    last.then_inc(turned, 1)

                def grams(k, heads_of, bank):
                    n = ROWS[k]
                    for i, h in enumerate(heads_of):
                        half = slice(64 * (h % 2), 64 * (h % 2) + 64)
                        kT = featT[half, 2 + h // 2, :n]
                        pe.matmul(bank[:, i * P:i * P + n], kT, featT[half, 4 + h // 2, :n], start=True, stop=True)
                        last = pe.matmul(bank[:, (2 + i) * P:(2 + i) * P + n], kT, featT[half, h // 2, :n], start=True, stop=True)
                    last.then_inc(gram, 1)

                def even_grams(k):
                    n = ROWS[k]
                    pe.wait_ge(feat_out, 3 * k + 3)
                    for h in range(H):
                        row = m.ps[:n, 6, h * P:h * P + n]
                        pe.matmul(row, gate[:n, GG, k, h:h + 1].to_broadcast([n, n]),
                                  C["upto" if k < TS else "upto_s"][:n, :n], start=True, stop=False)
                        last = pe.matmul(row, m.ident[:n, :n], C["neg" if k < TS else "neg_s"][:n, :n], start=False, stop=True)
                    last.then_inc(drow, 1)
                    grams(k, (0, 2), m.ps[:n, 7, :])

                def odd_grams(k):
                    pe.wait_ge(decay_ready, 4 * (k + 1))
                    grams(k, (1, 3), m.ps[:ROWS[k], 6, :])

                for k in pairs()[0]:
                    rows_of(k)
                    turn(k)
                    even_grams(k)
                    odd_grams(k)
                for p, pair in enumerate(pairs()):
                    for s in range(levels(pair[0])):
                        for k in pair:
                            n, x = ROWS[k], k % 2
                            pe.wait_ge(b_ready, order(k, s))
                            if s:
                                pe.wait_ge(t_ready, order(k, s - 1))
                            elif k >= 2:
                                pe.wait_ge(v_ready, k - 1)
                                pe.wait_ge(o_out, k - 1)
                                pe.wait_ge(s_ready, k - 1)
                                pe.wait_ge(w_ready, 2 * (k - 1))
                            for h in range(H):
                                last = pe.matmul(m.ps[:n, 3 * x, h * P:h * P + n], B[:n, x, h, :n],
                                                 T[:n, x, h, :n] if s else m.ident[:n, :n], start=True, stop=True)
                            last.then_inc(bt, 1)
                        for k in pair:
                            if s == 0:
                                continue
                            n, x = ROWS[k], k % 2
                            pe.wait_ge(u_ready, order1(k, s))
                            for h in range(H):
                                if s < levels(k) - 1:
                                    pe.matmul(m.ps[:n, 3 * x + 1, h * P:h * P + n], TT[:n, x, h, :n], U[:n, x, h, :n], start=True, stop=True)
                                last = pe.matmul(m.ps[:n, 3 * x + 2, h * P:h * P + n], U[:n, x, h, :n], TT[:n, x, h, :n], start=True, stop=True)
                            last.then_inc(tut, 1)
                        after_level(p, s, {0: rows_of, 1: turn, 2: even_grams, 3: odd_grams})
                    for k in pair:
                        n, x = ROWS[k], k % 2
                        pe.wait_ge(t_ready, order(k, levels(k) - 1))
                        pe.wait_ge(scaled, 4 * k + 4)
                        for h in range(H):
                            last = pe.matmul(m.ps[:, 3 * x, h * P:h * P + n], kbg[:n, k % 4, (h // 2) * P:(h // 2) * P + P],
                                             TT[:n, x, h, :n], start=True, stop=True)
                        last.then_inc(wprod, 1)
                        if k == TS:
                            n = NB * NQ
                            vbank, obank = m.ps[:n, 1, :], m.ps[:n, 2, :]
                            pe.wait_ge(masked, 1)
                            pe.wait_ge(s_in, 32)
                            for h in range(H):
                                pe.matmul(vbank[:, h * HD:(h + 1) * HD], TT[:n, x, h, :n], vb[:n, k % 4, h * HD:(h + 1) * HD],
                                          start=h == 0, stop=False, skip_group_check=True)
                            for b in range(NB):
                                for c in range(2):
                                    last = pe.matmul(vbank[:, c * P:(c + 1) * P], wTm[:, c, b, :], Ss[:, b, c, :],
                                                     start=False, stop=b == NB - 1, skip_group_check=True)
                            last.then_inc(vprod, 1)
                            for b in range(NB):
                                for c in range(2):
                                    pe.matmul(obank[:, c * P:(c + 1) * P], qgm[:, c, b, :], Ss[:, b, c, :],
                                              start=b + c == 0, stop=False, skip_group_check=True)
                            pe.wait_ge(v_ready, NT)
                            pe.wait_ge(v_ready, TS)
                            pe.wait_ge(o_out, TS)
                            pe.wait_ge(s_ready, TS)
                            for b in range(NB):
                                for c in range(2):
                                    last = pe.matmul(m.ps[:, 4 + b // 2, (b % 2) * 256 + c * P:(b % 2) * 256 + (c + 1) * P],
                                                     kdecm(b)[:, c * P:(c + 1) * P], vnew[:n, c * P:(c + 1) * P],
                                                     start=True, stop=True)
                            last.then_inc(sprod, 1)
                            for h in range(H):
                                last = pe.matmul(obank[:, h * HD:(h + 1) * HD], aqkT[:n, k % 4, h, :n], vnew[:n, h * HD:(h + 1) * HD],
                                                 start=False, stop=h == 3, skip_group_check=True)
                            last.then_inc(oprod, 1)
                            continue
                        pe.wait_ge(w_ready, 2 * (k + 1))
                        if k:
                            pe.wait_ge(s_ready, k)
                        else:
                            pe.wait_ge(s_zero, 1)
                        vbank, obank, sbank = (m.ps[:, 3 * x + c, :] for c in (1, 2, 0))
                        for h in range(H):
                            pe.matmul(vbank[:, h * HD:(h + 1) * HD], TT[:, x, h, :], vb[:, k % 4, h * HD:(h + 1) * HD],
                                      start=h == 0, stop=False, skip_group_check=True)
                        for c in range(2):
                            last = pe.matmul(vbank[:, c * P:(c + 1) * P], wT[:, x, c, :], S[:, c, :],
                                             start=False, stop=c == 1, skip_group_check=True)
                        last.then_inc(vprod, 1)
                        for c in range(2):
                            pe.matmul(obank[:, c * P:(c + 1) * P], qgT[:, k % 4, c, :], S[:, c, :],
                                      start=c == 0, stop=False, skip_group_check=True)
                        pe.wait_ge(v_ready, k + 1)
                        for c in range(2):
                            last = pe.matmul(sbank[:, c * P:(c + 1) * P], kdec[:, k % 4, c * P:(c + 1) * P],
                                             vnew[:, c * P:(c + 1) * P], start=True, stop=True)
                        last.then_inc(sprod, 1)
                        for h in range(H):
                            last = pe.matmul(obank[:, h * HD:(h + 1) * HD], aqkT[:, k % 4, h, :], vnew[:, h * HD:(h + 1) * HD],
                                             start=False, stop=h == 3, skip_group_check=True)
                        last.then_inc(oprod, 1)
                        if k % 2 == 0 and second_of(p) is not None:
                            odd_grams(second_of(p))
                for k in range(NT):
                    pe.wait_ge(fin, 1 if k < TS else 2)
                    if k >= 2:
                        pe.wait_ge(fout, k - 1)
                    for c in range(2):
                        last = pe.transpose(m.ps[:, k % 2, c * P:c * P + ROWS[k]], o_all[:ROWS[k], k, c * P:(c + 1) * P],
                                            m.ident[:ROWS[k], :ROWS[k]])
                    last.then_inc(fturn, 1)



def key_prep(nc, m, held):
    hold = lambda n, s: held.enter_context(nc.sbuf_tensor(n, s, F32))
    m.kselT, m.kwinT = hold("kselT", [P, TOK]), hold("kwinT", [P, TOK])
    m.kcT, m.vc = hold("kcT", [P, 16]), hold("vc", [16, P])
    m.wck, m.wcv = hold("wck", [P, 4]), hold("wcv", [P, 2, 62])
    with ExitStack() as ctx:
        sb = lambda n, s: ctx.enter_context(nc.sbuf_tensor(f"prep_{n}", s, F32))
        sem = lambda n: m.sem(f"prep_{n}")
        loaded, turned, pooled, out, gates = sem("loaded"), sem("turned"), sem("pooled"), sem("out"), sem("gates")
        jobs = [(KSEL, m.kselT, (0, 1, 2, 3)), (KSEL, m.kselT, (4, 5, 6, 7)),
                (KWIN, m.kwinT, (0, 1, 2, 3)), (KWIN, m.kwinT, (4, 5, 6, 7))]
        with nc.Block() as block:
            @block.sync
            def _(sp):
                sp.dma_start(m.wck[:], m.a["wck"]).then_inc(loaded, 16)
                sp.dma_start(m.wcv[:], m.a["wcv"]).then_inc(loaded, 16)
                sp.dma_start(m.cw[:], m.cache_win.rearrange("b (a p) n -> p (b a) n", p=P)).then_inc(m.sem("caches_loaded"), 16)
                sp.wait_ge(loaded, 32)

            @block.tensor
            def _(pe):
                for j, (col, _, tiles) in enumerate(jobs):
                    for c, t in enumerate(tiles):
                        last = pe.transpose(m.ps[:, j, c * P:(c + 1) * P], m.kv[:, t, col:col + P], m.ident[:])
                    last.then_inc(turned, 1)
                for c, col in enumerate((KSEL, KWIN)):
                    last = pe.transpose(m.ps[:, 4, c * P:c * P + 64], m.kv[:64, TS, col:col + P], m.ident[:64, :64])
                last.then_inc(turned, 1)
                pe.wait_ge(loaded, 32)
                for t in range(TS):
                    pe.matmul(m.ps[:, 5, 4 * t:4 * t + 4], m.kv[:, t, KCMP:KCMP + P], m.wck[:], start=True, stop=True)
                for g in range(G):
                    for t in range(TS):
                        last = pe.matmul(m.ps[:16, 6, g * HD:(g + 1) * HD], m.wcv[:, g, 30 - 2 * t:46 - 2 * t],
                                         m.kv[:, t, VCMP + g * HD:VCMP + (g + 1) * HD], start=t == 0, stop=t == TS - 1)
                last.then_inc(pooled, 1)

            @block.scalar
            def _(act):
                act.activation(m.small[:, :, 0:24], m.small[:, :, 0:24], ACT.Sigmoid).then_inc(gates, 1)
                for j, (_, dst, tiles) in enumerate(jobs):
                    act.wait_ge(turned, j + 1)
                    act.activation(dst[:, tiles[0] * P:tiles[0] * P + 512], m.ps[:, j, :], ACT.Copy).then_inc(out, 1)

            @block.vector
            def _(dve):
                dve.wait_ge(turned, 5)
                for c, dst in enumerate((m.kselT, m.kwinT)):
                    dve.tensor_copy(dst[:, SEQ:TOK], m.ps[:, 4, c * P:c * P + 64]).then_inc(out, 1)
                dve.wait_ge(pooled, 1)
                for g in range(G):
                    half = slice(64 * g, 64 * g + 64)
                    src = m.ps[half, 5, 0:32].rearrange("p (t g b) -> p t g b", t=TS, g=G)[:, :, g, :]
                    dve.tensor_copy(m.kcT[half, :].rearrange("p (t b) -> p t b", t=TS), src).then_inc(out, 1)
                dve.tensor_copy(m.vc[:], m.ps[:16, 6, 0:P]).then_inc(out, 1)


def prompt_attention(nc, m):
    with ExitStack() as ctx:
        sb = lambda n, s: ctx.enter_context(nc.sbuf_tensor(f"pa_{n}", s, F32))
        sem = lambda n: m.sem(f"pa_{n}")
        SLOTS = 8
        WIN_AT, CMP_AT, WIDTH = SEQ, SEQ + 640, SEQ + 640 + 16
        probs = sb("probs", [P, SLOTS, WIDTH])
        dsel, dwin, dcmp = sb("dsel", [P, 1024]), sb("dwin", [P, 640]), sb("dcmp", [P, 128])
        mx, nm, rs, fac = (sb(n, [P, SLOTS, 3]) for n in ("mx", "nm", "rs", "fac"))
        PTN = 4
        PT = sb("PT", [P, PTN, 512])
        (loaded, score_ready, score_out, nm_ready, exp_done, turned, pt_ready, pv_step, o_out, vec) = (
            sem(n) for n in ("loaded", "score_ready", "score_out", "nm_ready", "exp_done", "turned",
                             "pt_ready", "pv_step", "o_out", "vec"))
        vec_pool, scaled_pool, scaled_dve = sem("vec_pool"), sem("scaled_pool"), sem("scaled_dve")
        minus_one = sb("minus_one", [P, 3])
        units = [(i, g) for i in range(TS) for g in range(G)]
        RING = 4
        PARTS = 5
        POOL_HEADS = 2

        def window(i):
            f = max(0, i - WINDOW // P)
            return f, i - f + 1

        def pieces(i):
            out = [(o, min(512, (i + 1) * P - o), m.kselT, o, dsel[:, 1024 - (i + 1) * P + o:])
                   for o in range(0, (i + 1) * P, 512)]
            f, nw = window(i)
            out += [(WIN_AT + o, min(512, nw * P - o), m.kwinT, f * P + o, dwin[:, (f - i) * P + 512 + o:])
                    for o in range(0, nw * P, 512)]
            return out + [(CMP_AT, 16, m.kcT, 0, dcmp[:, 16 * i:])]

        def branches(i):
            return [(0, (i + 1) * P), (WIN_AT, window(i)[1] * P), (CMP_AT, 16)]

        def steps(n):
            i, g = units[n]
            f, nw = window(i)
            v = slice(g * HD, (g + 1) * HD)
            out = [(P * t, P, m.kv[:, t, VSEL:VSEL + P][:, v]) for t in range(i + 1)]
            out += [(WIN_AT + P * t, P, m.kv[:, f + t, VWIN:VWIN + P][:, v]) for t in range(nw)]
            return out + [(CMP_AT, 16, m.vc[:, v])]

        first_step = [0]
        for n in range(len(units)):
            first_step.append(first_step[-1] + len(steps(n)))

        def part(n, q):
            k = len(steps(n))
            return range(k * q // PARTS, k * (q + 1) // PARTS)

        with nc.Block() as block:
            @block.sync
            def _(sp):
                for name, dst in (("dist_sel", dsel), ("dist_win", dwin), ("dist_cmp", dcmp)):
                    at, w = CONST_AT[name]
                    sp.dma_start(dst[:], m.const[:, at:at + w]).then_inc(loaded, 16)
                sp.dma_start(m.out_raw[0][:], m.a["w_out"][0]).then_inc(m.out_raw[1], 16)

            @block.tensor
            def _(pe):
                count = [0]

                def scores(n, r):
                    i, g = units[n]
                    half = slice(64 * g, 64 * g + 64)
                    for _, w, keys, k0, _ in pieces(i):
                        c = count[0]
                        if c >= RING:
                            pe.wait_ge(score_out, c - RING + 1)
                        pe.matmul(m.ps[:, c % RING, :w], m.qT[half, r, i * P:(i + 1) * P], keys[half, k0:k0 + w],
                                  start=True, stop=True).then_inc(score_ready, 1)
                        count[0] += 1

                def multiply(n, s):
                    st = first_step[n] + s
                    _, k, values = steps(n)[s]
                    half = slice(64 * units[n][1], 64 * units[n][1] + 64)
                    if s == 0 and n >= 2:
                        pe.wait_ge(o_out, n - 1)
                    pe.wait_ge(pt_ready, st + 1)
                    pe.matmul(m.ps[half, 6 + n % 2, :], values, PT[:k, st % PTN, :], start=s == 0,
                              stop=s == len(steps(n)) - 1).then_inc(pv_step, 1)

                def turn(n, q):
                    if q == 0:
                        pe.wait_ge(scaled_pool, POOL_HEADS * (n + 1))
                        pe.wait_ge(scaled_dve, (R - POOL_HEADS) * (n + 1))
                    for s in part(n, q):
                        col, k, _ = steps(n)[s]
                        st = first_step[n] + s
                        if st >= 2:
                            pe.wait_ge(pt_ready, st - 1)
                        for h in range(R):
                            last = pe.transpose(m.ps[:k, 4 + st % 2, h * P:(h + 1) * P],
                                                probs[:, (R * n + h) % SLOTS, col:col + k], m.ident[:])
                        last.then_inc(turned, 1)
                        if s:
                            multiply(n, s - 1)
                    if q == PARTS - 1:
                        multiply(n, len(steps(n)) - 1)

                pe.wait_ge(loaded, 48)
                for n in range(len(units) + 1):
                    for q in range(PARTS):
                        if q < R and n < len(units):
                            scores(n, q)
                        if n:
                            turn(n - 1, q)

            @block.vector
            def _(dve):
                link = Link(dve, vec)
                count = [0]
                dve.wait_ge(loaded, 48)

                def rows(e):
                    n, r = e // R, e % R
                    i, g = units[n]
                    x = e % SLOTS
                    if n >= 2 and r == 0:
                        dve.wait_ge(turned, first_step[n - 1])
                    for col, w, _, _, table in pieces(i):
                        dve.wait_ge(score_ready, count[0] + 1)
                        last = dve.scalar_tensor_tensor(probs[:, x, col:col + w], table[:, :w], 2.0 ** -(4 * g + r + 1),
                                                        m.ps[:, count[0] % RING, :w], ALU.mult, ALU.add)
                        last.then_inc(score_out, 1)
                        count[0] += 1
                    dve.wait_ge(score_out, count[0])
                    for b, (o, w) in enumerate(branches(i)):
                        last = dve.tensor_reduce(mx[:, x, b:b + 1], probs[:, x, o:o + w], AX.X, ALU.max)
                    link(last)
                    dve.tensor_scalar(nm[:, x, :], mx[:, x, :], MFLOOR, -1.0, ALU.max, ALU.mult).then_inc(nm_ready, 1)

                def scale(e):
                    n, r = e // R, e % R
                    i, g = units[n]
                    x, h = e % SLOTS, R * g + r
                    dve.wait_ge(exp_done, e + 1)
                    link(dve.tensor_scalar(rs[:, x, :], rs[:, x, :], 1e-30, None, ALU.max))
                    link(dve.reciprocal(fac[:, x, :], rs[:, x, :]))
                    dve.tensor_tensor(fac[:, x, 0:2], fac[:, x, 0:2], m.small[:, i, 3 * h + 1:3 * h + 3], ALU.mult)
                    link(dve.tensor_tensor(fac[:, x, 2:3], fac[:, x, 2:3], m.small[:, i, 3 * h:3 * h + 1], ALU.mult))
                    for b, (o, w) in enumerate(branches(i)):
                        last = dve.tensor_scalar(probs[:, x, o:o + w], probs[:, x, o:o + w], fac[:, x, b:b + 1], None, ALU.mult)
                    last.then_inc(scaled_dve, 1)

                for e in range(R * len(units)):
                    rows(e)
                    if e % R == R - 1:
                        for x in range(R - POOL_HEADS):
                            scale(e - R + 1 + POOL_HEADS + x)

            @block.gpsimd
            def _(pool):
                link = Link(pool, vec_pool)
                link(pool.memset(minus_one[:], -1.0))
                for e in range(R * len(units)):
                    n, r = e // R, e % R
                    if r >= POOL_HEADS:
                        continue
                    i, g = units[n]
                    x, h = e % SLOTS, R * g + r
                    pool.wait_ge(exp_done, e + 1)
                    link(pool.tensor_scalar(rs[:, x, :], rs[:, x, :], 1e-30, None, ALU.max))
                    link(pool.tensor_tensor(rs[:, x, :], rs[:, x, :], minus_one[:], ALU.pow))
                    pool.tensor_tensor(fac[:, x, 0:2], m.small[:, i, 3 * h + 1:3 * h + 3], rs[:, x, 0:2], ALU.mult)
                    link(pool.tensor_tensor(fac[:, x, 2:3], m.small[:, i, 3 * h:3 * h + 1], rs[:, x, 2:3], ALU.mult))
                    for b, (o, w) in enumerate(branches(i)):
                        last = pool.tensor_scalar(probs[:, x, o:o + w], probs[:, x, o:o + w], fac[:, x, b:b + 1], None, ALU.mult)
                    last.then_inc(scaled_pool, 1)

            @block.scalar
            def _(act):
                def exps(e):
                    i, _ = units[e // R]
                    x = e % SLOTS
                    act.wait_ge(nm_ready, e + 1)
                    for b, (o, w) in enumerate(branches(i)):
                        last = act.activation(probs[:, x, o:o + w], probs[:, x, o:o + w], ACT.Exp, bias=nm[:, x, b:b + 1],
                                              accum_out=rs[:, x, b:b + 1])
                    last.then_inc(exp_done, 1)

                def copies(n, q):
                    for s in part(n, q):
                        st = first_step[n] + s
                        k = steps(n)[s][1]
                        act.wait_ge(turned, st + 1)
                        if st >= PTN:
                            act.wait_ge(pv_step, st - PTN + 1)
                        act.activation(PT[:k, st % PTN, :], m.ps[:k, 4 + st % 2, :], ACT.Copy).then_inc(pt_ready, 1)
                    if q == PARTS - 1:
                        i, g = units[n]
                        half = slice(64 * g, 64 * g + 64)
                        act.wait_ge(pv_step, first_step[n + 1])
                        act.activation(m.mixT[half, 0:4, i * P:(i + 1) * P],
                                       m.ps[half, 6 + n % 2, :].rearrange("p (h n) -> p h n", h=R), ACT.Copy).then_inc(o_out, 1)

                for n in range(len(units) + 1):
                    for q in range(PARTS):
                        if n:
                            copies(n - 1, q)
                        if q < R and n < len(units):
                            exps(R * n + q)


def sample_attention(nc, m):
    with ExitStack() as ctx:
        sb = lambda n, s: ctx.enter_context(nc.sbuf_tensor(f"sa_{n}", s, F32))
        sem = lambda n: m.sem(f"sa_{n}")
        ck, cw = m.ck, m.cw
        kT = sb("kT", [P, 2, NB * PAGES * P])
        dist, dcmp, slope = sb("dist", [P, 2, 320]), sb("dcmp", [P, 2, 32]), sb("slope", [P, 2])
        gsel = sb("gsel", [P, 2, R, P])
        qS = sb("qS", [P, NB, R, NQ])
        kcT, vc = sb("kcT", [P, 32]), sb("vc", [32, P])
        gates = sb("gates", [P, 2, 6])
        NEW = 64
        WIDTH = 2 * (PAST + NEW) + 32
        probs_of = sb("probs", [P, 2, WIDTH])
        mx, nm, rs, fac = (sb(n, [P, 4, 3]) for n in ("mx", "nm", "rs", "fac"))
        PT = sb("PT", [P, 7, P])
        BR = [(0, PAST + NEW), (PAST + NEW, PAST + NEW), (2 * (PAST + NEW), 32)]
        items = [(g, h) for h in range(2) for g in range(G)]

        def score_banks(it):
            sel, win = ((0, 1), (2, 5))[it % 2]
            return m.ps[:, sel, 0:PAST + NEW], m.ps[:, win, 0:PAST + NEW], m.ps[:, sel, PAST + NEW:PAST + NEW + 32]

        (consts, turned, t_out, pooled, pool_out, gate_prod, gate_out, sc, sc_out, nm_ready, exp_done,
         scaled, p_turned, p_out, pv, o_out, vec, q_out) = (sem(n) for n in (
             "consts", "turned", "t_out", "pooled", "pool_out", "gate_prod", "gate_out", "sc", "sc_out",
             "nm_ready", "exp_done", "scaled", "p_turned", "p_out", "pv", "o_out", "vec", "q_out"))
        jobs = [(which, j) for which in range(2) for j in range(4)]
        with nc.Block() as block:
            @block.sync
            def _(sp):
                for name, dst in (("sdist", dist[:].rearrange("p h n -> p (h n)")), ("sdist_cmp", dcmp[:].rearrange("p h n -> p (h n)")),
                                  ("sslope", slope[:]), ("gate_sel", gsel[:].rearrange("p h r n -> p (h r n)"))):
                    at, w = CONST_AT[name]
                    sp.dma_start(dst, m.const[:, at:at + w]).then_inc(consts, 16)

            @block.tensor
            def _(pe):
                pe.wait_ge(m.sem("caches_loaded"), 16 * (NB * PAGES + 1))
                pe.wait_ge(consts, 64)
                for j, (which, a) in enumerate(jobs):
                    if j >= 4:
                        pe.wait_ge(t_out, j - 3)
                    for c in range(4):
                        src = ck[:, 4 * a + c, 256:384] if which == 0 else cw[:, 4 * a + c, 0:128]
                        last = pe.transpose(m.ps[:, j % 4, c * P:(c + 1) * P], src, m.ident[:])
                    last.then_inc(turned, 1)
                for j in range(16):
                    pe.matmul(m.ps[:, 4, 4 * j:4 * j + 4], ck[:, j, 0:128], m.wck[:], start=True, stop=True)
                for g in range(G):
                    for j in range(16):
                        last = pe.matmul(m.ps[:32, 5, g * HD:(g + 1) * HD], m.wcv[:, g, 30 - 2 * j:62 - 2 * j],
                                         ck[:, j, 128 + g * HD:128 + (g + 1) * HD], start=j == 0, stop=j == 15)
                last.then_inc(pooled, 1)
                gt = m.small[:64, TS, 0:24].rearrange("p (g r c) -> p g r c", g=G, r=R)
                for h in range(2):
                    for r in range(R):
                        last = pe.matmul(m.ps[:, 6 + h, 0:6], gsel[:64, h, r, :], gt[:, :, r, :], start=r == 0, stop=r == R - 1)
                last.then_inc(gate_prod, 1)
                pe.wait_ge(t_out, 8)
                pe.wait_ge(q_out, R)
                pe.wait_ge(pool_out, 3)
                pe.wait_ge(gate_out, 1)

                def scores(it):
                    g, h = items[it]
                    half = slice(64 * g, 64 * g + 64)
                    if it >= 2:
                        pe.wait_ge(sc_out, it - 1)
                    sel, win, cmp = score_banks(it)
                    for b in range(4):
                        rows = slice(32 * b, 32 * b + 32)
                        seq = 4 * h + b
                        q = qS[half, seq].rearrange("p r q -> p (r q)")
                        pe.matmul(sel[rows, 0:PAST], q, kT[half, 0, seq * PAST:(seq + 1) * PAST], start=True, stop=True)
                        pe.matmul(sel[rows, PAST:], q, m.kselT[half, SEQ:TOK], start=True, stop=True)
                        pe.matmul(win[rows, 0:PAST], q, kT[half, 1, seq * PAST:(seq + 1) * PAST], start=True, stop=True)
                        pe.matmul(win[rows, PAST:], q, m.kwinT[half, SEQ:TOK], start=True, stop=True)
                        last = pe.matmul(cmp[rows, :], q, kcT[half, :], start=True, stop=True)
                    last.then_inc(sc, 1)

                scores(0)
                for it, (g, h) in enumerate(items):
                    half = slice(64 * g, 64 * g + 64)
                    probs = probs_of[:, it % 2]
                    if it + 1 < len(items):
                        scores(it + 1)
                    pe.wait_ge(scaled, it + 1)
                    if it:
                        pe.wait_ge(p_out, 3 * it)
                    for c, o in enumerate((0, P, 320, 320 + P)):
                        pe.transpose(m.ps[:, 6, c * P:(c + 1) * P], probs[:, o:o + P], m.ident[:])
                    for c, o in enumerate((PAST, 320 + PAST)):
                        pe.transpose(m.ps[:64, 7, c * P:(c + 1) * P], probs[:, o:o + NEW], m.ident[:])
                    pe.transpose(m.ps[:32, 7, 2 * P:3 * P], probs[:, 640:672], m.ident[:]).then_inc(p_turned, 1)
                    pe.wait_ge(p_out, 3 * (it + 1))
                    if it >= 2:
                        pe.wait_ge(o_out, it - 1)
                    acc = m.ps[half, 3 + it % 2, 0:P]
                    v = lambda t: t[:, g * HD:(g + 1) * HD]
                    args = dict(stop=False, skip_group_check=True)
                    pe.matmul(acc, v(m.kv[:64, TS, VSEL:VSEL + P]), PT[:64, 4, :], start=True, **args)
                    pe.matmul(acc, v(m.kv[:64, TS, VWIN:VWIN + P]), PT[:64, 5, :], start=False, **args)
                    pe.matmul(acc, v(vc[:, :]), PT[:32, 6, :], start=False, **args)
                    for b in range(4):
                        rows = slice(32 * b, 32 * b + 32)
                        for a in range(PAGES):
                            j = (4 * h + b) * PAGES + a
                            pe.matmul(acc[:, rows], v(ck[:, j, 384:512]), PT[:, a, rows], start=False, **args)
                            last = pe.matmul(acc[:, rows], v(cw[:, j, 128:256]), PT[:, 2 + a, rows], start=False,
                                             stop=b == 3 and a == 1, skip_group_check=True)
                    last.then_inc(pv, 1)

            @block.scalar
            def _(act):
                for r in range(R):
                    act.activation(qS[:, :, r, :], m.qT[:, r, SEQ:TOK].rearrange("p (b q) -> p b q", b=NB),
                                   ACT.Copy).then_inc(q_out, 1)
                for j, (which, a) in enumerate(jobs):
                    act.wait_ge(turned, j + 1)
                    act.activation(kT[:, which, 512 * a:512 * a + 512], m.ps[:, j % 4, :], ACT.Copy).then_inc(t_out, 1)
                def exps(it):
                    probs = probs_of[:, it % 2]
                    act.wait_ge(nm_ready, it + 1)
                    for b, (o, w) in enumerate(BR):
                        last = act.activation(probs[:, o:o + w], probs[:, o:o + w], ACT.Exp, bias=nm[:, it, b:b + 1],
                                              accum_out=rs[:, it, b:b + 1])
                    last.then_inc(exp_done, 1)

                exps(0)
                for it, (g, h) in enumerate(items):
                    if it + 1 < len(items):
                        exps(it + 1)
                    act.wait_ge(p_turned, it + 1)
                    if it:
                        act.wait_ge(pv, it)
                    act.activation(PT[:, 0:4, :], m.ps[:, 6, :].rearrange("p (c n) -> p c n", c=4), ACT.Copy).then_inc(p_out, 1)
                    act.activation(PT[:64, 4:6, :], m.ps[:64, 7, 0:256].rearrange("p (c n) -> p c n", c=2), ACT.Copy).then_inc(p_out, 1)
                    act.activation(PT[:32, 6, :], m.ps[:32, 7, 256:384], ACT.Copy).then_inc(p_out, 1)
                    act.wait_ge(pv, it + 1)
                    half = slice(64 * g, 64 * g + 64)
                    dst = m.mixT[half, 0:4, SEQ + 32 * h:SEQ + 32 * h + 32].rearrange("p r (b q) -> p r b q", b=4)
                    src = m.ps[half, 3 + it % 2, 0:P].rearrange("p (b r q) -> p r b q", b=4, r=R)
                    for r in range(R):
                        last = act.activation(dst[:, r], src[:, r], ACT.Copy)
                    last.then_inc(o_out, 1)

            @block.vector
            def _(dve):
                link = Link(dve, vec)
                dve.wait_ge(pooled, 1)
                for g in range(G):
                    half = slice(64 * g, 64 * g + 64)
                    src = m.ps[half, 4, 0:64].rearrange("p (j g b) -> p j g b", j=16, g=G)[:, :, g, :]
                    dve.tensor_copy(kcT[half, :].rearrange("p (j b) -> p j b", j=16), src).then_inc(pool_out, 1)
                dve.tensor_copy(vc[:], m.ps[:32, 5, 0:P]).then_inc(pool_out, 1)
                dve.wait_ge(gate_prod, 1)
                dve.tensor_copy(gates[:], m.ps[:, 6:8, 0:6]).then_inc(gate_out, 1)
                dve.wait_ge(gate_out, 1)
                dve.wait_ge(consts, 64)

                def rows(it):
                    g, h = items[it]
                    probs = probs_of[:, it % 2]
                    dve.wait_ge(sc, it + 1)
                    if it >= 2:
                        dve.wait_ge(p_turned, it - 1)
                    for b, ((o, w), src) in enumerate(zip(BR, score_banks(it))):
                        table = dist[:, h, :] if b < 2 else dcmp[:, h, :]
                        last = dve.scalar_tensor_tensor(probs[:, o:o + w], table, slope[:, g:g + 1], src, ALU.mult, ALU.add)
                    last.then_inc(sc_out, 1)
                    dve.wait_ge(sc_out, it + 1)
                    for b, (o, w) in enumerate(BR):
                        last = dve.tensor_reduce(mx[:, it, b:b + 1], probs[:, o:o + w], AX.X, ALU.max)
                    link(last)
                    dve.tensor_scalar(nm[:, it, :], mx[:, it, :], MFLOOR, -1.0, ALU.max, ALU.mult).then_inc(nm_ready, 1)

                rows(0)
                for it, (g, h) in enumerate(items):
                    probs = probs_of[:, it % 2]
                    if it + 1 < len(items):
                        rows(it + 1)
                    dve.wait_ge(exp_done, it + 1)
                    link(dve.tensor_scalar(rs[:, it, :], rs[:, it, :], 1e-30, None, ALU.max))
                    link(dve.reciprocal(fac[:, it, :], rs[:, it, :]))
                    for b, c in enumerate((1, 2, 0)):
                        last = dve.tensor_tensor(fac[:, it, b:b + 1], fac[:, it, b:b + 1], gates[:, h, 3 * g + c:3 * g + c + 1], ALU.mult)
                    link(last)
                    for b, (o, w) in enumerate(BR):
                        last = dve.tensor_scalar(probs[:, o:o + w], probs[:, o:o + w], fac[:, it, b:b + 1], None, ALU.mult)
                    last.then_inc(scaled, 1)



def output_projection(nc, m):
    with ExitStack() as ctx:
        sb = lambda n, s, dt=F32: ctx.enter_context(nc.sbuf_tensor(f"out_{n}_sb", s, dt))
        sem = lambda n: m.sem(f"out_{n}")
        mix2 = [sb(n, [P, KT, PADT], F32R) for n in ("mix_hi", "mix_lo")]
        units = [(c, t) for c in range(OUT_CHUNKS) for t in range(TILES)]
        width = D // OUT_CHUNKS
        mix_hi, mix_lo, padded = sem("mix_hi"), sem("mix_lo"), sem("padded")
        x_loaded = [sem(f"x_loaded{c}") for c in range(OUT_CHUNKS)]

        def load_x(sp, chunks):
            for c in chunks:
                cols = slice(width * c, width * (c + 1))
                sp.dma_start(m.x2[:, 0:TS, cols], m.x_prompt[:, cols].rearrange("(t p) n -> p t n", p=P)).then_inc(x_loaded[c], 16)
                sp.dma_start(m.x2[:NB * NQ, TS, cols], m.x_sample[:, cols]).then_inc(x_loaded[c], 16)

        def load_mlp(sp, evac):
            load_x(sp, range(2, OUT_CHUNKS))
            sp.wait_ge(evac[1], TILES * (OUT_CHUNKS - 1) + 1)
            sp.dma_start(m.out_raw[0][:], m.a["w_up"][0].rearrange("p a n -> p (a n)")).then_inc(m.sem("mlp_up_loaded"), 16)

        def pad(pool, _):
            for part in mix2:
                pool.memset(part[:, :, TOK:].bitcast(F32), 0.0).then_inc(padded, 1)

        def round_mix(act, _):
            for t in range(TILES):
                n = ROWS[t]
                act.activation(mix2[0][:, :, t * P:t * P + n], m.mixT[:, :, t * P:t * P + n], ACT.Copy).then_inc(mix_hi, 1)

        def rest_of_mix(dve, t):
            n = ROWS[t]
            dve.wait_ge(mix_hi, t + 1)
            dve.tensor_tensor(mix2[1][:, :, t * P:t * P + n], m.mixT[:, :, t * P:t * P + n],
                              mix2[0][:, :, t * P:t * P + n], ALU.subtract).then_inc(mix_lo, 1)

        def wait_for_mix(pe, t):
            pe.wait_ge(mix_lo, t + 1)
            if t == TS:
                pe.wait_ge(padded, 2)

        def rests_of_mix(dve, _):
            for t in range(TILES):
                rest_of_mix(dve, t)

        def tensor(pe, u):
            if u + 1 < TILES:
                wait_for_mix(pe, u + 1)

        def evacuation(dve, _, u):
            c, t = units[u]
            n = ROWS[t]
            if t == 0:
                dve.wait_ge(x_loaded[c], 32)
            part = m.x2[:n, t, width * c:width * (c + 1)]
            return dve.tensor_tensor(part, part, m.ps[:n, u % 8, :width], ALU.add)

        m.hT2 = mix2
        project(nc, m, "op", [m.a["w_out"][c] for c in range(OUT_CHUNKS)], [width] * OUT_CHUNKS, units, evacuation, False,
                side={"sync_first": lambda sp, _: load_x(sp, range(2)), "sync": load_mlp, "gpsimd": pad, "scalar_first": round_mix, "vector_first": rests_of_mix,
                      "tensor_first": lambda pe, _: wait_for_mix(pe, 0), "tensor": tensor},
                preload=m.out_raw, out_by_dve=True)


def mlp_products(nc, m):
    with ExitStack() as ctx:
        sb = lambda n, s, dt=F32R: ctx.enter_context(nc.sbuf_tensor(f"mlp_{n}", s, dt))
        sem = lambda n: m.sem(f"mlp_{n}")
        NG, FT = FF // FG, FG // P
        KINDS = ("up", "down")
        WN = KT * FG
        assert WN == FT * D
        assert KT * D // OUT_CHUNKS == WN
        raw = {"up": m.out_raw[0], "down": sb("raw_down", [P, WN], F32)}
        hi = {k: sb("hi_" + k, [P, WN]) for k in KINDS}
        lo = {k: sb("lo_" + k, [P, WN]) for k in KINDS}
        RT = 2
        rect = sb("rect", [P, RT, 512], F32)
        hid = [sb(n, [P, 2, FT, PADT]) for n in ("hid_hi", "hid_lo")]
        loaded = {k: m.sem(f"mlp_{k}_loaded") for k in KINDS}
        hi_made = {k: sem(k + "_hi_made") for k in KINDS}
        lo_made = {k: sem(k + "_lo_made") for k in KINDS}
        (product, rectified, squared, hid_hi, hid_lo, added) = (
            sem(n) for n in ("product", "rectified", "squared", "hid_hi", "hid_lo", "added"))
        padded = sem("padded")
        gain = sb("gain", [P, D], F32)
        stat = sb("stat", [P, 4, TILES], F32)
        (gain_loaded, rowsq, var_ready, std_ready, vec, y_ready) = (
            sem(n) for n in ("gain_loaded", "rowsq", "var_ready", "std_ready", "vec", "y_ready"))
        stored = m.sem("fin_stored")
        UPS, DOWNS = 3 * FT, 2 * TILES
        phases = [("up", 0)]
        for g in range(NG):
            phases += [("up", g + 1)] * (g + 1 < NG) + [("down", g)]
        units = []
        for kind, g in phases:
            units += [(kind, g, a, b) for a in range(FT if kind == "up" else TILES) for b in range(3 if kind == "up" else 2)]
        rank, seen = [], {"up": 0, "down": 0}
        for kind, *_ in units:
            seen[kind] += 1
            rank.append(seen[kind])
        ends = {}
        for u, (kind, g, _, _) in enumerate(units):
            ends[kind, g] = u + 1
        w_of = {"up": lambda t: t[:].rearrange("p (k n) -> p k n", k=KT),
                "down": lambda t: t[:].rearrange("p (f n) -> p f n", f=FT)}
        with nc.Block() as block:
            @block.sync
            def _(sp):
                for kind, g in phases[1:]:
                    if g:
                        sp.wait_ge(lo_made[kind], g)
                    src = m.a["w_" + kind][g].rearrange("p a n -> p (a n)")
                    sp.dma_start(raw[kind][:], src).then_inc(loaded[kind], 16)
                sp.dma_start(gain[:], m.a["ln_f"]).then_inc(gain_loaded, 16)
                for t in range(TILES):
                    sp.wait_ge(y_ready, t + 1)
                    dst = m.o["y_p"][t * P:(t + 1) * P, :] if t < TS else m.o["y_s"]
                    sp.dma_start(dst, m.x2[:ROWS[t], t, :]).then_inc(stored, 16)
                sp.wait_ge(stored, 16 * TILES)

            @block.scalar
            def _(act):
                def round_weights(kind, g):
                    act.wait_ge(loaded[kind], 16 * (g + 1))
                    if g:
                        act.wait_ge(product, ends[kind, g - 1])
                    act.activation(hi[kind][:], raw[kind][:], ACT.Copy).then_inc(hi_made[kind], 1)

                def round_hidden(u):
                    _, g, a, b = units[u]
                    o, w = GROUPS_N[b]
                    act.wait_ge(squared, rank[u])
                    act.activation(hid[0][:, g % 2, a, o:o + w], rect[:, (rank[u] - 1) % RT, :w], ACT.Copy).then_inc(hid_hi, 1)

                round_weights("up", 0)
                waiting = None
                for u, (kind, g, a, b) in enumerate(units):
                    if kind == "down":
                        if waiting is not None:
                            round_hidden(waiting)
                            waiting = None
                        if (a, b) == (0, 0) and g + 2 < NG:
                            round_weights("up", g + 2)
                        if (a, b) == (0, 0) and g == NG - 1:
                            round_weights("down", g)
                        continue
                    o, w = GROUPS_N[b]
                    if (a, b) == (0, 0):
                        if g:
                            round_weights("down", g - 1)
                        if g >= 2:
                            act.wait_ge(product, ends["down", g - 2])
                    act.wait_ge(product, u + 1)
                    if rank[u] > RT:
                        act.wait_ge(hid_lo, rank[u] - RT)
                    act.activation(rect[:, (rank[u] - 1) % RT, :w], m.ps[:, u % 8, :w], ACT.Relu).then_inc(rectified, 1)
                    if waiting is not None:
                        round_hidden(waiting)
                    waiting = u
                    if g == 0 and (a, b) == (FT - 1, 2):
                        round_hidden(waiting)
                        waiting = None
                        round_weights("up", 1)
                junk = rect[:].rearrange("p a n -> p (a n)")
                for t in range(TILES):
                    n = ROWS[t]
                    act.wait_ge(added, DOWNS * (NG - 1) + 2 * t + 2)
                    if t:
                        act.wait_ge(rowsq, t)
                    else:
                        act.wait_ge(hid_lo, UPS * NG)
                    act.activation(junk[:n, :], m.x2[:n, t, :], ACT.Square, accum_out=stat[:n, 0, t:t + 1]).then_inc(rowsq, 1)
                    act.wait_ge(var_ready, t + 1)
                    act.activation(stat[:n, 2, t:t + 1], stat[:n, 1, t:t + 1], ACT.Sqrt).then_inc(std_ready, 1)

            @block.gpsimd
            def _(pool):
                for part in hid:
                    pool.memset(part[:, :, :, TOK:].bitcast(F32), 0.0).then_inc(padded, 1)
                for u, (kind, g, a, b) in enumerate(units):
                    if kind == "up":
                        w = GROUPS_N[b][1]
                        pool.wait_ge(rectified, rank[u])
                        part = rect[:, (rank[u] - 1) % RT, :w]
                        pool.tensor_tensor(part, part, part, ALU.mult).then_inc(squared, 1)

            @block.vector
            def _(dve):
                def rest_of_weights(kind, g):
                    dve.wait_ge(hi_made[kind], g + 1)
                    dve.tensor_tensor(lo[kind][:], raw[kind][:], hi[kind][:], ALU.subtract).then_inc(lo_made[kind], 1)

                link = Link(dve, vec)

                def variance(t):
                    n = ROWS[t]
                    dve.wait_ge(rowsq, t + 1)
                    dve.tensor_scalar(stat[:n, 1, t:t + 1], stat[:n, 0, t:t + 1], 1.0 / D, EPS, ALU.mult, ALU.add).then_inc(var_ready, 1)

                def normalise(t):
                    n = ROWS[t]
                    dve.wait_ge(std_ready, t + 1)
                    link(dve.reciprocal(stat[:n, 3, t:t + 1], stat[:n, 2, t:t + 1]))
                    dve.scalar_tensor_tensor(m.x2[:n, t, :], m.x2[:n, t, :], stat[:n, 3, t:t + 1], gain[:n, :],
                                             ALU.mult, ALU.mult).then_inc(y_ready, 1)

                rest_of_weights("up", 0)
                for u, (kind, g, a, b) in enumerate(units):
                    if kind == "up":
                        o, w = GROUPS_N[b]
                        if (a, b) == (0, 0) and g:
                            rest_of_weights("down", g - 1)
                        dve.wait_ge(hid_hi, rank[u])
                        dve.tensor_tensor(hid[1][:, g % 2, a, o:o + w], rect[:, (rank[u] - 1) % RT, :w],
                                          hid[0][:, g % 2, a, o:o + w], ALU.subtract).then_inc(hid_lo, 1)
                        if g == 0 and (a, b) == (FT - 1, 2):
                            rest_of_weights("up", 1)
                        continue
                    if (a, b) == (0, 0) and g + 2 < NG:
                        rest_of_weights("up", g + 2)
                    if (a, b) == (0, 0) and g == NG - 1:
                        rest_of_weights("down", g)
                    n = ROWS[a]
                    dve.wait_ge(product, u + 1)
                    if g:
                        dve.wait_ge(added, DOWNS * (g - 1) + 2 * a + b + 1)
                    part = m.x2[:n, a, 512 * b:512 * b + 512]
                    dve.tensor_tensor(part, part, m.ps[:n, u % 8, :], ALU.add).then_inc(added, 1)
                    if g == NG - 1 and a:
                        if b == 0:
                            variance(a - 1)
                        else:
                            if a == 1:
                                dve.wait_ge(gain_loaded, 16)
                            normalise(a - 1)
                variance(TS)
                normalise(TS)

            @block.tensor
            def _(pe):
                for u, (kind, g, a, b) in enumerate(units):
                    x = g % 2
                    if (a, b) == (0, 0):
                        pe.wait_ge(lo_made[kind], g + 1)
                        if kind == "down":
                            pe.wait_ge(hid_lo, UPS * (g + 1))
                            pe.wait_ge(padded, 2)
                    if u >= 8:
                        pe.wait_ge(rectified if units[u - 8][0] == "up" else added, rank[u - 8])
                    w2 = [w_of[kind](t[kind]) for t in (hi, lo)]
                    if kind == "up":
                        o, w = GROUPS_N[b]
                        for k in range(KT):
                            last = triple(pe, m.ps[:, u % 8, :w], [t[:, k, a * P:(a + 1) * P] for t in w2],
                                          [t[:, k, o:o + w] for t in m.h2], k == 0, k == KT - 1)
                    else:
                        for f in range(FT):
                            last = triple(pe, m.ps[:, u % 8, :], [t[:, x, f, a * P:(a + 1) * P] for t in hid],
                                          [t[:, f, 512 * b:512 * b + 512] for t in w2], f == 0, f == FT - 1)
                    last.then_inc(product, 1)


def mlp(nc, m):
    with ExitStack() as normed:
        m.h2 = [normed.enter_context(nc.sbuf_tensor(n, [P, KT, TOK], F32R)) for n in ("h2_hi", "h2_lo")]
        norm_transpose(nc, m, "ln2", m.a["ln2"], m.h2, m.x2, False)
        mlp_products(nc, m)



def hymba_layer(nc, a, o):
    m = Memory()
    with ExitStack() as ctx:
        live = []
        stored = {n: nc.alloc_semaphore(n) for n in ("proj_stored", "dn_stored", "s5_stored", "fin_stored", "caches_loaded", "mlp_up_loaded")}

        def sem(name):
            if name in stored:
                return stored[name]
            live.append(nc.alloc_semaphore(name))
            return live[-1]

        def recycle_semaphores():
            nc.clear_and_free_semaphores(live)
            live.clear()
            nc.all_engine_barrier()

        m.sem = sem
        keep = lambda n, s: ctx.enter_context(nc.sbuf_tensor(n, s, F32))
        m.ps = ctx.enter_context(nc.psum_tensor("ps", [P, 8, 512], F32))
        m.const = a["const"]
        m.x_prompt, m.x_sample = a["x_prompt"], a["x_sample"]
        m.w_in = [a["w_feat"][c] for c in range(FEAT)] + [a["w_token"][c] for c in range(TOKEN_CHUNKS)]
        m.cache_win, m.state_conv, m.state_dn = a["cache_win"], a["state_conv"], a["state_dn"]
        m.conv_w, m.a_log, m.dt_bias, m.norm_w = a["conv_w"], a["a_log"], a["dt_bias"], a["norm_w"]
        m.kv_prompt, m.kv_sample, m.win_prompt, m.win_sample = o["kv_p"], o["kv_s"], o["win_p"], o["win_s"]
        m.conv_prompt, m.conv_sample = o["conv_p"], o["conv_s"]
        m.dn_prompt, m.dn_sample = o["dn_p"], o["dn_s"]
        m.a, m.o = a, o
        m.ident = keep("ident", [P, P])
        ident_loaded = m.sem("ident_loaded")
        with nc.Block() as block:
            @block.sync
            def _(sp):
                at, w = CONST_AT["ident"]
                sp.dma_start(m.ident[:], m.const[:, at:at + w]).then_inc(ident_loaded, 16)
                sp.wait_ge(ident_loaded, 16)
        right = lambda stack, n, s, dt=F32: stack.enter_context(nc.sbuf_tensor(n, s, dt, side="right"))
        with ExitStack() as mixed:
            m.mixT = mixed.enter_context(nc.sbuf_tensor("mixT", [P, KT, PADC], F32))
            mixers = mixed.enter_context(ExitStack())
            hold = lambda n, s: mixers.enter_context(nc.sbuf_tensor(n, s, F32))
            with ExitStack() as normed:
                m.hT2 = [right(normed, n, [P, KT, PADT], F32R) for n in ("h_hi", "h_lo")]
                m.uT = right(normed, "uT", [P, 2, TOK])
                with ExitStack() as features:
                    raw = right(features, "feat_raw", [P, KT * P])
                    m.feat_raw, m.query_raw = (raw, m.sem("feat_raw_loaded")), (raw, m.sem("query_raw_loaded"))
                    norm_transpose(nc, m, "ln1", a["ln1"], m.hT2, None, True)
                    m.dnx = right(features, "dnx", [P, 6, PADC])
                    feature_and_s5(nc, m)
                    m.qT = hold("qT", [P, 4, TOK])
                    m.convs = hold("convs", [P, 6, NB * NQ])
                    token_raw = m.uT[:].rearrange("p c n -> p (c n)")[:, :KT * (KV + SMALL) // TOKEN_CHUNKS]
                    m.token_raw = token_raw, m.sem("token_raw_loaded")
                    query_projection(nc, m)
                tokens = hold("tokens", [P, TILES, KV + SMALL])
                m.kv, m.small = tokens[:, :, :KV], tokens[:, :, KV:]
                token_projection(nc, m, tokens)
            with ExitStack() as caches:
                m.ck = right(caches, "ck", [P, NB * PAGES, 512])
                delta_net(nc, m)
                recycle_semaphores()
                m.cw = right(caches, "cw", [P, NB * PAGES, 256])
                key_tables = mixers.enter_context(ExitStack())
                key_prep(nc, m, key_tables)
                sample_attention(nc, m)
            m.out_raw = right(ctx, "out_raw", [P, KT * D // OUT_CHUNKS]), m.sem("out_raw_loaded")
            prompt_attention(nc, m)
            mixers.close()
            m.x2 = right(ctx, "x2", [P, TILES, D])
            output_projection(nc, m)
            recycle_semaphores()
        mlp(nc, m)
        nc.clear_and_free_semaphores(live)



def host_inputs(i):
    f = np.float32
    w = i["w_in"][0]
    kt = lambda x: np.ascontiguousarray(x.reshape(KT, P, -1).transpose(1, 0, 2).reshape(P, -1))
    feat = [np.concatenate([w[:, h * HD:(h + 1) * HD], w[:, (h + 4) * HD:(h + 5) * HD]], 1) for h in range(4)]
    feat += [w[:, 1304 + c * P:1304 + (c + 1) * P] for c in range(6)]
    feat += [w[:, 2336 + c * P:2336 + (c + 1) * P] for c in range(2)]
    a = {
        "const": constants_array(),
        "x_prompt": i["x_prompt"][0], "x_sample": i["x_sample"].reshape(NB * NQ, D),
        "ln1": i["ln1"][0].reshape(KT, P).T,
        "w_feat": np.stack([kt(x) for x in feat]),
        "w_token": np.stack([kt(x) for x in np.split(np.concatenate([w[:, 512:1304], w[:, 2072:2336]], 1), TOKEN_CHUNKS, 1)]),
        "cache_win": i["cache_win_kv"][0].reshape(NB, PAST, 256),
        "state_conv": i["state_dn_conv"][0].reshape(NB, 3, 6, P).transpose(3, 2, 0, 1),
        "conv_w": i["dn_conv_w"][0].reshape(6, P, 4).transpose(1, 0, 2),
        "a_log": np.broadcast_to(i["dn_a_log"][0], (P, 4)), "dt_bias": np.broadcast_to(i["dn_dt_bias"][0], (P, 4)),
        "norm_w": np.broadcast_to(i["dn_norm_w"][0], (P, HD)),
    }
    s = np.zeros((2, HD, NB, 2, 2, HD), f)
    dn = i["state_dn"][0].reshape(NB, 2, 2, HD, HD)
    for h in range(2):
        s[h, :, :, :, h] = dn[:, :, h].transpose(2, 0, 1, 3)
    state = lambda x: x.reshape(-1, 8, P).transpose(2, 0, 1)
    a["s5_par"] = state(np.stack([i["s5_lambda_re"][0], i["s5_lambda_im"][0],
                                  np.broadcast_to(i["s5_log_step"][0][:, None], (16, 64))]))
    a["s5_d"] = i["s5_d"][0].reshape(2, P).T
    a["w_glu"] = i["s5_w_glu"][0].reshape(2, P, 256).transpose(1, 0, 2)
    b, c = np.zeros((P, 2, 8, P), f), np.zeros((P, 2, 8, P), f)
    for g in range(16):
        rows, ch = slice((g % 2) * 64, (g % 2) * 64 + 64), slice((g % 8) * 16, (g % 8) * 16 + 16)
        for ri, part in enumerate(("re", "im")):
            b[rows, ri, g // 2, ch] = i["s5_b_" + part][0, g]
            c[rows, ri, g // 2, ch] = i["s5_c_" + part][0, g].T
    a["s5_b"], a["s5_c"] = b, c
    a["s5_h0"] = np.stack([i["state_s5_" + part][0].reshape(NB, 8, P).transpose(2, 1, 0) for part in ("re", "im")], 1)
    wck, wcv = np.zeros((P, 2, 2), f), np.zeros((P, 2, 62), f)
    for blk in range(2):
        wck[64 * blk:64 * blk + 64, :, blk] = i["nsa_wck"][0].T
        wcv[64 * blk:64 * blk + 64, :, 30 + blk] = i["nsa_wcv"][0].T
    a["wck"], a["wcv"] = wck.reshape(P, 4), wcv
    a["page_table"] = i["page_table"].reshape(1, NB * PAGES)
    a["cache_nsa"] = i["cache_nsa_kv"][0].reshape(-1, P, 512)
    a["ln2"] = i["ln2"][0].reshape(KT, P).T
    a["ln_f"] = np.broadcast_to(i["ln_f"], (P, D))
    wo = i["w_out"][0]
    heads = np.concatenate([np.concatenate([wo[h * HD:(h + 1) * HD], wo[(h + 4) * HD:(h + 5) * HD]], 0) for h in range(4)], 0)
    a["w_out"] = np.stack([kt(x) for x in np.split(np.concatenate([heads, wo[512:]], 0), OUT_CHUNKS, 1)])
    a["w_up"] = i["mlp_up"][0].reshape(KT, P, FF // FG, FG).transpose(2, 1, 0, 3)
    a["w_down"] = i["mlp_down"][0].reshape(FF // FG, FG // P, P, D).transpose(0, 2, 1, 3)
    a["state_dn"] = s.reshape(P, NB, 2, P)
    return a


OUTS = {"y_p": (SEQ, D), "y_s": (NB * NQ, D), "kv_p": (SEQ, 512), "kv_s": (NB * NQ, 512),
        "win_p": (512, 256), "win_s": (NB, PAST + NQ, 256), "conv_p": (P, 6, 3), "conv_s": (P, 6, NB, 3),
        "dn_p": (P, 2, HD), "dn_s": (P, NB, 2, HD), "s5_p": (P, 8, 2), "s5_s": (P, 8, 2, NB)}


def host_outputs(r):
    dn_s = r["dn_s"].reshape(2, HD, NB, 2, HD).transpose(2, 3, 0, 1, 4).reshape(1, NB, 4, HD, HD)
    dn_p = r["dn_p"].reshape(2, HD, 2, HD).transpose(2, 0, 1, 3).reshape(1, 1, 4, HD, HD)
    s5_p = r["s5_p"].transpose(2, 1, 0).reshape(2, 1, 1, 16, 64)
    s5_s = r["s5_s"].transpose(2, 3, 1, 0).reshape(2, 1, NB, 16, 64)
    return (r["y_p"].reshape(1, SEQ, D), r["y_s"].reshape(NB, NQ, D),
            r["kv_p"].reshape(1, 1, SEQ, 4, 2, HD), r["kv_s"].reshape(1, NB, NQ, 4, 2, HD),
            r["win_p"].reshape(1, 1, 512, 2, 2, HD), r["win_s"].reshape(1, NB, PAST + NQ, 2, 2, HD),
            r["conv_p"].transpose(2, 1, 0).reshape(1, 1, 3, KV), r["conv_s"].transpose(2, 3, 1, 0).reshape(1, NB, 3, KV),
            dn_p, dn_s, s5_p[0], s5_s[0], s5_p[1], s5_s[1])


def kernel(**inputs):
    import concourse.bacc as bacc
    from concourse.bass_utils import run_bass_kernel_spmd

    nc = bacc.Bacc("TRN2", target_bir_lowering=False, num_devices=1)
    arrays, a, o = {}, {}, {}
    for name, x in host_inputs({k: np.asarray(v) for k, v in inputs.items()}).items():
        x = np.ascontiguousarray(x)
        arrays["in_" + name] = x
        a[name] = nc.dram_tensor("in_" + name, x.shape, mybir.dt.from_np(x.dtype), kind="ExternalInput").ap()
    for name, shape in OUTS.items():
        o[name] = nc.dram_tensor("out_" + name, shape, F32, kind="ExternalOutput").ap()
    hymba_layer(nc, a, o)
    r = run_bass_kernel_spmd(nc, [arrays], core_ids=[0])
    return tuple(np.ascontiguousarray(x) for x in host_outputs({n: np.asarray(r.results[0]["out_" + n]) for n in OUTS}))
```
